# Optimizing a Trainium2 kernel written in Bass

```python
import math
import jax, jax.numpy as jnp
from jax import lax
import numpy as np

D_MODEL = 1024
BATCH = 1
SEQ = 256
DEPTH = 2

GRID_W = 64
CTX_LEN = 256
N_MIXERS = 3
N_MOD = 9
FFN_HIDDEN = 256 * ((8 * D_MODEL + 767) // 768)
FFN_RESIDUAL = 0.5
DN_HEAD_DIM = 128
DN_HEADS = D_MODEL // DN_HEAD_DIM
DN_CONV = 5
DN_CHUNK = 64
SWA_HEAD_DIM = 64
SWA_HEADS = D_MODEL // SWA_HEAD_DIM
SWA_KV_HEADS = SWA_HEADS // 4
WINDOW = 128
ATTN_BLOCK = 128
RET_HEADS = 4
RET_QK_DIM = D_MODEL // RET_HEADS
RET_V_DIM = 2 * RET_QK_DIM
RET_CHUNK = 128
ROPE_BASE = 10000.0
EPS = 1e-6


def _rms_norm(x, gain):
    xf = x.astype(jnp.float32)
    y = xf * lax.rsqrt(jnp.mean(xf * xf, axis=-1, keepdims=True) + EPS)
    return (y * gain.astype(jnp.float32)).astype(x.dtype)

def _head_group_norm(x, gain):
    xf = x.astype(jnp.float32)
    mu = jnp.mean(xf, axis=-1, keepdims=True)
    var = jnp.mean(jnp.square(xf - mu), axis=-1, keepdims=True)
    return ((xf - mu) * lax.rsqrt(var + EPS) * gain.astype(jnp.float32)).astype(x.dtype)

def _l2_normalize(x):
    xf = x.astype(jnp.float32)
    return (xf * lax.rsqrt(jnp.sum(xf * xf, axis=-1, keepdims=True) + EPS)).astype(x.dtype)

def _modulated_norm(h, gain, shift, scale):
    return _rms_norm(h, gain) * (1.0 + scale) + shift

def _swiglu(h, w1, w2):
    a, b = jnp.split(h @ w1, 2, axis=-1)
    return (jax.nn.silu(a) * b) @ w2

def _rotary_tables(positions, n_freq):
    inv = ROPE_BASE ** (-jnp.arange(n_freq, dtype=jnp.float32) / n_freq)
    ang = jnp.concatenate([p.astype(jnp.float32)[:, None] * inv[None, :] for p in positions], axis=-1)
    return jnp.cos(ang), jnp.sin(ang)

def _rope(x, cos, sin):
    x1, x2 = jnp.split(x, 2, axis=-1)
    c = cos[:, None, :].astype(x.dtype)
    s = sin[:, None, :].astype(x.dtype)
    return jnp.concatenate([x1 * c - x2 * s, x1 * s + x2 * c], axis=-1)

def _short_conv(x, w):
    k = w.shape[0]
    return lax.conv_general_dilated(x, w[:, None, :], window_strides=(1,), padding=[(k // 2, k // 2)],
                                    dimension_numbers=('NWC', 'WIO', 'NWC'), feature_group_count=x.shape[-1])

def _join(a_ctx, a_lat, reverse):
    if reverse:
        a_ctx, a_lat = jnp.flip(a_ctx, 1), jnp.flip(a_lat, 1)
    return jnp.concatenate([a_ctx, a_lat], axis=1)

def _both_dirs(a_ctx, a_lat):
    return jnp.concatenate([_join(a_ctx, a_lat, False), _join(a_ctx, a_lat, True)], axis=0)

def _split_dirs(o, n_batch, ctx_len):
    of, ob = o[:n_batch], o[n_batch:]
    return (of[:, :ctx_len], of[:, ctx_len:], jnp.flip(ob[:, :ctx_len], 1), jnp.flip(ob[:, ctx_len:], 1))

def _to_chunks(a, size):
    n, t, h = a.shape[:3]
    a = a.astype(jnp.float32).reshape((n, t // size, size, h) + a.shape[3:])
    return jnp.moveaxis(a, 3, 1)

def _from_chunks(a):
    n, h, nc, c = a.shape[:4]
    return jnp.moveaxis(a, 1, 3).reshape((n, nc * c, h) + a.shape[4:])

def _gated_delta_chunked(q, k, v, g, beta):
    out_dtype = v.dtype
    n, t, h, dk = q.shape
    dv = v.shape[-1]
    q = _to_chunks(q, DN_CHUNK) * dk ** -0.5
    k = _to_chunks(k, DN_CHUNK)
    v = _to_chunks(v, DN_CHUNK)
    gc = jnp.cumsum(_to_chunks(g, DN_CHUNK), axis=-1)
    beta = _to_chunks(beta, DN_CHUNK)
    causal = jnp.tril(jnp.ones((DN_CHUNK, DN_CHUNK), bool))
    strict = jnp.tril(jnp.ones((DN_CHUNK, DN_CHUNK), bool), -1)
    decay = jnp.exp(jnp.where(causal, gc[..., :, None] - gc[..., None, :], -jnp.inf))
    kb = k * beta[..., None]
    lower = jnp.where(strict, jnp.einsum('nhcid,nhcjd->nhcij', kb, k) * decay, 0.0)
    rhs = jnp.concatenate([v * beta[..., None], kb * jnp.exp(gc)[..., None]], axis=-1)
    uw = lax.linalg.triangular_solve(lower, rhs, left_side=True, lower=True, unit_diagonal=True)
    u, w = uw[..., :dv], uw[..., dv:]
    qk = jnp.einsum('nhcid,nhcjd->nhcij', q, k) * decay
    qg = q * jnp.exp(gc)[..., None]
    g_last = gc[..., -1]
    kd = k * jnp.exp(g_last[..., None] - gc)[..., None]
    xs = tuple(jnp.moveaxis(a, 2, 0) for a in (u, w, qk, qg, kd, jnp.exp(g_last)))

    def step(state, inp):
        u_c, w_c, qk_c, qg_c, kd_c, a_c = inp
        v_new = u_c - jnp.einsum('nhik,nhkv->nhiv', w_c, state)
        o = jnp.einsum('nhik,nhkv->nhiv', qg_c, state) + jnp.einsum('nhij,nhjv->nhiv', qk_c, v_new)
        state = state * a_c[..., None, None] + jnp.einsum('nhjk,nhjv->nhkv', kd_c, v_new)
        return state, o

    _, o = lax.scan(step, jnp.zeros((n, h, dk, dv), jnp.float32), xs)
    return _from_chunks(jnp.moveaxis(o, 0, 2)).astype(out_dtype)

def _retention_log_decay():
    return jnp.log1p(-jnp.exp2(-5.0 - jnp.arange(RET_HEADS, dtype=jnp.float32)))

def _retention_chunked(q, k, v, log_gamma):
    out_dtype = v.dtype
    n, t, h, dk = q.shape
    dv = v.shape[-1]
    q = _to_chunks(q, RET_CHUNK)
    k = _to_chunks(k, RET_CHUNK) * dk ** -0.5
    v = _to_chunks(v, RET_CHUNK)
    pos = jnp.arange(RET_CHUNK, dtype=jnp.float32)
    lg = log_gamma[:, None]
    rel = pos[:, None] - pos[None, :]
    decay = jnp.exp(jnp.where(rel >= 0, lg[:, :, None] * rel, -jnp.inf))
    scores = jnp.einsum('nhcid,nhcjd->nhcij', q, k) * decay[:, None]
    o_intra = jnp.einsum('nhcij,nhcje->nhcie', scores, v)
    q_in = q * jnp.exp(lg * (pos + 1.0))[:, None, :, None]
    k_st = k * jnp.exp(lg * (RET_CHUNK - 1.0 - pos))[:, None, :, None]
    chunk_decay = jnp.exp(lg * RET_CHUNK)[:, :, None]

    def step(state, inp):
        q_c, k_c, v_c = inp
        o = jnp.einsum('nhid,nhde->nhie', q_c, state)
        state = state * chunk_decay + jnp.einsum('nhjd,nhje->nhde', k_c, v_c)
        return state, o

    xs = tuple(jnp.moveaxis(a, 2, 0) for a in (q_in, k_st, v))
    _, o_inter = lax.scan(step, jnp.zeros((n, h, dk, dv), jnp.float32), xs)
    return _from_chunks(o_intra + jnp.moveaxis(o_inter, 0, 2)).astype(out_dtype)

def _sink_softmax(logits, sink):
    sink_col = jnp.broadcast_to(sink.astype(jnp.float32)[None, :, :, None, None], logits.shape[:-1] + (1,))
    return jax.nn.softmax(jnp.concatenate([sink_col, logits], axis=-1), axis=-1)[..., 1:]

def _deltanet_mixer(hc, hx, w_in, conv_w, a_log, dt_bias, o_gain, w_out):
    n_batch, ctx_len = hx.shape[0], hc.shape[1]
    qkv_w = 3 * DN_HEADS * DN_HEAD_DIM
    z_w = DN_HEADS * DN_HEAD_DIM

    def project(h):
        n = h.shape[1]
        qkv, z, ab = jnp.split(h @ w_in, [qkv_w, qkv_w + z_w], axis=-1)
        qkv = jax.nn.silu(_short_conv(qkv, conv_w))
        q, k, v = [a.reshape(n_batch, n, DN_HEADS, DN_HEAD_DIM) for a in jnp.split(qkv, 3, axis=-1)]
        ab = ab.astype(jnp.float32).reshape(n_batch, n, 2, 2, DN_HEADS)
        g = -jnp.exp(a_log.astype(jnp.float32)) * jax.nn.softplus(ab[:, :, :, 0] + dt_bias.astype(jnp.float32))
        beta = jax.nn.sigmoid(ab[:, :, :, 1])
        return _l2_normalize(q), _l2_normalize(k), v, z.reshape(n_batch, n, DN_HEADS, DN_HEAD_DIM), g, beta

    qc, kc, vc, zc, gc, bc = project(hc)
    qx, kx, vx, zx, gx, bx = project(hx)
    g_all = jnp.concatenate([_join(gc[:, :, 0], gx[:, :, 0], False), _join(gc[:, :, 1], gx[:, :, 1], True)], axis=0)
    b_all = jnp.concatenate([_join(bc[:, :, 0], bx[:, :, 0], False), _join(bc[:, :, 1], bx[:, :, 1], True)], axis=0)
    o = _gated_delta_chunked(_both_dirs(qc, qx), _both_dirs(kc, kx), _both_dirs(vc, vx), g_all, b_all)
    ofc, ofx, obc, obx = _split_dirs(o, n_batch, ctx_len)

    def finish(o_f, o_b, z):
        y = _rms_norm(o_f + o_b, o_gain) * jax.nn.silu(z)
        return y.reshape(y.shape[0], y.shape[1], -1) @ w_out

    return finish(ofc, obc, zc), finish(ofx, obx, zx)

def _window_attention_mixer(hc, hx, w_qkv, q_gain, k_gain, sink, w_out, cos, sin):
    n_batch, n_tok = hx.shape[0], hx.shape[1]
    ctx_len = hc.shape[1]
    group = SWA_HEADS // SWA_KV_HEADS
    q_w = SWA_HEADS * SWA_HEAD_DIM
    kv_w = SWA_KV_HEADS * SWA_HEAD_DIM
    scale = SWA_HEAD_DIM ** -0.5
    sink_hg = sink.reshape(SWA_KV_HEADS, group)

    def project(h, rotate):
        n = h.shape[1]
        q, k, v = jnp.split(h @ w_qkv, [q_w, q_w + kv_w], axis=-1)
        q = _rms_norm(q.reshape(n_batch, n, SWA_HEADS, SWA_HEAD_DIM), q_gain)
        k = _rms_norm(k.reshape(n_batch, n, SWA_KV_HEADS, SWA_HEAD_DIM), k_gain)
        if rotate:
            q, k = _rope(q, cos, sin), _rope(k, cos, sin)
        q = (q * scale).reshape(n_batch, n, SWA_KV_HEADS, group, SWA_HEAD_DIM)
        return q, k, v.reshape(n_batch, n, SWA_KV_HEADS, SWA_HEAD_DIM)

    qc, kc, vc = project(hc, False)
    qx, kx, vx = project(hx, True)

    s_c = jnp.einsum('bqhgd,bkhd->bhgqk', qc, kc).astype(jnp.float32)
    p_c = _sink_softmax(s_c, sink_hg).astype(vc.dtype)
    oc = jnp.einsum('bhgqk,bkhd->bqhgd', p_c, vc).reshape(n_batch, ctx_len, q_w)

    span = ATTN_BLOCK + 2 * WINDOW
    pad = ((0, 0), (WINDOW, WINDOW), (0, 0), (0, 0))
    kp, vp = jnp.pad(kx, pad), jnp.pad(vx, pad)
    q_off = jnp.arange(ATTN_BLOCK)
    k_off = jnp.arange(span)

    def block(j):
        start = j * ATTN_BLOCK
        qb = lax.dynamic_slice_in_dim(qx, start, ATTN_BLOCK, axis=1)
        kb = lax.dynamic_slice_in_dim(kp, start, span, axis=1)
        vb = lax.dynamic_slice_in_dim(vp, start, span, axis=1)
        t_pos = start + q_off
        s_pos = start - WINDOW + k_off
        allowed = (jnp.abs(t_pos[:, None] - s_pos[None, :]) <= WINDOW) & (s_pos >= 0) & (s_pos < n_tok)
        s_ctx = jnp.einsum('bqhgd,bkhd->bhgqk', qb, kc).astype(jnp.float32)
        s_win = jnp.where(allowed, jnp.einsum('bqhgd,bkhd->bhgqk', qb, kb).astype(jnp.float32), -jnp.inf)
        p = _sink_softmax(jnp.concatenate([s_ctx, s_win], axis=-1), sink_hg).astype(vb.dtype)
        return (jnp.einsum('bhgqk,bkhd->bqhgd', p[..., :ctx_len], vc)
                + jnp.einsum('bhgqk,bkhd->bqhgd', p[..., ctx_len:], vb))

    ox = lax.map(block, jnp.arange(n_tok // ATTN_BLOCK))
    ox = jnp.moveaxis(ox, 0, 1).reshape(n_batch, n_tok, q_w)
    return oc @ w_out, ox @ w_out

def _retention_mixer(hc, hx, w_in, gn_gain, w_out, cos, sin):
    n_batch, ctx_len = hx.shape[0], hc.shape[1]
    qk_w = RET_HEADS * RET_QK_DIM
    v_w = RET_HEADS * RET_V_DIM

    def project(h):
        n = h.shape[1]
        q, k, v, gf, gb = jnp.split(h @ w_in, [qk_w, 2 * qk_w, 2 * qk_w + v_w, 2 * qk_w + 2 * v_w], axis=-1)
        hq = lambda a: a.reshape(n_batch, n, RET_HEADS, RET_QK_DIM)
        hv = lambda a: a.reshape(n_batch, n, RET_HEADS, RET_V_DIM)
        return hq(q), hq(k), hv(v), hv(gf), hv(gb)

    qc, kc, vc, gfc, gbc = project(hc)
    qx, kx, vx, gfx, gbx = project(hx)
    qx, kx = _rope(qx, cos, sin), _rope(kx, cos, sin)
    o = _retention_chunked(_both_dirs(qc, qx), _both_dirs(kc, kx), _both_dirs(vc, vx), _retention_log_decay())
    ofc, ofx, obc, obx = _split_dirs(o, n_batch, ctx_len)
    gain = gn_gain.reshape(2, RET_HEADS, RET_V_DIM)

    def finish(o_f, o_b, g_f, g_b):
        y = (jax.nn.silu(g_f) * _head_group_norm(o_f, gain[0]) + jax.nn.silu(g_b) * _head_group_norm(o_b, gain[1]))
        return y.reshape(y.shape[0], y.shape[1], -1) @ w_out

    return finish(ofc, obc, gfc, gbc), finish(ofx, obx, gfx, gbx)

def first_inputs(seed: int = 0) -> dict:
    key = jax.random.key(seed)
    ks = jax.random.split(key, 24)
    d, f = D_MODEL, FFN_HIDDEN
    n_dn, n_swa, n_ret = (len(range(kind, DEPTH, N_MIXERS)) for kind in range(N_MIXERS))

    def nrm(k, shape, std):
        return std * jax.random.normal(k, shape, jnp.float32)

    dn_in = 4 * DN_HEADS * DN_HEAD_DIM + 4 * DN_HEADS
    swa_in = (SWA_HEADS + 2 * SWA_KV_HEADS) * SWA_HEAD_DIM
    ret_v = RET_HEADS * RET_V_DIM
    ret_in = 2 * RET_HEADS * RET_QK_DIM + 3 * ret_v
    dt = jnp.exp(jax.random.uniform(ks[12], (n_dn, 2, DN_HEADS), jnp.float32, math.log(1e-3), math.log(1e-1)))
    return {
        "x": nrm(ks[0], (BATCH, SEQ, d), 1.0),
        "c": nrm(ks[1], (BATCH, d), 1.0),
        "ctx": nrm(ks[2], (BATCH, CTX_LEN, d), 1.0),
        "c_ctx": nrm(ks[3], (d,), 1.0),
        "ada_w": nrm(ks[4], (DEPTH, d, N_MOD * d), 0.5 * d ** -0.5),
        "ada_b": nrm(ks[5], (DEPTH, N_MOD * d), 0.02),
        "norm_g": 1.0 + nrm(ks[6], (DEPTH, 3, d), 0.02),
        "ffn_w1": nrm(ks[7], (DEPTH, 2, d, 2 * f), d ** -0.5),
        "ffn_w2": nrm(ks[8], (DEPTH, 2, f, d), f ** -0.5),
        "dn_w_in": nrm(ks[9], (n_dn, d, dn_in), d ** -0.5),
        "dn_conv": nrm(ks[10], (n_dn, DN_CONV, 3 * DN_HEADS * DN_HEAD_DIM), DN_CONV ** -0.5),
        "dn_a_log": jnp.log(jax.random.uniform(ks[11], (n_dn, 2, DN_HEADS), jnp.float32, 1.0, 16.0)),
        "dn_dt_bias": dt + jnp.log(-jnp.expm1(-dt)),
        "dn_o_gain": 1.0 + nrm(ks[13], (n_dn, DN_HEAD_DIM), 0.02),
        "dn_w_out": nrm(ks[14], (n_dn, DN_HEADS * DN_HEAD_DIM, d), (DN_HEADS * DN_HEAD_DIM) ** -0.5),
        "swa_w_qkv": nrm(ks[15], (n_swa, d, swa_in), d ** -0.5),
        "swa_q_gain": 1.0 + nrm(ks[16], (n_swa, SWA_HEAD_DIM), 0.02),
        "swa_k_gain": 1.0 + nrm(ks[17], (n_swa, SWA_HEAD_DIM), 0.02),
        "swa_sink": nrm(ks[18], (n_swa, SWA_HEADS), 1.0),
        "swa_w_out": nrm(ks[19], (n_swa, SWA_HEADS * SWA_HEAD_DIM, d), (SWA_HEADS * SWA_HEAD_DIM) ** -0.5),
        "ret_w_in": nrm(ks[20], (n_ret, d, ret_in), d ** -0.5),
        "ret_gn_gain": 1.0 + nrm(ks[21], (n_ret, 2, ret_v), 0.02),
        "ret_w_out": nrm(ks[22], (n_ret, ret_v, d), ret_v ** -0.5),
    }

def first_block(x, c, ctx, c_ctx, ada_w, ada_b, norm_g, ffn_w1, ffn_w2, dn_w_in, dn_conv, dn_a_log, dn_dt_bias,
              dn_o_gain, dn_w_out, swa_w_qkv, swa_q_gain, swa_k_gain, swa_sink, swa_w_out, ret_w_in, ret_gn_gain,
              ret_w_out):
    n_batch, n_tok, d = x.shape
    ROWS = n_tok // GRID_W
    rows = jnp.repeat(jnp.arange(ROWS), GRID_W)
    cols = jnp.tile(jnp.arange(GRID_W), ROWS)
    swa_cos, swa_sin = _rotary_tables((rows, cols), SWA_HEAD_DIM // 4)
    ret_cos, ret_sin = _rotary_tables((jnp.arange(n_tok),), RET_QK_DIM // 2)
    cond_x = jax.nn.silu(c)
    cond_c = jax.nn.silu(c_ctx)

    for i in range(DEPTH):
        kind, slot, last = i % N_MIXERS, i // N_MIXERS, i == DEPTH - 1
        mx = (cond_x @ ada_w[i] + ada_b[i]).reshape(n_batch, 3, 3, 1, d)
        mc = (cond_c @ ada_w[i] + ada_b[i]).reshape(3, 3, d)

        x = x + FFN_RESIDUAL * mx[:, 0, 2] * _swiglu(
            _modulated_norm(x, norm_g[i, 0], mx[:, 0, 0], mx[:, 0, 1]), ffn_w1[i, 0], ffn_w2[i, 0])
        ctx = ctx + FFN_RESIDUAL * mc[0, 2] * _swiglu(
            _modulated_norm(ctx, norm_g[i, 0], mc[0, 0], mc[0, 1]), ffn_w1[i, 0], ffn_w2[i, 0])

        hx = _modulated_norm(x, norm_g[i, 1], mx[:, 1, 0], mx[:, 1, 1])
        hc = _modulated_norm(ctx, norm_g[i, 1], mc[1, 0], mc[1, 1])
        if kind == 0:
            oc, ox = _deltanet_mixer(hc, hx, dn_w_in[slot], dn_conv[slot], dn_a_log[slot], dn_dt_bias[slot],
                                     dn_o_gain[slot], dn_w_out[slot])
        elif kind == 1:
            oc, ox = _window_attention_mixer(hc, hx, swa_w_qkv[slot], swa_q_gain[slot], swa_k_gain[slot],
                                             swa_sink[slot], swa_w_out[slot], swa_cos, swa_sin)
        else:
            oc, ox = _retention_mixer(hc, hx, ret_w_in[slot], ret_gn_gain[slot], ret_w_out[slot], ret_cos, ret_sin)
        x = x + mx[:, 1, 2] * ox

        x = x + FFN_RESIDUAL * mx[:, 2, 2] * _swiglu(
            _modulated_norm(x, norm_g[i, 2], mx[:, 2, 0], mx[:, 2, 1]), ffn_w1[i, 1], ffn_w2[i, 1])
        if not last:
            ctx = ctx + mc[1, 2] * oc
            ctx = ctx + FFN_RESIDUAL * mc[2, 2] * _swiglu(
                _modulated_norm(ctx, norm_g[i, 2], mc[2, 0], mc[2, 1]), ffn_w1[i, 1], ffn_w2[i, 1])
    return x


D_RNN = 1024
RNN_BLOCKS = 16
RNN_BLOCK = D_RNN // RNN_BLOCKS
CONV_WIDTH = 4
LRU_C = 8.0
N_HEADS = 16
QK_NOPE = 64
QK_ROPE = 32
V_HEAD = 64
Q_LORA = 384
KV_LORA = 256
ROPE_THETA = 10000.0
Q_BLOCK = 128
D_MIX = N_HEADS * V_HEAD
IN_WIDTH = 2 * D_RNN + Q_LORA + KV_LORA + QK_ROPE + 2 * D_MIX
D_FF = 3 * D_MODEL
FFN_CONV_WIDTH = 3
ALPHA = (2 * DEPTH) ** 0.25
BETA = (8 * DEPTH) ** -0.25
NEG_INF = -1e30


def _split_points():
    sizes = (D_RNN, D_RNN, Q_LORA, KV_LORA, QK_ROPE, D_MIX, D_MIX)
    pts, acc = [], 0
    for s in sizes[:-1]:
        acc += s
        pts.append(acc)
    return pts

def layer_norm(x, g, b):
    xf = x.astype(jnp.float32)
    mu = xf.mean(-1, keepdims=True)
    var = jnp.square(xf - mu).mean(-1, keepdims=True)
    y = (xf - mu) * lax.rsqrt(var + EPS) * g.astype(jnp.float32) + b.astype(jnp.float32)
    return y.astype(x.dtype)

def rms_norm(x, g):
    xf = x.astype(jnp.float32)
    y = xf * lax.rsqrt(jnp.mean(xf * xf, -1, keepdims=True) + EPS) * g.astype(jnp.float32)
    return y.astype(x.dtype)

def causal_dwconv(x, w, b):
    width, c = w.shape
    y = lax.conv_general_dilated(
        x, w[:, None, :].astype(x.dtype), window_strides=(1,), padding=[(width - 1, 0)],
        dimension_numbers=("NWC", "WIO", "NWC"), feature_group_count=c)
    return y + b.astype(x.dtype)

def rope_tables(positions, dtype):
    inv_freq = ROPE_THETA ** (-jnp.arange(0, QK_ROPE, 2, dtype=jnp.float32) / QK_ROPE)
    ang = positions.astype(jnp.float32)[..., None] * inv_freq
    return jnp.cos(ang)[:, :, None, :].astype(dtype), jnp.sin(ang)[:, :, None, :].astype(dtype)

def apply_rope(x, cos, sin):
    x1, x2 = jnp.split(x, 2, axis=-1)
    return jnp.concatenate([x1 * cos - x2 * sin, x2 * cos + x1 * sin], axis=-1)

def rg_lru(x, gx_w, gx_b, ga_w, ga_b, lru_lambda):
    B, S, _ = x.shape
    xb = x.reshape(B, S, RNN_BLOCKS, RNN_BLOCK)
    gate_x = jax.nn.sigmoid(jnp.einsum("bshi,hij->bshj", xb, gx_w).reshape(B, S, D_RNN) + gx_b)
    gate_a = jax.nn.sigmoid(jnp.einsum("bshi,hij->bshj", xb, ga_w).reshape(B, S, D_RNN) + ga_b)
    log_a = -LRU_C * gate_a.astype(jnp.float32) * jax.nn.softplus(-lru_lambda.astype(jnp.float32))
    a = jnp.exp(log_a)
    mult = jnp.sqrt(-jnp.expm1(2.0 * log_a))
    u = mult * (gate_x * x).astype(jnp.float32)

    def step(h, au):
        a_t, u_t = au
        h = a_t * h + u_t
        return h, h

    _, hs = lax.scan(step, jnp.zeros((B, D_RNN), jnp.float32),
                     (jnp.swapaxes(a, 0, 1), jnp.swapaxes(u, 0, 1)))
    return jnp.swapaxes(hs, 0, 1).astype(x.dtype)

def mla_attention(q_lat, kv_lat, k_rope_raw, cos, sin, q_norm_g, w_uq, kv_norm_g, w_ukv):
    B, S, _ = q_lat.shape
    q = (rms_norm(q_lat, q_norm_g) @ w_uq).reshape(B, S, N_HEADS, QK_NOPE + QK_ROPE)
    q_nope, q_pe = q[..., :QK_NOPE], apply_rope(q[..., QK_NOPE:], cos, sin)
    kv = (rms_norm(kv_lat, kv_norm_g) @ w_ukv).reshape(B, S, N_HEADS, QK_NOPE + V_HEAD)
    k_nope, v = kv[..., :QK_NOPE], kv[..., QK_NOPE:]
    k_pe = apply_rope(k_rope_raw[:, :, None, :], cos, sin)[:, :, 0, :]
    scale = (QK_NOPE + QK_ROPE) ** -0.5
    outs = []
    for start in range(0, S, Q_BLOCK):
        end = start + Q_BLOCK
        s = (jnp.einsum("bqhd,bkhd->bhqk", q_nope[:, start:end], k_nope[:, :end])
             + jnp.einsum("bqhd,bkd->bhqk", q_pe[:, start:end], k_pe[:, :end]))
        s = s.astype(jnp.float32) * scale
        causal = (start + jnp.arange(Q_BLOCK))[:, None] >= jnp.arange(end)[None, :]
        p = jax.nn.softmax(jnp.where(causal, s, NEG_INF), axis=-1).astype(v.dtype)
        outs.append(jnp.einsum("bhqk,bkhd->bqhd", p, v[:, :end]))
    return jnp.concatenate(outs, axis=1).reshape(B, S, D_MIX)

def mixer_sublayer(x, cos, sin, w_in, conv_w, conv_b, gx_w, gx_b, ga_w, ga_b, lru_lambda,
                   q_norm_g, w_uq, kv_norm_g, w_ukv, w_out):
    proj = x @ w_in
    x_rnn, g_rnn, q_lat, kv_lat, k_rope, gate_a, gate_b = jnp.split(proj, _split_points(), axis=-1)
    y_rnn = jax.nn.gelu(g_rnn) * rg_lru(causal_dwconv(x_rnn, conv_w, conv_b),
                                        gx_w, gx_b, ga_w, ga_b, lru_lambda)
    y_mla = mla_attention(q_lat, kv_lat, k_rope, cos, sin, q_norm_g, w_uq, kv_norm_g, w_ukv)
    merged = jax.nn.sigmoid(gate_a) * y_rnn + jax.nn.sigmoid(gate_b) * y_mla
    return merged @ w_out

def conv_ffn(x, w_up, ffn_conv_w, ffn_conv_b, w_down):
    h = causal_dwconv(x @ w_up, ffn_conv_w, ffn_conv_b)
    h_gate, h_val = jnp.split(h, 2, axis=-1)
    return (jax.nn.gelu(h_gate) * h_val) @ w_down

def second_inputs(seed: int = 0) -> dict:
    key = jax.random.key(seed)
    ks = jax.random.split(key, 24)
    f32 = jnp.float32

    def nrm(k, shape, scale):
        return jax.random.normal(k, shape, f32) * scale

    x = jax.random.normal(ks[0], (BATCH, SEQ, D_MODEL), f32)
    offsets = jax.random.randint(ks[1], (BATCH, 1), 0, 4096, dtype=jnp.int32)
    positions = (jnp.arange(SEQ, dtype=jnp.int32)[None, :] + offsets).astype(jnp.int32)
    u = jax.random.uniform(ks[2], (DEPTH, D_RNN), f32, 0.9, 0.999)
    a0 = u ** (1.0 / LRU_C)
    lru_lambda = jnp.log(a0) - jnp.log1p(-a0)
    return {
        "x": x,
        "positions": positions,
        "w_in": nrm(ks[3], (DEPTH, D_MODEL, IN_WIDTH), D_MODEL ** -0.5),
        "conv_w": nrm(ks[4], (DEPTH, CONV_WIDTH, D_RNN), CONV_WIDTH ** -0.5),
        "conv_b": nrm(ks[5], (DEPTH, D_RNN), 0.02),
        "gx_w": nrm(ks[6], (DEPTH, RNN_BLOCKS, RNN_BLOCK, RNN_BLOCK), RNN_BLOCK ** -0.5),
        "gx_b": nrm(ks[7], (DEPTH, D_RNN), 0.02),
        "ga_w": nrm(ks[8], (DEPTH, RNN_BLOCKS, RNN_BLOCK, RNN_BLOCK), RNN_BLOCK ** -0.5),
        "ga_b": nrm(ks[9], (DEPTH, D_RNN), 0.02),
        "lru_lambda": lru_lambda,
        "q_norm_g": 1.0 + nrm(ks[10], (DEPTH, Q_LORA), 0.02),
        "w_uq": nrm(ks[11], (DEPTH, Q_LORA, N_HEADS * (QK_NOPE + QK_ROPE)), Q_LORA ** -0.5),
        "kv_norm_g": 1.0 + nrm(ks[12], (DEPTH, KV_LORA), 0.02),
        "w_ukv": nrm(ks[13], (DEPTH, KV_LORA, N_HEADS * (QK_NOPE + V_HEAD)), KV_LORA ** -0.5),
        "w_out": nrm(ks[14], (DEPTH, D_MIX, D_MODEL), BETA * D_MIX ** -0.5),
        "ln1_g": 1.0 + nrm(ks[15], (DEPTH, D_MODEL), 0.02),
        "ln1_b": nrm(ks[16], (DEPTH, D_MODEL), 0.02),
        "w_up": nrm(ks[17], (DEPTH, D_MODEL, 2 * D_FF), D_MODEL ** -0.5),
        "ffn_conv_w": nrm(ks[18], (DEPTH, FFN_CONV_WIDTH, 2 * D_FF), FFN_CONV_WIDTH ** -0.5),
        "ffn_conv_b": nrm(ks[19], (DEPTH, 2 * D_FF), 0.02),
        "w_down": nrm(ks[20], (DEPTH, D_FF, D_MODEL), BETA * D_FF ** -0.5),
        "ln2_g": 1.0 + nrm(ks[21], (DEPTH, D_MODEL), 0.02),
        "ln2_b": nrm(ks[22], (DEPTH, D_MODEL), 0.02),
    }

def second_block(x, positions, w_in, conv_w, conv_b, gx_w, gx_b, ga_w, ga_b, lru_lambda,
              q_norm_g, w_uq, kv_norm_g, w_ukv, w_out, ln1_g, ln1_b,
              w_up, ffn_conv_w, ffn_conv_b, w_down, ln2_g, ln2_b):
    cos, sin = rope_tables(positions, x.dtype)
    for l in range(DEPTH):
        mix = mixer_sublayer(x, cos, sin, w_in[l], conv_w[l], conv_b[l], gx_w[l], gx_b[l],
                             ga_w[l], ga_b[l], lru_lambda[l], q_norm_g[l], w_uq[l],
                             kv_norm_g[l], w_ukv[l], w_out[l])
        x = layer_norm(ALPHA * x + mix, ln1_g[l], ln1_b[l])
        ffn = conv_ffn(x, w_up[l], ffn_conv_w[l], ffn_conv_b[l], w_down[l])
        x = layer_norm(ALPHA * x + ffn, ln2_g[l], ln2_b[l])
    return x


def setup_inputs(seed=0):
    out = dict(first_inputs(seed))
    for name, value in second_inputs(seed + 1).items():
        if name != "x":
            out[name + "_2"] = value
    return out


def reference(
    x, c, ctx, c_ctx, ada_w, ada_b, norm_g, ffn_w1, ffn_w2, dn_w_in, dn_conv, dn_a_log,
    dn_dt_bias, dn_o_gain, dn_w_out, swa_w_qkv, swa_q_gain, swa_k_gain, swa_sink, swa_w_out,
    ret_w_in, ret_gn_gain, ret_w_out, positions_2, w_in_2, conv_w_2, conv_b_2, gx_w_2, gx_b_2,
    ga_w_2, ga_b_2, lru_lambda_2, q_norm_g_2, w_uq_2, kv_norm_g_2, w_ukv_2, w_out_2, ln1_g_2,
    ln1_b_2, w_up_2, ffn_conv_w_2, ffn_conv_b_2, w_down_2, ln2_g_2, ln2_b_2,
):
    x = first_block(
        x, c, ctx, c_ctx, ada_w, ada_b, norm_g, ffn_w1, ffn_w2, dn_w_in, dn_conv, dn_a_log,
        dn_dt_bias, dn_o_gain, dn_w_out, swa_w_qkv, swa_q_gain, swa_k_gain, swa_sink, swa_w_out,
        ret_w_in, ret_gn_gain, ret_w_out,
    )
    return second_block(
        x, positions_2, w_in_2, conv_w_2, conv_b_2, gx_w_2, gx_b_2, ga_w_2, ga_b_2,
        lru_lambda_2, q_norm_g_2, w_uq_2, kv_norm_g_2, w_ukv_2, w_out_2, ln1_g_2, ln1_b_2,
        w_up_2, ffn_conv_w_2, ffn_conv_b_2, w_down_2, ln2_g_2, ln2_b_2,
    )


_drawn_inputs = setup_inputs


def setup_inputs(seed=0):
    import zlib

    import numpy as np

    out = dict(_drawn_inputs(seed))
    spreads = {}
    factors = {'norm_g': 6.241,
     'dn_o_gain': 8.0,
     'swa_q_gain': 8.0,
     'swa_k_gain': 8.0,
     'swa_sink': 8.0,
     'conv_b_2': 4.044,
     'gx_b_2': 8.0,
     'ga_b_2': 8.0,
     'q_norm_g_2': 8.0,
     'kv_norm_g_2': 8.0,
     'ffn_conv_b_2': 6.07}
    for name, (base, spread) in spreads.items():
        noise = np.random.default_rng([zlib.crc32(name.encode()), seed]).standard_normal(out[name].shape)
        drawn = base * np.exp(spread * noise) if base else spread * noise
        out[name] = __import__('jax').numpy.asarray(drawn.astype(out[name].dtype))
    for name, factor in factors.items():
        out[name] = (out[name] * factor).astype(out[name].dtype)
    return out
```

```python
from contextlib import ExitStack

import numpy as np

import concourse.bass as bass
from concourse import mybir

F32 = mybir.dt.float32
I32 = mybir.dt.int32
ALU = mybir.AluOpType
ACT = mybir.ActivationFunctionType
AX = mybir.AxisListType

P = 128
D = 1024
DC = D // P
CTX = 256
SEQ = 256
T = CTX + SEQ
DEPTH = 2
RING = 4
SLOT = 2048
BANK = 512
CREDIT = 2

FH = 2816
FHC = FH // P
NMOD = 9
DNH = 8
CONV = 5
CK = 128
LEVELS = 7
QUAD = 4
SH, SKV, SD = 16, 4, 64
WINDOW = 128
RC, FC2, CW, FCW = 8, 24, 4, 3
MH, NOPE, ROPE, VH = 16, 64, 32, 64
QL, KVL = 3, 2
ALPHA = float((2 * DEPTH) ** 0.25)
EPS = 1e-6
GELU_C = float(np.sqrt(2.0 / np.pi))

STREAMS = [("ada", 72, 2048)]
for _l in range(DEPTH):
    STREAMS += [(f"w1_{_l}0", 22, 2048), (f"w2_{_l}0", 16, 1408)]
    if _l == 0:
        STREAMS += [("dn_in", 16, 2048), ("dn_ab", 1, 256), ("dn_out", 4, 2048)]
    else:
        STREAMS += [("swa_qk", 5, 2048), ("swa_v", 1, 2048), ("swa_out", 4, 2048)]
    STREAMS += [(f"w1_{_l}1", 22, 2048), (f"w2_{_l}1", 16, 1408)]
for _l in range(DEPTH):
    STREAMS += [(f"mla_r{_l}", 4, 2048), (f"mla_in{_l}", 15, 2048), (f"rnn_gate{_l}", 1, 2048), (f"mla_uq{_l}", 4, 1152),
                (f"mla_uk{_l}", 1, 2048), (f"mla_uv{_l}", 1, 2048),
                (f"mla_out{_l}", 4, 2048), (f"up{_l}", 24, 2048), (f"down{_l}", 16, 1536)]
BASE = {}
_n = 0
for _name, _slots, _w in STREAMS:
    BASE[_name] = _n
    _n += _slots
SLOTS = _n

PARAMS = [("ada_b", 288), ("norm_g", 96), ("dn_conv", 120), ("dn_a", 64), ("dn_dt", 64), ("dn_gain", 1),
          ("q_gain", 1), ("k_gain", 1), ("sink", 16), ("conv_w", 64), ("conv_b", 16), ("gx_b", 16), ("ga_b", 16),
          ("lam", 16), ("qn_g", 6), ("kvn_g", 4), ("ln1_g", 16), ("ln1_b", 16), ("ln2_g", 16), ("ln2_b", 16),
          ("fc_w", 288), ("fc_b", 96), ("cond", 16)]
POFF = {}
_n = 0
for _name, _w in PARAMS:
    POFF[_name] = _n
    _n += _w
NPARAM = _n
PW = dict(PARAMS)

CONSTS = [("eps", 1), ("ident", 128), ("ones", 128), ("level", 2 * LEVELS * 128), ("incl", 2 * 128)]
COFF = {}
_n = 0
for _name, _w in CONSTS:
    COFF[_name] = _n
    _n += _w
NCONST = _n


LATE = [("s_cos", 256), ("s_sin", 256), ("s_swap", 128), ("s_ones", 128), ("s_mask", 1024),
        ("m_swap", 128), ("m_mask", 384), ("m_freq", 1), ("m_sign", 1)]
TABLES = [("pos", 256), ("m_cos", 256), ("m_sin", 256), ("t0", 256), ("t1", 256), ("nspl", 16), ("sp", 96)]
LOFF = {}
_n = 0
for _name, _w in LATE + TABLES:
    LOFF[_name] = _n
    _n += _w
LW = dict(LATE + TABLES)
NLATE = LOFF["pos"]
TWO_PI = [6.28125, float(np.round((2 * np.pi - 6.28125) * 2 ** 21) / 2 ** 21)]
TWO_PI.append(float(2 * np.pi - TWO_PI[0] - TWO_PI[1]))
ROUND = 1.5 * 2.0 ** 23
PI_IN = 3.1415925


def late_constants():
    c = np.zeros((P, NLATE), np.float32)

    def put(name, v):
        c[:, LOFF[name]:LOFF[name] + LW[name]] = v
    j, i = np.meshgrid(np.arange(P), np.arange(P), indexing="ij")
    freq = np.float32(10000.0) ** (-np.arange(16, dtype=np.float32) / np.float32(16))
    t = np.arange(SEQ)
    ang = np.concatenate([(t // 64).astype(np.float32)[:, None] * freq, (t % 64).astype(np.float32)[:, None] * freq], 1)
    put("s_cos", np.tile(np.cos(ang).T, (4, 1)))
    put("s_sin", np.tile(np.concatenate([-np.sin(ang).T, np.sin(ang).T]), (2, 1)))
    put("s_swap", (j // 64 == i // 64) & ((j % 64 + 32) % 64 == i % 64))
    put("s_ones", j // 64 == i // 64)
    m = np.zeros((P, 2, T), np.float32)
    for blk in range(2):
        q = blk * P + np.arange(P)
        m[:, blk, CTX:] = np.where(np.abs(q[:, None] - t[None, :]) <= WINDOW, 0.0, -1e30)
    put("s_mask", m.reshape(P, -1))
    put("m_swap", (j >= 64) & (j < 96) & (i >= 64) & (i < 96) & ((j - 64 + 16) % 32 == i - 64))
    causal = np.where(j >= i, 0.0, -1e30)
    put("m_mask", np.concatenate([causal, np.zeros((P, P)), causal], 1))
    p = np.arange(P)
    inv = np.float32(10000.0) ** (-np.arange(0, 32, 2, dtype=np.float32) / np.float32(32))
    put("m_freq", inv[p % 16][:, None])
    put("m_sign", np.where(p % 32 < 16, -1.0, 1.0)[:, None])
    return c


def constants():
    c = np.zeros((P, NCONST), np.float32)
    j, i = np.meshgrid(np.arange(P), np.arange(P), indexing="ij")
    c[:, COFF["eps"]] = EPS
    c[:, COFF["ident"]:COFF["ident"] + 128] = j == i
    c[:, COFF["ones"]:COFF["ones"] + 128] = 1.0
    for s in range(2):
        a, b = (j, i) if s == 0 else (i, j)
        c[:, COFF["incl"] + 128 * s:COFF["incl"] + 128 * (s + 1)] = a <= b
        for n in range(LEVELS):
            m = 1 << n
            at = COFF["level"] + (s * LEVELS + n) * 128
            c[:, at:at + 128] = -1.0 * ((a // (2 * m) == b // (2 * m)) & ((a // m) % 2 == 0) & ((b // m) % 2 == 1))
    return c


def build(nc, A, out):
    es = ExitStack()
    with es:
        def sb(name, shape, dt=F32):
            return es.enter_context(nc.sbuf_tensor(name, shape, dt))

        def sem(name):
            return es.enter_context(nc.semaphore(name))

        x = sb("x", [P, DC, T])
        h = sb("h", [P, DC, T])
        ring = sb("ring", [P, RING, SLOT])
        big = sb("big", [P, 24 * T])
        core = sb("core", [P, 30 * 512])
        zbuf = sb("zbuf", [P, 8 * T])
        par = sb("par", [P, NPARAM])
        con = sb("con", [P, NCONST])
        mod = sb("mod", [P, 6, 3, 16])
        amp = sb("amp", [P, 6, 16])
        hgate = sb("hgate", [P, 6, 16])
        cond = sb("cond", [P, DC, 2])
        ctmp = sb("ctmp", [P, DC, 2])
        tok = sb("tok", [P, 8, 64])

        psum = [es.enter_context(nc.psum_tensor(f"bank{i}", [P, BANK], F32)) for i in range(8)]
        OUT_BANK, STAT, MISC = 4, 6, 7

        def p_(name, a=0, n=None):
            o = POFF[name] + a
            return par[:, o:o + (PW[name] - a if n is None else n)]

        def incl(s):
            return con[:, COFF["incl"] + 128 * s:COFF["incl"] + 128 * (s + 1)]

        def level(s, n):
            o = COFF["level"] + (s * LEVELS + n) * 128
            return con[:, o:o + 128]

        ident = con[:, COFF["ident"]:COFF["ident"] + 128]
        ones = con[:, COFF["ones"]:COFF["ones"] + 128]
        eps = con[:, COFF["eps"]:COFF["eps"] + 1]

        hid = big[:, 0:FHC * T].rearrange("p (c t) -> p c t", t=T)
        std = core[:, 0:512]
        rstd = core[:, 512:1024]
        tanh2 = core[:, 1024:2048].rearrange("p (b t) -> p b t", b=2)
        swu2 = core[:, 2048:3072].rearrange("p (b t) -> p b t", b=2)

        def late(name, a=0, n=None):
            o = LOFF[name] + a
            return zbuf[:, o:o + (LW[name] - a if n is None else n)]

        sqk = big[:, 0:10 * T].rearrange("p (c t) -> p c t", t=T)
        svt = big[:, 10 * T:12 * T].rearrange("p (c f) -> p c f", f=256)
        stage_q = core[:, 13312:13312 + 2 * 512].rearrange("p (b t) -> p b t", b=2)
        stage_v = core[:, 14336:14336 + 2 * 256].rearrange("p (b c f) -> p b c f", b=2, c=2)
        logit = core[:, 0:1024].rearrange("p (b t) -> p b t", b=2)
        expo = core[:, 1024:2048].rearrange("p (b t) -> p b t", b=2)
        probt = core[:, 2048:3072].rearrange("p (b t) -> p b t", b=2)
        small = core[:, 14848:14848 + 8 * 8].rearrange("p (n u) -> p n u", n=8)
        by8 = lambda ap: ap.rearrange("p (c t) -> p c t", t=SEQ)
        xc = by8(big[:, 0:2048])
        gelu_in = big[:, 2048:4096]
        gate_a_b = big[:, 4096:8192]
        gate_a, gate_b = big[:, 4096:6144], big[:, 6144:8192]
        lat = by8(big[:, 8192:9472])
        vtok = big[:, 9472:11520].rearrange("p (c f) -> p c f", f=1024)
        kpe = big[:, 11520:11776]
        mhid = by8(big[:, 0:FC2 * SEQ])
        mq = by8(core[:, 3072:3072 + 4096])
        mk = by8(core[:, 7168:7168 + 4096])
        mtmp = core[:, 11264:13312]
        lat_sq = by8(core[:, 0:1280])
        lat_std = core[:, 1280:1792]
        lat_r = core[:, 1792:2304]
        rx, ra = core[:, 3072:5120], core[:, 5120:7168]
        rdec, re2, rth = core[:, 7168:9216], core[:, 9216:11264], core[:, 11264:13312]
        hlow, hhigh = h[:, :, 0:SEQ], h[:, :, SEQ:T]
        ln_mu, ln_std, ln_r = core[:, 14912:15168], core[:, 0:256], core[:, 256:512]
        conv_g = core[:, 512:1024].rearrange("p (b t) -> p b t", b=2)
        conv_v = core[:, 1024:1536].rearrange("p (b t) -> p b t", b=2)
        gsq = core[:, 1536:2048].rearrange("p (b t) -> p b t", b=2)
        gpoly = core[:, 2048:2560].rearrange("p (b t) -> p b t", b=2)
        gtanh = core[:, 2560:3072].rearrange("p (b t) -> p b t", b=2)

        qkv = big[:, 0:24 * T].rearrange("p (c t) -> p c t", t=T)
        zs = zbuf[:, :].rearrange("p (c t) -> p c t", t=T)
        conv2 = core[:, 3072:4096].rearrange("p (b t) -> p b t", b=2)
        ttmp = core[:, 4096:5120].rearrange("p (b t) -> p b t", b=2)
        sqh = core[:, 5120:5120 + 4 * 512].rearrange("p (b t) -> p b t", b=4)
        dstd = core[:, 7168:7168 + 8 * 512].rearrange("p (b t) -> p b t", b=8)
        grec = core[:, 11264:11264 + 4 * 512].rearrange("p (b t) -> p b t", b=4)
        TOK_G, TOK_BETA, TOK_GC, TOK_EGC, TOK_BEG, TOK_T1, TOK_T2, TOK_T3 = range(8)

        def tokv(n):
            return tok[:, n, :]

        QN = ["K", "V", "TG", "TB", "DT", "EG", "QD", "LT", "M0", "M1", "X", "XT", "Y", "KD", "S"]
        quad = [{q: core[:, (s * len(QN) + n) * 512:(s * len(QN) + n + 1) * 512].rearrange("p (h t) -> p h t", h=QUAD)
                 for n, q in enumerate(QN)} for s in range(2)]
        dbank = [[psum[4 * s + n][:, :].rearrange("p (h t) -> p h t", h=QUAD) for n in range(4)] for s in range(2)]

        landed = [sem(f"landed{i}") for i in range(RING)]
        slots_used = sem("slots_used")
        inputs_in = sem("inputs_in")
        cond_done = sem("cond_done")
        mod_done = sem("mod_done")
        x_done = sem("x_done")
        sq_done = sem("sq_done")
        stat_done = sem("stat_done")
        std_done = sem("std_done")
        xn_done = sem("xn_done")
        h0_done = sem("h0_done")
        h1_done = sem("h1_done")
        tanh_done = sem("tanh_done")
        hid_done = sem("hid_done")
        stored = sem("stored")
        dve_step = sem("dve_step")
        dve_turn = sem("dve_turn")
        act_step = sem("act_step")
        pool_step = sem("pool_step")
        pool_turn = sem("pool_turn")

        pr_free = sem("pr_free")
        pr_tanh = sem("pr_tanh")
        conv_done = sem("conv_done")
        hs_done = sem("hs_done")
        hsum_done = sem("hsum_done")
        hstd_done = sem("hstd_done")
        hnorm_done = sem("hnorm_done")
        gate_step = sem("gate_step")
        gate_pe = sem("gate_pe")
        gate_act = sem("gate_act")
        gates_done = sem("gates_done")
        y_in_done = sem("y_in_done")
        late_in = sem("late_in")
        sw_done = sem("sw_done")
        rot_done = sem("rot_done")
        rope_done = sem("rope_done")
        at = {nm: sem(f"at_{nm}") for nm in ("q", "s", "m", "e", "p", "t", "tc", "o", "od")}
        tab_dve = sem("tab_dve")
        tab_act = sem("tab_act")
        xc_done = sem("xc_done")
        pj_done = sem("pj_done")
        rg_done = sem("rg_done")
        rt_done = sem("rt_done")
        rl_dve = sem("rl_dve")
        rl_act = sem("rl_act")
        ml_sq = sem("ml_sq")
        ml_sum = sem("ml_sum")
        ml_std = sem("ml_std")
        ml_n = sem("ml_n")
        uq_done = sem("uq_done")
        uk_done = sem("uk_done")
        uv_done = sem("uv_done")
        kpe_done = sem("kpe_done")
        kb_done = sem("kb_done")
        merged = sem("merged")
        ln_mean = sem("ln_mean")
        ln_cent = sem("ln_cent")
        ln_sq = sem("ln_sq")
        ln_var = sem("ln_var")
        ln_root = sem("ln_root")
        ln_done = sem("ln_done")
        cg_done = sem("cg_done")
        gs_done = sem("gs_done")
        gp_done = sem("gp_done")
        gt_done = sem("gt_done")
        h2_done = sem("h2_done")
        dn = {}
        for nm in ("staged", "gr", "kq", "eg", "d", "dt", "dtm", "lt", "qg", "xt0", "mt", "xtr", "ttok", "x0", "toks",
                   "y", "yc", "z", "xu", "wt", "nw", "vmm", "vn", "end", "state"):
            dn[nm] = [sem(f"dn_{nm}{s}") for s in range(2)]

        class Steps:

            def __init__(self, eng, s):
                self.eng, self.s, self.n = eng, s, 0

            def __call__(self, ins):
                self.n += 1
                ins.then_inc(self.s, 1)
                self.eng.wait_ge(self.s, self.n)

            def last(self, ins):
                self(ins)
                self.eng.sem_clear(self.s)
                self.n = 0

        def over_slots(eng, slots, body):
            full = slots // RING
            if full > 1:
                with eng.Fori(0, full) as i:
                    for u in range(RING):
                        body(i * RING + u, i, u)
                rest = range(full * RING, slots)
            else:
                rest = range(slots)
            for n in rest:
                body(n, n // RING, n % RING)

        def weights(eng, name, i, u):
            k = BASE[name] + u
            eng.wait_ge(landed[k % RING], 16 * (i + (k // RING + 1)))
            return ring[:, k % RING, :]

        def used(name, n):
            return BASE[name] + n + 1

        block = es.enter_context(nc.Block())

        @block.sync
        def _(sp):
            sp.dma_start(x[:, :, :], A["x_t"]).then_inc(inputs_in, 16)
            for name, slots, width in STREAMS:

                def load(n, i, u, name=name, width=width):
                    k = BASE[name] + u
                    if not (name == "ada" and isinstance(n, int) and n < RING):
                        sp.wait_ge(slots_used, n + (BASE[name] - RING + 1))
                    sp.dma_start(ring[:, k % RING, 0:width], A[name][n, :, :]).then_inc(landed[k % RING], 16)

                if name == "ada":
                    for n in range(RING):
                        load(n, 0, n)
                    with sp.Fori(1, slots // RING) as i:
                        for u in range(RING):
                            load(i * RING + u, i, u)
                else:
                    over_slots(sp, slots, load)

            sp.wait_ge(ln_done, 4)
            sp.dma_start(out, x[:, :, CTX:T]).then_inc(stored, 16)
            sp.wait_ge(stored, 16)

        @block.tensor
        def _(pe):
            def column_sum(k, n_chunks, t0):
                for c in range(n_chunks):
                    pe.wait_ge(sq_done, DC * k + c + 1)
                    mm = pe.matmul(psum[STAT][:, t0:T], ones, h[:, c, t0:T], start=(c == 0), stop=(c == n_chunks - 1))
                mm.then_inc(stat_done, 1)

            def ada():
                pe.wait_ge(cond_done, 1)

                def slot(n, i, u):
                    w = weights(pe, "ada", i, u)
                    for q in range(2):
                        for c in range(DC):
                            mm = pe.matmul(psum[MISC][:, bass.ds(n * 4 + 2 * q, 2)],
                                           w[:, c * 256 + q * 128:c * 256 + (q + 1) * 128], cond[:, c, :],
                                           start=(c == 0), stop=(c == DC - 1))
                    mm.then_inc(slots_used, 1)
                over_slots(pe, 72, slot)

            def ffn(f, k, t0):
                l, half = divmod(f, 2)
                name = f"w1_{l}{half}"

                def up(n, i, u):
                    w = weights(pe, name, i, u)
                    pe.wait_ge(hid_done, n + (FHC * f + 1))
                    for q in range(2):
                        for c in range(DC):
                            mm = pe.matmul(psum[2 * q + u % 2][:, t0:T], w[:, c * 256 + q * 128:c * 256 + (q + 1) * 128],
                                           h[:, c, t0:T], start=(c == 0), stop=(c == DC - 1))
                    mm.then_inc(slots_used, 1)
                normed(k, t0)
                over_slots(pe, FHC, up)
                pe.wait_ge(hid_done, CREDIT + FHC * (f + 1))
                project_out(f"w2_{l}{half}", k, hid, 11, 2, t0)

            def normed(k, t0):
                if t0 == 0:
                    pe.wait_ge(h0_done, DC * (k + 1))
                pe.wait_ge(h1_done, DC * (k + 1))

            def project_out(name, k, src, kc, parts, t0, s0=None):
                s0 = t0 if s0 is None else s0
                s1 = s0 + T - t0

                def slot(n, i, u):
                    w = weights(pe, name, i, u)
                    if parts == 2:
                        o, part = u // 2, u % 2
                        if part == 0:
                            pe.wait_ge(x_done, i * 2 + (DC * k + o + 1))
                        for c in range(kc):
                            mm = pe.matmul(psum[OUT_BANK + o][:, t0:T], w[:, c * 128:(c + 1) * 128],
                                           src[:, part * kc + c, s0:s1], start=(part == 0 and c == 0),
                                           stop=(part == 1 and c == kc - 1))
                    else:
                        for q in range(2):
                            pe.wait_ge(x_done, 2 * n + (DC * k + q + 1))
                            for c in range(kc):
                                mm = pe.matmul(psum[OUT_BANK + q][:, t0:T], w[:, (q * kc + c) * 128:(q * kc + c + 1) * 128],
                                               src[:, c, s0:s1], start=(c == 0), stop=(c == kc - 1))
                    mm.then_inc(slots_used, 1)
                over_slots(pe, 2 * DC if parts == 2 else DC // 2, slot)

            def delta_in(k):
                normed(k, 0)

                def slot(n, i, u):
                    w = weights(pe, "dn_in", i, u)
                    for q in range(2):
                        bank = (2 * u + q) % 4
                        pe.wait_ge(pr_free, 2 * n + (q + 1))
                        for c in range(DC):
                            mm = pe.matmul(psum[bank][:, :], w[:, c * 256 + q * 128:c * 256 + (q + 1) * 128], h[:, c, :],
                                           start=(c == 0), stop=(c == DC - 1))
                    mm.then_inc(slots_used, 1)
                over_slots(pe, 16, slot)
                w = weights(pe, "dn_ab", 0, 0)
                for tc in range(4):
                    for c in range(DC):
                        mm = pe.matmul(psum[MISC][:, tc * 32:(tc + 1) * 32], h[:, c, tc * CK:(tc + 1) * CK],
                                       w[:, c * 32:(c + 1) * 32], start=(c == 0), stop=(c == DC - 1))
                mm.then_inc(slots_used, 1)
                for c in range(16):
                    pe.wait_ge(hs_done, c + 1)
                    if c >= 2:
                        pe.wait_ge(hstd_done, c - 1)
                    pe.matmul(psum[4 + c % 2][:, :], ones, sqh[:, c % 4, :], start=True, stop=True).then_inc(hsum_done, 1)
                pe.wait_ge(gates_done, 1)
                for s in range(2):
                    mm = pe.matmul(psum[MISC][:, 32 * s:32 * (s + 1)], incl(s), tokv(TOK_G)[:, 32 * s:32 * (s + 1)],
                                   start=True, stop=True)
                mm.then_inc(gate_pe, 1)

            def delta_core():
                pe.wait_ge(gates_done, 2)
                pe.wait_ge(hnorm_done, 16)
                with pe.Fori(0, 2) as hg:
                    with pe.Fori(0, 2) as cp:
                        for cc in range(2):
                            delta_unit_pe(hg, cp, cc)

            def delta_unit_pe(hg, cp, cc):
                U = hg * 4 + cp * 2 + cc
                for s in range(2):
                    q, b = quad[s], dbank[s]
                    tc = 2 * cp + (cc if s == 0 else 1 - cc)
                    pe.wait_ge(dn["staged"][s], 4 * U + 4)
                    pe.wait_ge(dn["state"][s], U + hg + 1)
                    pe.matmul(psum[4 * s][:, :], ones, q["TG"].rearrange("p h t -> p (h t)"), start=True, stop=True)\
                        .then_inc(dn["gr"][s], 1)
                    pe.matmul(psum[4 * s + 1][:, :], ones, q["TB"].rearrange("p h t -> p (h t)"), start=True, stop=True)
                    for hd in range(QUAD):
                        pe.matmul(b[2][:, hd, :], q["K"][:, hd, :], q["K"][:, hd, :], start=True, stop=True)
                    for hd in range(QUAD):
                        mm = pe.matmul(b[3][:, hd, :], q["K"][:, hd, :],
                                       big[:, bass.ds(hg * (QUAD * T) + tc * CK + hd * T, CK)], start=True, stop=True)
                    mm.then_inc(dn["kq"][s], 1)
                for s in range(2):
                    q, b = quad[s], dbank[s]
                    pe.wait_ge(dn["xt0"][s], U + 1)
                    for hd in range(QUAD):
                        mm = pe.transpose(b[0][:, hd, :], q["XT"][:, hd, :], ident)
                    mm.then_inc(dn["xtr"][s], 1)
                    for hd in range(QUAD):
                        pe.transpose(b[2][:, hd, :], q["K"][:, hd, :], ident)
                    for hd in range(QUAD):
                        mm = pe.transpose(b[3][:, hd, :], q["V"][:, hd, :], ident)
                    mm.then_inc(dn["ttok"][s], 1)
                for n in range(1, LEVELS):
                    for s in range(2):
                        q, b = quad[s], dbank[s]
                        if n == 1:
                            pe.wait_ge(dn["x0"][s], U + 1)
                            pe.wait_ge(dn["toks"][s], U + 1)
                        else:
                            pe.wait_ge(dn["xu"][s], U * (LEVELS - 1) + n - 1)
                        pe.wait_ge(dn["mt"][s], U * (LEVELS - 1) + n)
                        for hd in range(QUAD):
                            mm = pe.matmul(b[0][:, hd, :], q[f"M{n % 2}"][:, hd, :], q["X"][:, hd, :], start=True, stop=True)
                        mm.then_inc(dn["y"][s], 1)
                    for s in range(2):
                        q, b = quad[s], dbank[s]
                        pe.wait_ge(dn["yc"][s], U * (LEVELS - 1) + n)
                        if n < LEVELS - 1:
                            for hd in range(QUAD):
                                pe.matmul(b[1][:, hd, :], q["XT"][:, hd, :], q["Y"][:, hd, :], start=True, stop=True)
                        for hd in range(QUAD):
                            mm = pe.matmul(b[2][:, hd, :], q["Y"][:, hd, :], q["XT"][:, hd, :], start=True, stop=True)
                        mm.then_inc(dn["z"][s], 1)
                for s in range(2):
                    q, b = quad[s], dbank[s]
                    pe.wait_ge(dn["xu"][s], U * (LEVELS - 1) + LEVELS - 1)
                    for hd in range(QUAD):
                        mm = pe.matmul(b[0][:, hd, :], q["K"][:, hd, :], q["XT"][:, hd, :], start=True, stop=True)
                    mm.then_inc(dn["wt"][s], 1)
                for s in range(2):
                    q, b = quad[s], dbank[s]
                    pe.wait_ge(dn["nw"][s], U + 1)
                    for hd in range(QUAD):
                        pe.matmul(b[1][:, hd, :], q["XT"][:, hd, :], q["V"][:, hd, :], start=True, stop=False)
                        mm = pe.matmul(b[1][:, hd, :], q["Y"][:, hd, :], q["S"][:, hd, :], start=False, stop=True)
                    mm.then_inc(dn["vmm"][s], 1)
                for s in range(2):
                    q, b = quad[s], dbank[s]
                    pe.wait_ge(dn["vn"][s], U + 1)
                    pe.wait_ge(dn["qg"][s], U + 1)
                    for hd in range(QUAD):
                        pe.matmul(b[2][:, hd, :], q["S"][:, hd, :], q["TB"][:, hd, :], start=True, stop=False)
                        pe.matmul(b[2][:, hd, :], q["X"][:, hd, :], q["QD"][:, hd, :], start=False, stop=True)
                    for hd in range(QUAD):
                        mm = pe.matmul(b[3][:, hd, :], q["KD"][:, hd, :], q["X"][:, hd, :], start=True, stop=True)
                    mm.then_inc(dn["end"][s], 1)

            def delta_out(k):
                for c in range(DNH):
                    pe.wait_ge(hs_done, 16 + c + 1)
                    if c >= 2:
                        pe.wait_ge(hstd_done, 16 + c - 1)
                    pe.matmul(psum[6 + c % 2][:, :], ones, sqh[:, c % 4, :], start=True, stop=True).then_inc(hsum_done, 1)
                pe.wait_ge(y_in_done, DNH)
                project_out("dn_out", k, h, DC, 1, 0)

            def window(k):
                normed(k, 0)
                for n in range(5):
                    w = weights(pe, "swa_qk", n // RING, n % RING)
                    t0 = CTX if n < 4 else 0
                    for q in range(2):
                        m = 2 * n + q
                        if m >= 4:
                            pe.wait_ge(sw_done, m - 3)
                        for c in range(DC):
                            mm = pe.matmul(psum[m % 4][:, t0:T], w[:, c * 256 + q * 128:c * 256 + (q + 1) * 128],
                                           h[:, c, t0:T], start=(c == 0), stop=(c == DC - 1))
                    mm.then_inc(slots_used, 1)
                w = weights(pe, "swa_v", 0, 0)
                for tc in range(4):
                    pe.wait_ge(sw_done, 7 + tc)
                    for c in range(DC):
                        mm = pe.matmul(psum[(tc + 2) % 4][:, 0:256], h[:, c, tc * P:(tc + 1) * P], w[:, c * 256:(c + 1) * 256],
                                       start=(c == 0), stop=(c == DC - 1))
                mm.then_inc(slots_used, 1)
                for c in range(10):
                    t0 = CTX if c < 8 else 0
                    pe.wait_ge(hs_done, 24 + c + 1)
                    if c == 0:
                        pe.wait_ge(late_in, 32)
                    if c >= 2:
                        pe.wait_ge(hstd_done, 24 + c - 1)
                    pe.matmul(psum[4 + c % 2][:, t0:T], late("s_ones"), sqh[:, c % 4, t0:T], start=True, stop=True)\
                        .then_inc(hsum_done, 1)
                    if c >= 1:
                        rotate(c - 1)
                rotate(9)
                pe.wait_ge(rope_done, 10)
                for kvp in range(2):
                    with pe.Fori(0, 2) as i:
                        attend_pe(8, lambda U: U + i * 8 + kvp * 16, lambda u: scores(kvp, u),
                                  lambda u: values(kvp, u), 4, lambda u: 2 * (kvp * 2 + i) + u // 4 + 1)
                pe.wait_ge(at["od"], CREDIT + 32)
                project_out("swa_out", k, h, DC, 1, CTX)

            def rotate(c):
                pe.wait_ge(hnorm_done, 24 + c + 1)
                if c >= 2:
                    pe.wait_ge(rope_done, c - 1)
                pe.matmul(psum[6 + c % 2][:, 0:SEQ], late("s_swap"), sqk[:, c, CTX:T], start=True, stop=True).then_inc(rot_done, 1)

            def scores(kvp, u):
                b, j, r = u // 4, u // 2 % 2, u % 2
                pe.matmul(psum[u % 2][:, :], stage_q[64 * r:64 * r + 64, b, j * P:(j + 1) * P], sqk[64 * r:64 * r + 64, 8 + kvp, :],
                          start=True, stop=True).then_inc(at["s"], 1)

            def values(kvp, u):
                r = u % 2
                kv = 2 * kvp + r
                for c in range(4):
                    mm = pe.matmul(psum[4 + u % 2][64 * r:64 * r + 64, 0:P], svt[:, c, kv * SD:(kv + 1) * SD],
                                   probt[:, u % 2, c * P:(c + 1) * P], start=(c == 0), stop=(c == 3))
                mm.then_inc(at["o"], 1)

            def attend_pe(units, at_unit, score, value, blocks, staged):
                for t in range(units + 2):
                    if t < units:
                        pe.wait_ge(at["q"], staged(t))
                        score(t)
                    if 1 <= t <= units:
                        u = t - 1
                        pe.wait_ge(at["p"], at_unit(u + 1))
                        for c in range(blocks):
                            mm = pe.transpose(psum[2 + u % 2][:, c * P:(c + 1) * P], expo[:, u % 2, c * P:(c + 1) * P], ident)
                        mm.then_inc(at["t"], 1)
                    if t >= 2:
                        u = t - 2
                        pe.wait_ge(at["tc"], at_unit(u + 1))
                        pe.wait_ge(at["od"], at_unit(u + 1))
                        value(u)

            def block2(l):
                def rnn_in(n):
                    w = weights(pe, f"mla_r{l}", 0, n)
                    for q in range(2):
                        m = 2 * n + q
                        if m >= 4:
                            pe.wait_ge(xc_done, 8 * l + m - 3)
                        for c in range(DC):
                            mm = pe.matmul(psum[m % 4][:, 0:SEQ], w[:, c * 256 + q * 128:c * 256 + (q + 1) * 128],
                                           x[:, c, CTX:T], start=(c == 0), stop=(c == DC - 1))
                    mm.then_inc(slots_used, 1)
                pe.wait_ge(x_done, CREDIT + 48 + 2 * DC * l)
                for n in range(4):
                    rnn_in(n)

                def proj(n, i, u):
                    w = weights(pe, f"mla_in{l}", i, u)
                    for q in range(2):
                        pe.wait_ge(pj_done, 2 * n + (30 * l + q + 1))
                        for c in range(DC):
                            mm = pe.matmul(psum[(2 * u + q) % 4][:, 0:SEQ], w[:, c * 256 + q * 128:c * 256 + (q + 1) * 128],
                                           x[:, c, CTX:T], start=(c == 0), stop=(c == DC - 1))
                    mm.then_inc(slots_used, 1)
                pe.wait_ge(xc_done, 8 * l + 8)
                over_slots(pe, 15, proj)
                pe.wait_ge(ml_sq, l + 1)
                for c in range(QL):
                    pe.matmul(psum[STAT][:, 0:SEQ], ones, lat_sq[:, c, :], start=(c == 0), stop=(c == QL - 1))
                for c in range(KVL):
                    mm = pe.matmul(psum[STAT][:, SEQ:T], ones, lat_sq[:, QL + c, :], start=(c == 0), stop=(c == KVL - 1))
                mm.then_inc(ml_sum, 1)
                w = weights(pe, f"rnn_gate{l}", 0, 0)
                pe.wait_ge(pj_done, 4 + 30 * (l + 1))
                for c in range(RC):
                    if c >= 4:
                        pe.wait_ge(rt_done, RC * l + c - 3)
                    pe.matmul(psum[c % 4][:, 0:SEQ], w[:, c * P:(c + 1) * P], xc[:, c, :], start=True, stop=True)
                    mm = pe.matmul(psum[c % 4][:, SEQ:T], w[:, (RC + c) * P:(RC + c + 1) * P], xc[:, c, :], start=True, stop=True)
                    mm.then_inc(rg_done, 1)
                pe.matmul(psum[MISC][:, 0:1], ones, eps, start=True, stop=True).then_inc(slots_used, 1)
                pe.wait_ge(ml_n, l + 1)
                pe.wait_ge(rl_dve, 4 * (l + 1))
                for n in range(4):
                    w = weights(pe, f"mla_uq{l}", 0, n)
                    for q in range(2):
                        m = 2 * n + q
                        if m >= 4:
                            pe.wait_ge(uq_done, 20 * l + m - 3)
                        for e in range(2):
                            hd = 2 * q + e
                            for c in range(QL):
                                mm = pe.matmul(psum[m % 4][0:96, e * SEQ:(e + 1) * SEQ], w[:, c * 384 + hd * 96:c * 384 + hd * 96 + 96],
                                               lat[:, c, :], start=(c == 0), stop=(c == QL - 1))
                    mm.then_inc(slots_used, 1)
                w = weights(pe, f"mla_uk{l}", 0, 0)
                for m in range(8):
                    pe.wait_ge(uq_done, 20 * l + 8 + m - 3)
                    for e in range(2):
                        hd = 2 * m + e
                        for c in range(KVL):
                            mm = pe.matmul(psum[m % 4][0:64, e * SEQ:(e + 1) * SEQ], w[:, c * 1024 + hd * 64:c * 1024 + hd * 64 + 64],
                                           lat[:, QL + c, :], start=(c == 0), stop=(c == KVL - 1))
                    mm.then_inc(uk_done, 1)
                pe.matmul(psum[MISC][:, 0:1], ones, eps, start=True, stop=True).then_inc(slots_used, 1)
                w = weights(pe, f"mla_uv{l}", 0, 0)
                for m in range(4):
                    tc, half = divmod(m, 2)
                    pe.wait_ge(uq_done, 20 * l + 16 + m - 3)
                    for c in range(KVL):
                        mm = pe.matmul(psum[m % 4][:, :], lat[:, QL + c, tc * P:(tc + 1) * P],
                                       w[:, c * 1024 + half * 512:c * 1024 + half * 512 + 512], start=(c == 0), stop=(c == KVL - 1))
                    mm.then_inc(uv_done, 1)
                pe.matmul(psum[MISC][:, 0:1], ones, eps, start=True, stop=True).then_inc(slots_used, 1)
                for m in range(9):
                    if m >= 2:
                        pe.wait_ge(rope_done, 10 + 9 * l + m - 1)
                    if m == 0:
                        pe.wait_ge(tab_dve, 5)
                        pe.matmul(psum[4][0:96, 0:SEQ], late("m_swap")[64:96, 0:96], kpe[64:96, :], start=True, stop=True)\
                            .then_inc(rot_done, 1)
                    else:
                        pe.wait_ge(uq_done, 20 * l + m)
                        pe.matmul(psum[4 + m % 2][0:96, :], late("m_swap")[0:96, 0:96],
                                  mq[0:96, 2 * m - 2:2 * m, :].rearrange("p c t -> p (c t)"), start=True, stop=True).then_inc(rot_done, 1)
                pe.wait_ge(kb_done, l + 1)
                pe.wait_ge(uq_done, 20 * (l + 1))
                with pe.Fori(0, 4) as i:
                    attend_pe(4, lambda U: U + i * 4 + (32 + 16 * l), lambda u: mla_scores(i, u), mla_values, 3,
                              lambda u: 2 * i + (8 + 8 * l) + u // 2 + 1)
                pe.wait_ge(merged, l + 1)
                project_out(f"mla_out{l}", 6 + 2 * l, h, DC, 1, CTX)
                layer_norm(2 * l)

                def up(n, i, u):
                    w = weights(pe, f"up{l}", i, u)
                    pe.wait_ge(h2_done, n + (FC2 * l + 1))
                    for q in range(2):
                        for c in range(DC):
                            mm = pe.matmul(psum[u % 4][:, q * SEQ:(q + 1) * SEQ], w[:, c * 256 + q * 128:c * 256 + (q + 1) * 128],
                                           x[:, c, CTX:T], start=(c == 0), stop=(c == DC - 1))
                    mm.then_inc(slots_used, 1)
                pe.wait_ge(ln_done, 2 * l + 1)
                over_slots(pe, FC2, up)
                pe.wait_ge(h2_done, 4 + FC2 * (l + 1))
                project_out(f"down{l}", 7 + 2 * l, mhid, 12, 2, CTX, 0)
                layer_norm(2 * l + 1)
                if l < DEPTH - 1:
                    pe.wait_ge(ln_done, 2 * l + 2)

            def mla_scores(i, u):
                b, e = u // 2, u % 2
                keys = lambda n: mk[0:96, bass.ds(i * 4 + u, 1), 0:n].rearrange("p a t -> p (a t)")
                pe.matmul(psum[u % 2][:, 0:P], stage_q[0:96, b, e * SEQ:e * SEQ + P], keys(P), start=True, stop=True)
                pe.matmul(psum[u % 2][:, P:3 * P], stage_q[0:96, b, e * SEQ + P:e * SEQ + 2 * P], keys(SEQ), start=True, stop=True)\
                    .then_inc(at["s"], 1)

            def mla_values(u):
                b, r = u // 2, u % 2
                dst = psum[4 + u % 2][64 * r:64 * r + 64, :]
                v = lambda c: stage_v[:, b, c, r * VH:(r + 1) * VH]
                pe.matmul(dst[:, 0:P], v(0), probt[:, u % 2, 0:P], start=True, stop=True)
                pe.matmul(dst[:, P:2 * P], v(0), probt[:, u % 2, P:2 * P], start=True, stop=False)
                pe.matmul(dst[:, P:2 * P], v(1), probt[:, u % 2, 2 * P:3 * P], start=False, stop=True).then_inc(at["o"], 1)

            def layer_norm(m):
                for c in range(DC):
                    pe.wait_ge(x_done, CREDIT + 48 + DC * m + c + 1)
                    mm = pe.matmul(psum[STAT][:, 0:SEQ], ones, x[:, c, CTX:T], start=(c == 0), stop=(c == DC - 1))
                mm.then_inc(ln_mean, 1)
                for c in range(DC):
                    pe.wait_ge(ln_sq, DC * m + c + 1)
                    mm = pe.matmul(psum[STAT][:, SEQ:T], ones, hlow[:, c, :], start=(c == 0), stop=(c == DC - 1))
                mm.then_inc(ln_var, 1)

            pe.wait_ge(inputs_in, 48)
            ada()
            for l in range(DEPTH):
                for sub in range(3):
                    k = 3 * l + sub
                    t0 = CTX if k == 5 else 0
                    column_sum(k, DC, t0)
                    if sub != 1:
                        ffn(2 * l + sub // 2, k, t0)
                    if k == 4:
                        window(k)
                    if k == 1:
                        delta_in(k)
                        delta_core()
                        delta_out(k)

            for l in range(DEPTH):
                block2(l)

        @block.scalar
        def _(act):
            act.dma_start(par[:, :], A["params"]).then_inc(inputs_in, 16)
            act.dma_start(con[:, :], A["consts"]).then_inc(inputs_in, 16)
            act.wait_ge(inputs_in, 48)
            act.activation(ctmp[:, :, :], p_("cond").rearrange("p (c s) -> p c s", s=2), ACT.Tanh, scale=0.5)\
                .then_inc(act_step, 1)

            def norm(k, t0):
                act.wait_ge(x_done, CREDIT + DC * k)
                for c in range(DC):
                    act.activation(h[:, c, t0:T], x[:, c, t0:T], ACT.Square).then_inc(sq_done, 1)
                act.wait_ge(stat_done, k + 1)
                act.activation(std[:, t0:T], psum[STAT][:, t0:T], ACT.Sqrt, scale=1.0 / D, bias=eps).then_inc(std_done, 1)
                if t0 == 0:
                    act.wait_ge(mod_done, 1)
                    for c in range(DC):
                        act.wait_ge(xn_done, DC * k + c + 1)
                        act.activation(h[:, c, 0:CTX], h[:, c, 0:CTX], ACT.Identity, scale=amp[:, k, 2 * c:2 * c + 1],
                                       bias=mod[:, k, 0, 2 * c:2 * c + 1]).then_inc(h0_done, 1)

            def ffn(f, k, t0):
                l, half = divmod(f, 2)

                def slot(n, i, u):
                    act.wait_ge(slots_used, n + used(f"w1_{l}{half}", 0))
                    act.activation(tanh2[:, u % 2, t0:T], psum[u % 2][:, t0:T], ACT.Tanh, scale=0.5).then_inc(tanh_done, 1)
                over_slots(act, FHC, slot)

            def window(k):
                for m in range(10):
                    t0 = CTX if m < 8 else 0
                    act.wait_ge(slots_used, used("swa_qk", m // 2))
                    act.activation(sqk[:, m, t0:T], psum[m % 4][:, t0:T], ACT.Copy).then_inc(sw_done, 1)
                act.wait_ge(slots_used, used("swa_v", 0))
                for tc in range(4):
                    act.activation(svt[:, tc, :], psum[(tc + 2) % 4][:, 0:256], ACT.Copy).then_inc(sw_done, 1)
                for c in range(10):
                    t0 = CTX if c < 8 else 0
                    act.wait_ge(sw_done, c + 1)
                    if c >= 4:
                        act.wait_ge(hsum_done, 24 + c - 3)
                    act.activation(sqh[:, c % 4, t0:T], sqk[:, c, t0:T], ACT.Square).then_inc(hs_done, 1)
                    if c >= 1:
                        roots(c - 1, 24, 10, 1.0 / SD, 4, CTX if c - 1 < 8 else 0)
                roots(9, 24, 10, 1.0 / SD, 4)
                for kvp in range(2):
                    with act.Fori(0, 2) as i:
                        attend_act(8, lambda U: U + i * 8 + kvp * 16, lambda u: window_exp(kvp, i, u), 512)

            def window_exp(kvp, i, u):
                j, r = u // 2 % 2, u % 2
                sink = par[:, bass.ds(i * 2 + (POFF["sink"] + 4 * (2 * kvp + r) + u // 4), 1)]
                act.activation(expo[:, u % 2, :], logit[:, u % 2, :], ACT.Exp, bias=small[:, 1, u:u + 1],
                               accum_out=small[:, 2, u:u + 1])
                act.activation(small[:, 3, u:u + 1], sink, ACT.Exp, bias=small[:, 1, u:u + 1]).then_inc(at["e"], 1)

            def attend_act(units, at_unit, exps, width):
                for t in range(units + 1):
                    if t < units:
                        act.wait_ge(at["m"], at_unit(t + 1))
                        exps(t)
                    if t >= 1:
                        u = t - 1
                        act.wait_ge(at["t"], at_unit(u + 1))
                        act.activation(probt[:, u % 2, 0:width], psum[2 + u % 2][:, 0:width], ACT.Copy).then_inc(at["tc"], 1)

            def tables():
                act.wait_ge(tab_dve, 1)
                act.activation(late("sp", 0, 16), late("sp", 0, 16), ACT.Exp).then_inc(tab_act, 1)
                act.wait_ge(tab_dve, 2)
                act.activation(late("sp", 32, 16), late("sp", 16, 16), ACT.Ln).then_inc(tab_act, 1)
                act.wait_ge(tab_dve, 3)
                act.activation(late("m_sin"), late("t0"), ACT.Sin).then_inc(tab_act, 1)
                act.wait_ge(tab_dve, 4)
                act.activation(late("m_cos"), late("t0"), ACT.Sin).then_inc(tab_act, 1)

            def block2(l):
                if l == 0:
                    act.sem_inc(pj_done, 4)

                def proj(n, i, u):
                    for q in range(2):
                        if q == 0:
                            act.wait_ge(slots_used, n + used(f"mla_in{l}", 0))
                        m = 2 * n + q
                        src = psum[(2 * u + q) % 4][:, 0:SEQ]
                        if m < 8:
                            act.activation(gelu_in[:, m * SEQ:(m + 1) * SEQ], src, ACT.Copy).then_inc(pj_done, 1)
                        elif m < 13:
                            act.activation(lat[:, m - 8, :], src, ACT.Copy).then_inc(pj_done, 1)
                        elif m < 29:
                            act.activation(gate_a_b[:, (m - 13) * SEQ:(m - 12) * SEQ], src, ACT.Tanh, scale=0.5).then_inc(pj_done, 1)
                        else:
                            act.activation(kpe[64:96, :], src[64:96, :], ACT.Copy).then_inc(pj_done, 1)
                for n in range(15):
                    proj(n, n // RING, n % RING)
                act.wait_ge(pj_done, 4 + 30 * (l + 1))
                act.activation(core[:, 0:1280], big[:, 8192:9472], ACT.Square).then_inc(ml_sq, 1)
                act.wait_ge(ml_sum, l + 1)
                act.activation(lat_std[:, 0:SEQ], psum[STAT][:, 0:SEQ], ACT.Sqrt, scale=1.0 / (QL * P), bias=eps)
                act.activation(lat_std[:, SEQ:T], psum[STAT][:, SEQ:T], ACT.Sqrt, scale=1.0 / (KVL * P), bias=eps)\
                    .then_inc(ml_std, 1)
                for c in range(RC):
                    act.wait_ge(rg_done, RC * l + c + 1)
                    act.activation(rx[:, c * SEQ:(c + 1) * SEQ], psum[c % 4][:, 0:SEQ], ACT.Tanh, scale=0.5,
                                   bias=p_("gx_b", RC * l + c, 1))
                    act.activation(ra[:, c * SEQ:(c + 1) * SEQ], psum[c % 4][:, SEQ:T], ACT.Tanh, scale=0.5,
                                   bias=p_("ga_b", RC * l + c, 1)).then_inc(rt_done, 1)
                act.wait_ge(rl_dve, 4 * l + 1)
                act.activation(rdec, ra, ACT.Exp)
                act.activation(re2, ra, ACT.Exp, scale=2.0)
                act.activation(rth, ra, ACT.Tanh).then_inc(rl_act, 1)
                act.wait_ge(rl_dve, 4 * l + 2)
                act.activation(re2, re2, ACT.Sqrt, scale=-1.0).then_inc(rl_act, 1)
                act.activation(rth, gelu_in, ACT.Square).then_inc(rl_act, 1)
                act.wait_ge(rl_dve, 4 * l + 3)
                act.activation(rth, rth, ACT.Tanh, scale=GELU_C).then_inc(rl_act, 1)
                for m in range(20):
                    if m < 8:
                        act.wait_ge(slots_used, used(f"mla_uq{l}", m // 2))
                        act.activation(mq[0:96, 2 * m:2 * m + 2, :].rearrange("p c t -> p (c t)"), psum[m % 4][0:96, :], ACT.Copy)\
                            .then_inc(uq_done, 1)
                    elif m < 16:
                        c = m - 8
                        act.wait_ge(uk_done, 8 * l + c + 1)
                        act.activation(mk[0:64, 2 * c:2 * c + 2, :].rearrange("p c t -> p (c t)"), psum[m % 4][0:64, :], ACT.Copy)\
                            .then_inc(uq_done, 1)
                    else:
                        c = m - 16
                        act.wait_ge(uv_done, 4 * l + c + 1)
                        act.activation(vtok[:, c // 2, (c % 2) * 512:(c % 2) * 512 + 512], psum[m % 4][:, :], ACT.Copy)\
                            .then_inc(uq_done, 1)
                with act.Fori(0, 4) as i:
                    attend_act(4, lambda U: U + i * 4 + (32 + 16 * l), mla_exp, 384)
                layer_norm(2 * l)

                def gel(n, i, u):
                    act.wait_ge(cg_done, n + (FC2 * l + 1))
                    act.activation(gsq[:, u % 2, :], conv_g[:, u % 2, :], ACT.Square).then_inc(gs_done, 1)
                    act.wait_ge(gp_done, n + (FC2 * l + 1))
                    act.activation(gtanh[:, u % 2, :], gpoly[:, u % 2, :], ACT.Tanh, scale=GELU_C).then_inc(gt_done, 1)
                over_slots(act, FC2, gel)
                layer_norm(2 * l + 1)

            def mla_exp(u):
                act.activation(expo[:, u % 2, 0:P], logit[:, u % 2, 0:P], ACT.Exp, bias=small[:, 2, u:u + 1],
                               accum_out=small[:, 4, u:u + 1])
                act.activation(expo[:, u % 2, P:3 * P], logit[:, u % 2, P:3 * P], ACT.Exp, bias=small[:, 3, u:u + 1],
                               accum_out=small[:, 5, u:u + 1]).then_inc(at["e"], 1)

            def layer_norm(m):
                for c in range(DC):
                    act.wait_ge(ln_cent, DC * m + c + 1)
                    act.activation(hlow[:, c, :], hhigh[:, c, :], ACT.Square).then_inc(ln_sq, 1)
                act.wait_ge(ln_var, m + 1)
                act.activation(ln_std, psum[STAT][:, SEQ:T], ACT.Sqrt, scale=1.0 / D, bias=eps).then_inc(ln_root, 1)

            def delta(k):
                mine = Steps(act, act_step)
                mine.n = act_steps[0]

                def proj(n, i, u):
                    for q in range(2):
                        act.wait_ge(conv_done, 2 * n + (q + 1))
                        act.activation(ttmp[:, q, :], conv2[:, q, :], ACT.Tanh).then_inc(pr_tanh, 1)
                over_slots(act, 16, proj)
                for c in range(16):
                    if c >= 4:
                        act.wait_ge(hsum_done, c - 3)
                    if c == 0:
                        act.wait_ge(pr_free, 4 + 32)
                    act.activation(sqh[:, c % 4, :], qkv[:, c, :], ACT.Square).then_inc(hs_done, 1)
                    if c >= 1:
                        roots(c - 1, 0, 16, 1.0, 4)
                roots(15, 0, 16, 1.0, 4)
                act.wait_ge(gate_step, 1)
                mine(act.activation(tokv(TOK_T2), tokv(TOK_T2), ACT.Exp, scale=-1.0))
                mine(act.activation(p_("dn_a"), p_("dn_a"), ACT.Exp))
                act.activation(tokv(TOK_T2), tokv(TOK_T2), ACT.Ln, bias=ones[:, 0:1]).then_inc(gate_act, 1)
                act.activation(tokv(TOK_BETA), tokv(TOK_BETA), ACT.Tanh, scale=0.5).then_inc(gate_act, 1)
                act.wait_ge(gate_pe, 1)
                act.activation(tokv(TOK_EGC), psum[MISC][:, 0:64], ACT.Exp).then_inc(gate_act, 1)
                with act.Fori(0, 2) as hg:
                    with act.Fori(0, 2) as cp:
                        for cc in range(2):
                            delta_unit_act(hg, cp, cc)
                for c in range(DNH):
                    if c == 0:
                        act.wait_ge(dn["state"][0], 10)
                        act.wait_ge(dn["state"][1], 10)
                    if c >= 4:
                        act.wait_ge(hsum_done, 16 + c - 3)
                    act.activation(sqh[:, c % 4, :], h[:, c, :], ACT.Square).then_inc(hs_done, 1)
                    if c >= 1:
                        roots(c - 1, 16, DNH, 1.0 / 128, 6)
                roots(DNH - 1, 16, DNH, 1.0 / 128, 6)
                act_steps[0] = mine.n

            act_steps = [1]

            def roots(c, base, count, scale, bank, t0=0):
                act.wait_ge(hsum_done, base + c + 1)
                if c >= 8:
                    act.wait_ge(hnorm_done, base + c - 7)
                act.activation(dstd[:, c % 8, t0:T], psum[bank + c % 2][:, t0:T], ACT.Sqrt, scale=scale, bias=eps)\
                    .then_inc(hstd_done, 1)

            def delta_unit_act(hg, cp, cc):
                U = hg * 4 + cp * 2 + cc
                for s in range(2):
                    q, b = quad[s], dbank[s]
                    act.wait_ge(dn["gr"][s], U + 1)
                    act.activation(q["EG"], b[0], ACT.Exp).then_inc(dn["eg"][s], 1)
                for s in range(2):
                    q, b = quad[s], dbank[s]
                    act.wait_ge(dn["d"][s], U + 1)
                    act.activation(q["DT"], q["TG"], ACT.Exp).then_inc(dn["dt"][s], 1)
                for s in range(2):
                    q, b = quad[s], dbank[s]
                    act.wait_ge(dn["xtr"][s], U + 1)
                    act.activation(q["X"], b[0], ACT.Copy).then_inc(dn["x0"][s], 1)
                for n in range(1, LEVELS):
                    for s in range(2):
                        q, b = quad[s], dbank[s]
                        act.wait_ge(dn["y"][s], U * (LEVELS - 1) + n)
                        act.activation(q["Y"], b[0], ACT.Copy).then_inc(dn["yc"][s], 1)
                for s in range(2):
                    q, b = quad[s], dbank[s]
                    act.wait_ge(dn["wt"][s], U + 1)
                    act.activation(q["Y"], b[0], ACT.Copy, scale=-1.0).then_inc(dn["nw"][s], 1)
                for s in range(2):
                    q, b = quad[s], dbank[s]
                    act.wait_ge(dn["vmm"][s], U + 1)
                    act.activation(q["X"], b[1], ACT.Copy).then_inc(dn["vn"][s], 1)

            for l in range(DEPTH):
                for sub in range(3):
                    k = 3 * l + sub
                    t0 = CTX if k == 5 else 0
                    norm(k, t0)
                    if sub != 1:
                        ffn(2 * l + sub // 2, k, t0)
                    if k == 1:
                        delta(k)
                    if k == 4:
                        window(k)

            tables()
            for l in range(DEPTH):
                block2(l)

        @block.vector
        def _(dve):
            step = Steps(dve, dve_step)
            turn = Steps(dve, dve_turn)
            for _ in range(CREDIT):
                dve.sem_inc(x_done, 1)
                dve.sem_inc(hid_done, 1)
            dve.sem_inc(h2_done, 4)
            dve.wait_ge(act_step, 1)
            step(dve.scalar_tensor_tensor(ctmp[:, :, :], ctmp[:, :, :], 1.0, p_("cond").rearrange("p (c s) -> p c s", s=2),
                                          ALU.add, ALU.mult))
            dve.tensor_scalar(cond[:, :, :], ctmp[:, :, :], 0.5, None, ALU.mult).then_inc(cond_done, 1)
            dve.wait_ge(slots_used, used("ada", 71))
            step(dve.tensor_tensor(mod[:, :, :, :].rearrange("p a b c -> p (a b c)"), psum[MISC][:, 0:288], p_("ada_b"), ALU.add))
            dve.tensor_scalar(hgate[:, :, :], mod[:, :, 2, :], 0.5, None, ALU.mult)
            dve.scalar_tensor_tensor(amp[:, :, :], mod[:, :, 1, :], 1.0, p_("norm_g").rearrange("p (k c) -> p k c", k=6),
                                     ALU.add, ALU.mult).then_inc(mod_done, 1)
            dve.wait_ge(mod_done, 1)

            def norm(k, t0):
                dve.wait_ge(std_done, k + 1)
                step(dve.reciprocal(rstd[:, t0:T], std[:, t0:T]))
                for c in range(DC):
                    dve.tensor_tensor(h[:, c, t0:T], x[:, c, t0:T], rstd[:, t0:T], ALU.mult).then_inc(xn_done, 1)
                for c in range(DC):
                    dve.wait_ge(xn_done, DC * k + c + 1)
                    dve.tensor_scalar(h[:, c, CTX:T], h[:, c, CTX:T], amp[:, k, 2 * c + 1:2 * c + 2],
                                      mod[:, k, 0, 2 * c + 1:2 * c + 2], ALU.mult, ALU.add).then_inc(h1_done, 1)

            def add_out(name, k, per_chunk, gate, t0):
                for c in range(DC):
                    slot = 2 * c + 1 if per_chunk == 2 else c // 2
                    dve.wait_ge(slots_used, used(name, slot))
                    for s in range(0 if t0 == 0 else 1, 2):
                        xs = x[:, c, s * CTX:(s + 1) * CTX]
                        ins = dve.scalar_tensor_tensor(xs, psum[OUT_BANK + c % 2][:, s * CTX:(s + 1) * CTX],
                                                       gate[:, 2 * c + s:2 * c + s + 1], xs, ALU.mult, ALU.add)
                    ins.then_inc(x_done, 1)

            def ffn(f, k, t0):
                l, half = divmod(f, 2)

                def slot(n, i, u):
                    dve.wait_ge(tanh_done, n + (FHC * f + 1))
                    turn.last(dve.scalar_tensor_tensor(swu2[:, u % 2, t0:T], tanh2[:, u % 2, t0:T], 1.0, psum[u % 2][:, t0:T],
                                                  ALU.add, ALU.mult))
                    dve.scalar_tensor_tensor(hid[:, bass.ds(n, 1), t0:T].rearrange("p a t -> p (a t)"), swu2[:, u % 2, t0:T], 0.5,
                                             psum[2 + u % 2][:, t0:T], ALU.mult, ALU.mult).then_inc(hid_done, 1)
                over_slots(dve, FHC, slot)
                add_out(f"w2_{l}{half}", k, 2, hgate[:, k, :], t0)

            def window(k):
                dve.sem_inc(at["od"], CREDIT)
                dve.wait_ge(late_in, 32)
                for c in range(10):
                    t0 = CTX if c < 8 else 0
                    gain = p_("q_gain") if c < 8 else p_("k_gain")
                    dve.wait_ge(hstd_done, 24 + c + 1)
                    step(dve.reciprocal(grec[:, c % 4, t0:T], dstd[:, c % 8, t0:T]))
                    dve.scalar_tensor_tensor(sqk[:, c, t0:T], sqk[:, c, t0:T], gain, grec[:, c % 4, t0:T],
                                             ALU.mult, ALU.mult).then_inc(hnorm_done, 1)
                    if c >= 1:
                        rope(c - 1)
                rope(9)
                for kvp in range(2):
                    with dve.Fori(0, 2) as i:
                        sink_now[0] = (kvp, i)
                        attend_dve(8, lambda U: U + i * 8 + kvp * 16, window_logits, window_norm,
                                   lambda u: window_take(kvp, i, u))
                add_out("swa_out", k, 1, mod[:, k, 2, :], CTX)

            def rope(c):
                xs = sqk[:, c, CTX:T]
                tmp = conv2[:, c % 2, 0:SEQ]
                dve.wait_ge(rot_done, c + 1)
                step(dve.tensor_tensor(tmp, psum[6 + c % 2][:, 0:SEQ], late("s_sin"), ALU.mult))
                step(dve.tensor_tensor(xs, xs, late("s_cos"), ALU.mult))
                dve.tensor_tensor(xs, xs, tmp, ALU.add).then_inc(rope_done, 1)

            def attend_dve(units, at_unit, logits, norm, take):
                for t in range(units + 2):
                    if t < units:
                        dve.wait_ge(at["s"], at_unit(t + 1))
                        logits(t)
                    if 1 <= t <= units:
                        dve.wait_ge(at["e"], at_unit(t))
                        norm(t - 1)
                    if t >= 2:
                        dve.wait_ge(at["o"], at_unit(t - 1))
                        take(t - 2)

            def window_logits(u):
                j, r = u // 2 % 2, u % 2
                turn(dve.scalar_tensor_tensor(logit[:, u % 2, :], psum[u % 2][:, :], SD ** -0.5, late("s_mask", j * T, T),
                                              ALU.mult, ALU.add))
                turn(dve.reduce_max(small[:, 0, u:u + 1], logit[:, u % 2, :], AX.X))
                dve.tensor_scalar(small[:, 1, u:u + 1], small[:, 0, u:u + 1], sink_of(u), -1.0, ALU.max, ALU.mult)\
                    .then_inc(at["m"], 1)

            sink_now = [None]

            def sink_of(u):
                kvp, i = sink_now[0]
                return par[:, bass.ds(i * 2 + (POFF["sink"] + 4 * (2 * kvp + u % 2) + u // 4), 1)]

            def window_norm(u):
                turn(dve.tensor_tensor(small[:, 4, u:u + 1], small[:, 2, u:u + 1], small[:, 3, u:u + 1], ALU.add))
                (turn.last if u == 7 else turn)(dve.reciprocal(small[:, 5, u:u + 1], small[:, 4, u:u + 1]))
                dve.tensor_scalar(expo[:, u % 2, :], expo[:, u % 2, :], small[:, 5, u:u + 1], None, ALU.mult).then_inc(at["p"], 1)

            def window_take(kvp, i, u):
                b, j, r = u // 4, u // 2 % 2, u % 2
                dst = h[64 * r:64 * r + 64, bass.ds(i * 2 + (kvp * 4 + b), 1), CTX + j * P:CTX + (j + 1) * P]
                dve.tensor_copy(dst.rearrange("p a t -> p (a t)"), psum[4 + u % 2][64 * r:64 * r + 64, 0:P]).then_inc(at["od"], 1)

            def tables():
                lam = p_("lam")
                dve.wait_ge(late_in, 32)
                dve.scalar_tensor_tensor(late("sp", 0, 16), lam, -1.0, lam, ALU.mult, ALU.min).then_inc(tab_dve, 1)
                for nm in ("gx_b", "ga_b"):
                    step(dve.tensor_scalar(p_(nm), p_(nm), 0.5, None, ALU.mult))
                dve.wait_ge(tab_act, 1)
                dve.tensor_scalar(late("sp", 16, 16), late("sp", 0, 16), 1.0, None, ALU.add).then_inc(tab_dve, 1)
                dve.wait_ge(tab_dve, 2)
                step(dve.tensor_scalar(late("sp", 48, 16), late("sp", 16, 16), -1.0, None, ALU.add))
                step(dve.tensor_scalar(late("sp", 64, 16), late("sp", 48, 16), 0.0, None, ALU.is_equal))
                step(dve.tensor_tensor(late("sp", 48, 16), late("sp", 48, 16), late("sp", 64, 16), ALU.add))
                dve.wait_ge(tab_act, 2)
                step(dve.tensor_tensor(late("sp", 32, 16), late("sp", 32, 16), late("sp", 64, 16), ALU.add))
                step(dve.reciprocal(late("sp", 80, 16), late("sp", 48, 16)))
                step(dve.tensor_tensor(late("sp", 32, 16), late("sp", 32, 16), late("sp", 80, 16), ALU.mult))
                step(dve.tensor_tensor(late("sp", 32, 16), late("sp", 32, 16), late("sp", 0, 16), ALU.mult))
                step(dve.tensor_scalar(late("sp", 0, 16), lam, -1.0, 0.0, ALU.mult, ALU.max))
                step(dve.tensor_tensor(late("sp", 0, 16), late("sp", 0, 16), late("sp", 32, 16), ALU.add))
                step(dve.tensor_scalar(late("nspl"), late("sp", 0, 16), -4.0, None, ALU.mult))
                t0, t1, cos = late("t0"), late("t1"), late("m_cos")
                pos = late("pos").bitcast(I32)
                step(dve.tensor_copy(t1, pos))
                step(dve.tensor_scalar(t1, t1, late("m_freq"), None, ALU.mult))
                for n, quarter in enumerate((0.0, 0.25)):
                    if n:
                        dve.wait_ge(tab_act, 3)
                    k = cos
                    step(dve.tensor_scalar(k, t1, 1.0 / (2 * np.pi), quarter, ALU.mult, ALU.add))
                    step(dve.tensor_scalar(k, k, ROUND, None, ALU.add))
                    step(dve.tensor_scalar(k, k, -ROUND, None, ALU.add))
                    step(dve.scalar_tensor_tensor(t0, k, -TWO_PI[0], t1, ALU.mult, ALU.add))
                    step(dve.scalar_tensor_tensor(t0, k, -TWO_PI[1], t0, ALU.mult, ALU.add))
                    step(dve.scalar_tensor_tensor(t0, k, -TWO_PI[2], t0, ALU.mult, ALU.add))
                    step(dve.tensor_scalar(t0, t0, 2 * np.pi * quarter, None, ALU.add))
                    dve.tensor_scalar(t0, t0, -PI_IN, PI_IN, ALU.max, ALU.min).then_inc(tab_dve, 1)
                dve.wait_ge(tab_act, 4)
                dve.tensor_scalar(late("m_sin"), late("m_sin"), late("m_sign"), None, ALU.mult).then_inc(tab_dve, 1)
                dve.wait_ge(tab_dve, 5)

            def block2(l):
                cw = lambda c, tap: p_("conv_w", (RC * l + c) * CW + tap, 1)
                for c in range(RC):
                    if c % 2 == 0:
                        dve.wait_ge(slots_used, used(f"mla_r{l}", c // 2))
                    src, dst = psum[c % 4], xc[:, c, :]
                    step(dve.tensor_scalar(dst, src[:, 0:SEQ], cw(c, 3), p_("conv_b", RC * l + c, 1), ALU.mult, ALU.add))
                    for tap in (0, 1, 2):
                        o = 3 - tap
                        ins = dve.scalar_tensor_tensor(dst[:, o:SEQ], src[:, 0:SEQ - o], cw(c, tap), dst[:, o:SEQ],
                                                       ALU.mult, ALU.add)
                        if tap < 2:
                            step(ins)
                        else:
                            ins.then_inc(xc_done, 1)
                dve.wait_ge(ml_std, l + 1)
                step(dve.reciprocal(lat_r, lat_std))
                for c in range(QL + KVL):
                    g = p_("qn_g", QL * l + c, 1) if c < QL else p_("kvn_g", KVL * l + c - QL, 1)
                    r = lat_r[:, 0:SEQ] if c < QL else lat_r[:, SEQ:T]
                    ins = dve.scalar_tensor_tensor(lat[:, c, :], lat[:, c, :], g, r, ALU.mult, ALU.mult)
                ins.then_inc(ml_n, 1)
                for c in range(RC):
                    dve.wait_ge(rt_done, RC * l + c + 1)
                    n = late("nspl", RC * l + c, 1)
                    seg = ra[:, c * SEQ:(c + 1) * SEQ]
                    ins = dve.tensor_scalar(seg, seg, n, n, ALU.mult, ALU.add)
                ins.then_inc(rl_dve, 1)
                step(dve.scalar_tensor_tensor(rx, rx, 1.0, big[:, 0:2048], ALU.add, ALU.mult))
                dve.wait_ge(rl_act, 4 * l + 1)
                dve.scalar_tensor_tensor(re2, re2, 1.0, rth, ALU.add, ALU.mult).then_inc(rl_dve, 1)
                dve.wait_ge(rl_act, 4 * l + 2)
                step(dve.scalar_tensor_tensor(rx, rx, 0.5, re2, ALU.mult, ALU.mult))
                for c in range(RC):
                    sl = slice(c * SEQ, (c + 1) * SEQ)
                    step(dve.tensor_tensor_scan(ra[:, sl], rdec[:, sl], rx[:, sl], 0.0, ALU.mult, ALU.add))
                dve.wait_ge(rl_act, 4 * l + 3)
                step(dve.tensor_scalar(rth, rth, 0.044715, 1.0, ALU.mult, ALU.add))
                dve.tensor_tensor(rth, rth, gelu_in, ALU.mult).then_inc(rl_dve, 1)
                step(dve.scalar_tensor_tensor(gate_a, gate_a, 1.0, ra, ALU.add, ALU.mult))
                step(dve.tensor_tensor(gate_a, gate_a, gelu_in, ALU.mult))
                dve.wait_ge(rl_act, 4 * l + 4)
                dve.scalar_tensor_tensor(gate_a, rth, 1.0, gate_a, ALU.add, ALU.mult).then_inc(rl_dve, 1)
                dve.wait_ge(rl_dve, 4 * (l + 1))
                for m in range(9):
                    dve.wait_ge(rot_done, 10 + 9 * l + m + 1)
                    if m == 0:
                        v, tmp, sw = kpe[64:96, :], mtmp[64:96, 0:SEQ], psum[4][64:96, 0:SEQ]
                        cs, sn = late("m_cos")[64:96, :], late("m_sin")[64:96, :]
                    else:
                        v, tmp = mq[64:96, 2 * m - 2:2 * m, :], by8(mtmp[64:96, 512:1024])
                        sw = psum[4 + m % 2][64:96, :].rearrange("p (c t) -> p c t", t=SEQ)
                        cs, sn = (late(nm)[64:96, :].unsqueeze(1).broadcast_to([32, 2, SEQ]) for nm in ("m_cos", "m_sin"))
                    step(dve.tensor_tensor(tmp, sw, sn, ALU.mult))
                    step(dve.tensor_tensor(v, v, cs, ALU.mult))
                    dve.tensor_tensor(v, v, tmp, ALU.add).then_inc(rope_done, 1)
                    dve.wait_ge(rope_done, 10 + 9 * l + m + 1)
                with dve.Fori(0, 4) as i:
                    attend_dve(4, lambda U: U + i * 4 + (32 + 16 * l), mla_logits, mla_norm, lambda u: mla_take(i, u, l))
                dve.wait_ge(at["od"], CREDIT + 32 + 16 * (l + 1))
                step(dve.tensor_scalar(gate_a, gate_a, 0.25, None, ALU.mult))
                dve.scalar_tensor_tensor(hhigh, hhigh, 0.5, by8(gate_a), ALU.mult, ALU.add).then_inc(merged, 1)
                add_scaled(f"mla_out{l}", 1, 6 + 2 * l)
                layer_norm(2 * l, "ln1", l)

                def conv(dst, src, c):
                    w = lambda tap: par[:, bass.ds(c * FCW + (POFF["fc_w"] + tap), 1)]
                    turn(dve.tensor_scalar(dst, src, w(2), par[:, bass.ds(c + POFF["fc_b"], 1)], ALU.mult, ALU.add))
                    turn(dve.scalar_tensor_tensor(dst[:, 1:SEQ], src[:, 0:SEQ - 1], w(1), dst[:, 1:SEQ], ALU.mult, ALU.add))
                    return dve.scalar_tensor_tensor(dst[:, 2:SEQ], src[:, 0:SEQ - 2], w(0), dst[:, 2:SEQ], ALU.mult, ALU.add)

                def gel(n, i, u):
                    b = u % 2
                    bank = psum[u % 4]
                    dve.wait_ge(slots_used, n + used(f"up{l}", 0))
                    dve.wait_ge(h2_done, n + (FC2 * l + 3))
                    conv(conv_g[:, b, :], bank[:, 0:SEQ], n + 48 * l).then_inc(cg_done, 1)
                    turn(conv(conv_v[:, b, :], bank[:, SEQ:T], n + (48 * l + 24)))
                    dve.wait_ge(gs_done, n + (FC2 * l + 1))
                    turn(dve.tensor_scalar(gpoly[:, b, :], gsq[:, b, :], 0.044715, 1.0, ALU.mult, ALU.add))
                    dve.tensor_tensor(gpoly[:, b, :], gpoly[:, b, :], conv_g[:, b, :], ALU.mult).then_inc(gp_done, 1)
                    dve.wait_ge(gt_done, n + (FC2 * l + 1))
                    turn.last(dve.scalar_tensor_tensor(conv_g[:, b, :], gtanh[:, b, :], 1.0, conv_g[:, b, :], ALU.add, ALU.mult))
                    dve.scalar_tensor_tensor(mhid[:, bass.ds(n, 1), :].rearrange("p a t -> p (a t)"), conv_g[:, b, :], 0.5,
                                             conv_v[:, b, :], ALU.mult, ALU.mult).then_inc(h2_done, 1)
                over_slots(dve, FC2, gel)
                add_scaled(f"down{l}", 2, 7 + 2 * l)
                layer_norm(2 * l + 1, "ln2", l)

            def mla_logits(u):
                turn(dve.scalar_tensor_tensor(logit[:, u % 2, 0:384], psum[u % 2][:, 0:384], (NOPE + ROPE) ** -0.5, late("m_mask"),
                                              ALU.mult, ALU.add))
                dve.reduce_max(small[:, 0, u:u + 1], logit[:, u % 2, 0:P], AX.X)
                turn(dve.reduce_max(small[:, 1, u:u + 1], logit[:, u % 2, P:3 * P], AX.X))
                dve.tensor_scalar(small[:, 2:4, u:u + 1], small[:, 0:2, u:u + 1], -1.0, None, ALU.mult).then_inc(at["m"], 1)

            def mla_norm(u):
                (turn.last if u == 3 else turn)(dve.reciprocal(small[:, 6:8, u:u + 1], small[:, 4:6, u:u + 1]))
                dve.tensor_scalar(expo[:, u % 2, 0:P], expo[:, u % 2, 0:P], small[:, 6, u:u + 1], None, ALU.mult)
                dve.tensor_scalar(expo[:, u % 2, P:3 * P], expo[:, u % 2, P:3 * P], small[:, 7, u:u + 1], None, ALU.mult)\
                    .then_inc(at["p"], 1)

            def mla_take(i, u, l):
                r = u % 2
                dst = h[64 * r:64 * r + 64, bass.ds(i * 2 + u // 2, 1), CTX:T].rearrange("p a t -> p (a t)")
                g = gate_b[64 * r:64 * r + 64, bass.ds(i * (2 * SEQ) + (u // 2) * SEQ, SEQ)]
                dve.scalar_tensor_tensor(dst, g, 1.0, psum[4 + u % 2][64 * r:64 * r + 64, 0:SEQ], ALU.add, ALU.mult)\
                    .then_inc(at["od"], 1)

            def add_scaled(name, per_chunk, k):
                for c in range(DC):
                    dve.wait_ge(slots_used, used(name, 2 * c + 1 if per_chunk == 2 else c // 2))
                    xs = x[:, c, CTX:T]
                    dve.scalar_tensor_tensor(xs, xs, ALPHA, psum[OUT_BANK + c % 2][:, CTX:T], ALU.mult, ALU.add).then_inc(x_done, 1)

            def layer_norm(m, name, l):
                dve.wait_ge(ln_mean, m + 1)
                step(dve.tensor_scalar(ln_mu, psum[STAT][:, 0:SEQ], 1.0 / D, None, ALU.mult))
                for c in range(DC):
                    dve.tensor_tensor(hhigh[:, c, :], x[:, c, CTX:T], ln_mu, ALU.subtract).then_inc(ln_cent, 1)
                dve.wait_ge(ln_root, m + 1)
                step(dve.reciprocal(ln_r, ln_std))
                for c in range(DC):
                    ins = dve.scalar_tensor_tensor(x[:, c, CTX:T], hhigh[:, c, :], p_(name + "_g", DC * l + c, 1), ln_r, ALU.mult, ALU.mult)
                step(ins)
                for c in range(DC):
                    ins = dve.tensor_scalar(x[:, c, CTX:T], x[:, c, CTX:T], p_(name + "_b", DC * l + c, 1), None, ALU.add)
                ins.then_inc(ln_done, 1)

            def delta(k):
                halves = lambda ap: ap.rearrange("p (s t) -> p s t", s=2)
                step(dve.tensor_scalar(p_("dn_conv"), p_("dn_conv"), 0.5, None, ALU.mult))
                for _ in range(4):
                    dve.sem_inc(pr_free, 1)

                def taps(n, i, u):
                    for q in range(2):
                        bank = (2 * u + q) % 4
                        src, dst = halves(psum[bank][:, :]), halves(conv2[:, q, :])
                        if q == 0:
                            dve.wait_ge(slots_used, n + used("dn_in", 0))
                        dve.wait_ge(pr_free, 2 * n + (q + 3))
                        w = lambda tap: par[:, bass.ds(n * (2 * CONV) + (POFF["dn_conv"] + q * CONV + tap), 1)]
                        turn(dve.tensor_scalar(dst, src, w(2), None, ALU.mult))
                        for tap, o in ((0, -2), (1, -1), (3, 1), (4, 2)):
                            a0, a1 = max(0, -o), CTX - max(0, o)
                            ins = dve.scalar_tensor_tensor(dst[:, :, a0:a1], src[:, :, a0 + o:a1 + o], w(tap),
                                                           dst[:, :, a0:a1], ALU.mult, ALU.add)
                            if tap < 4:
                                (turn.last if (q, tap) == (1, 3) else turn)(ins)
                            else:
                                ins.then_inc(conv_done, 1)
                        dve.wait_ge(conv_done, 2 * n + (q + 1))
                    for q in range(2):
                        dve.wait_ge(pr_tanh, 2 * n + (q + 1))
                        dve.scalar_tensor_tensor(big[:, bass.ds(n * (2 * T) + q * T, T)], ttmp[:, q, :], 1.0, conv2[:, q, :],
                                                 ALU.add, ALU.mult).then_inc(pr_free, 1)

                def gate(n, i, u):
                    for q in range(2):
                        c = 2 * n + q - 24
                        if q == 0:
                            dve.wait_ge(slots_used, used("dn_in", n))
                        dve.wait_ge(pr_free, 2 * n + q + 3)
                        dve.tensor_scalar(conv2[:, q, :], psum[(2 * u + q) % 4][:, :], 0.5, None, ALU.mult).then_inc(conv_done, 1)
                    for q in range(2):
                        c = 2 * n + q - 24
                        dve.wait_ge(pr_tanh, 2 * n + q + 1)
                        dve.scalar_tensor_tensor(zs[:, c, :], ttmp[:, q, :], 1.0, conv2[:, q, :], ALU.add, ALU.mult)\
                            .then_inc(pr_free, 1)
                over_slots(dve, 12, taps)
                for n in range(12, 16):
                    gate(n, n // 4, n % 4)

                dve.wait_ge(slots_used, used("dn_ab", 0))
                ab = psum[MISC][:, 0:128].rearrange("p (c d g h) -> p d g c h", c=4, d=2, g=2)
                by = lambda n: tokv(n).rearrange("p (d c h) -> p d c h", d=2, c=4)
                for d in range(2):
                    step(dve.tensor_copy(by(TOK_BETA)[:, d], ab[:, d, 1]))
                    step(dve.tensor_tensor(by(TOK_T1)[:, d], ab[:, d, 0], p_("dn_dt").rearrange("p (d c h) -> p d c h", d=2, c=4)[:, d], ALU.add))
                dve.scalar_tensor_tensor(tokv(TOK_T2), tokv(TOK_T1), -1.0, tokv(TOK_T1), ALU.mult, ALU.max).then_inc(gate_step, 1)
                heads_norm(0, 16)
                dve.wait_ge(gate_act, 1)
                step(dve.scalar_tensor_tensor(tokv(TOK_T3), tokv(TOK_T1), 0.0, tokv(TOK_T2), ALU.max, ALU.add))
                dve.scalar_tensor_tensor(tokv(TOK_G), tokv(TOK_T3), -1.0, p_("dn_a"), ALU.mult, ALU.mult).then_inc(gates_done, 1)
                dve.wait_ge(gate_act, 2)
                step(dve.tensor_scalar(tokv(TOK_BETA), tokv(TOK_BETA), 0.5, 0.5, ALU.mult, ALU.add))
                dve.wait_ge(gate_act, 3)
                dve.tensor_copy(tokv(TOK_GC), psum[MISC][:, 0:64])
                dve.tensor_tensor(tokv(TOK_BEG), tokv(TOK_BETA), tokv(TOK_EGC), ALU.mult).then_inc(gates_done, 1)
                with dve.Fori(0, 2) as hg:
                    for s in range(2):
                        dve.memset(quad[s]["S"], 0.0).then_inc(dn["state"][s], 1)
                    with dve.Fori(0, 2) as cp:
                        for cc in range(2):
                            delta_unit_dve(hg, cp, cc)
                heads_norm(16, DNH)
                add_out("dn_out", k, 1, mod[:, k, 2, :], 0)

            def heads_norm(base, count):
                for c in range(count):
                    dve.wait_ge(hstd_done, base + c + 1)
                    step(dve.reciprocal(grec[:, c % 4, :], dstd[:, c % 8, :]))
                    if base == 0:
                        dve.scalar_tensor_tensor(qkv[:, c, :], qkv[:, c, :], P ** -0.5 if c < DNH else 1.0, grec[:, c % 4, :],
                                                 ALU.mult, ALU.mult).then_inc(hnorm_done, 1)
                    else:
                        dve.scalar_tensor_tensor(h[:, c, :], h[:, c, :], p_("dn_gain"), grec[:, c % 4, :],
                                                 ALU.mult, ALU.mult).then_inc(hnorm_done, 1)
                        dve.wait_ge(hnorm_done, base + c + 1)
                        dve.tensor_tensor(h[:, c, :], h[:, c, :], zs[:, c, :], ALU.mult).then_inc(y_in_done, 1)

            def delta_unit_dve(hg, cp, cc):
                U = hg * 4 + cp * 2 + cc

                def percol(n, s, tc):
                    return tok[:, n, bass.ds(tc * DNH + hg * QUAD + 32 * s, QUAD)].unsqueeze(2).broadcast_to([P, QUAD, CK])
                tcs = [2 * cp + cc, 2 * cp + (1 - cc)]
                for s in range(2):
                    q, b = quad[s], dbank[s]
                    dve.wait_ge(dn["eg"][s], U + 1)
                    turn(dve.tensor_tensor(q["TG"], b[0], percol(TOK_GC, s, tcs[s]), ALU.subtract))
                    dve.tensor_scalar(q["TG"], q["TG"], 0.0, None, ALU.min).then_inc(dn["d"][s], 1)
                for s in range(2):
                    q, b = quad[s], dbank[s]
                    dve.wait_ge(dn["dtm"][s], U + 1)
                    dve.wait_ge(dn["kq"][s], U + 1)
                    turn(dve.tensor_tensor(q["LT"], b[2], q["DT"], ALU.mult))
                    dve.tensor_tensor(q["QD"], b[3], q["DT"], ALU.mult)
                    dve.tensor_tensor(q["LT"], b[1], q["LT"], ALU.mult).then_inc(dn["lt"][s], 1)
                for s in range(2):
                    q, b = quad[s], dbank[s]
                    edge = CK - 1 if s == 0 else 0
                    dve.wait_ge(dn["ttok"][s], U + 1)
                    dve.tensor_tensor(q["V"], b[3], percol(TOK_BETA, s, tcs[s]), ALU.mult)
                    dve.tensor_tensor(q["KD"], b[2], q["DT"][:, :, edge:edge + 1].broadcast_to([P, QUAD, CK]), ALU.mult)
                    dve.tensor_tensor(q["K"], b[2], percol(TOK_BEG, s, tcs[s]), ALU.mult).then_inc(dn["toks"][s], 1)
                for n in range(1, LEVELS):
                    for s in range(2):
                        q, b = quad[s], dbank[s]
                        dve.wait_ge(dn["z"][s], U * (LEVELS - 1) + n)
                        if n < LEVELS - 1:
                            dve.tensor_tensor(q["X"], q["X"], b[1], ALU.add)
                        dve.tensor_tensor(q["XT"], q["XT"], b[2], ALU.add).then_inc(dn["xu"][s], 1)
                for s in range(2):
                    q, b = quad[s], dbank[s]
                    edge = CK - 1 if s == 0 else 0
                    dve.wait_ge(dn["end"][s], U + 1)
                    dst = h[:, bass.ds(hg * QUAD, QUAD), bass.ds(tcs[s] * CK, CK)]
                    if cc == 0:
                        dve.tensor_copy(dst, b[2])
                    else:
                        dve.wait_ge(dn["state"][1 - s], U + hg + 1)
                        dve.tensor_tensor(dst, dst, b[2], ALU.add)
                    (turn.last if s == 1 else turn)(dve.tensor_tensor(q["S"], q["S"], q["EG"][:, :, edge:edge + 1].broadcast_to([P, QUAD, CK]), ALU.mult))
                    dve.tensor_tensor(q["S"], q["S"], b[3], ALU.add).then_inc(dn["state"][s], 1)
                    dve.wait_ge(dn["state"][s], U + hg + 2)

            for l in range(DEPTH):
                for sub in range(3):
                    k = 3 * l + sub
                    t0 = CTX if k == 5 else 0
                    norm(k, t0)
                    if sub != 1:
                        ffn(2 * l + sub // 2, k, t0)
                    if k == 1:
                        delta(k)
                    if k == 4:
                        window(k)

            tables()
            for l in range(DEPTH):
                block2(l)

        @block.gpsimd
        def _(pool):
            psteps = Steps(pool, pool_turn)

            def delta():
                pool.wait_ge(gates_done, 2)
                pool.wait_ge(hnorm_done, 16)
                with pool.Fori(0, 2) as hg:
                    with pool.Fori(0, 2) as cp:
                        for cc in range(2):
                            delta_unit_pool(hg, cp, cc)

            def delta_unit_pool(hg, cp, cc):
                U = hg * 4 + cp * 2 + cc

                def percol(n, s, tc):
                    return tok[:, n, bass.ds(tc * DNH + hg * QUAD + 32 * s, QUAD)].unsqueeze(2).broadcast_to([P, QUAD, CK])

                def over_heads(m):
                    return m.unsqueeze(1).broadcast_to([P, QUAD, CK])
                tcs = [2 * cp + cc, 2 * cp + (1 - cc)]
                for s in range(2):
                    q = quad[s]
                    pool.wait_ge(dn["state"][s], U + hg + 1)
                    pool.tensor_tensor(q["TG"], over_heads(incl(s)), percol(TOK_G, s, tcs[s]), ALU.mult)\
                        .then_inc(dn["staged"][s], 1)
                    pool.tensor_tensor(q["TB"], over_heads(ident), percol(TOK_BETA, s, tcs[s]), ALU.mult)\
                        .then_inc(dn["staged"][s], 1)
                    for nm, first in (("K", DNH), ("V", 2 * DNH)):
                        pool.tensor_copy(q[nm], qkv[:, bass.ds(hg * QUAD + first, QUAD), bass.ds(tcs[s] * CK, CK)])\
                            .then_inc(dn["staged"][s], 1)
                for s in range(2):
                    q = quad[s]
                    pool.wait_ge(dn["dt"][s], U + 1)
                    pool.tensor_tensor(q["DT"], q["DT"], over_heads(incl(s)), ALU.mult).then_inc(dn["dtm"][s], 1)
                for s in range(2):
                    q = quad[s]
                    pool.wait_ge(dn["lt"][s], U + 1)
                    (psteps.last if s == 1 else psteps)(pool.tensor_tensor(q["XT"], q["LT"], over_heads(level(s, 0)), ALU.mult))
                    pool.tensor_tensor(q["XT"], q["XT"], over_heads(ident), ALU.add).then_inc(dn["xt0"][s], 1)
                    pool.tensor_tensor(q["M1"], q["LT"], over_heads(level(s, 1)), ALU.mult).then_inc(dn["mt"][s], 1)
                for s in range(2):
                    q = quad[s]
                    pool.tensor_tensor(q["TB"], qkv[:, bass.ds(hg * QUAD, QUAD), bass.ds(tcs[s] * CK, CK)], q["EG"], ALU.mult)\
                        .then_inc(dn["qg"][s], 1)
                for n in range(2, LEVELS):
                    for s in range(2):
                        q = quad[s]
                        if n > 2:
                            pool.wait_ge(dn["y"][s], U * (LEVELS - 1) + n - 2)
                        pool.tensor_tensor(q[f"M{n % 2}"], q["LT"], over_heads(level(s, n)), ALU.mult).then_inc(dn["mt"][s], 1)

            def attend_pool(l):
                if l is None:
                    for kvp in range(2):
                        with pool.Fori(0, 2) as i:
                            for b in range(2):
                                pool.wait_ge(at["od"], i * 8 + (kvp * 16 + CREDIT))
                                pool.tensor_copy(stage_q[:, b, 0:SEQ], sqk[:, bass.ds(i * 2 + (kvp * 4 + b), 1), CTX:T]
                                                 .rearrange("p a t -> p (a t)")).then_inc(at["q"], 1)
                else:
                    with pool.Fori(0, 4) as i:
                        for b in range(2):
                            pool.wait_ge(at["o"], i * 4 + (32 + 16 * l))
                            pool.tensor_copy(stage_q[0:96, b, :], mq[0:96, bass.ds(i * 4 + 2 * b, 2), :].rearrange("p a t -> p (a t)"))
                            pool.tensor_copy(stage_v[:, b, :, :], vtok[:, :, bass.ds(i * 256 + b * 128, 128)]).then_inc(at["q"], 1)

            delta()
            pool.wait_ge(x_done, CREDIT + 2 * DC)
            pool.dma_start(zbuf[:, 0:NLATE], A["late"]).then_inc(late_in, 16)
            pool.dma_start(late("pos").bitcast(I32), A["positions"]).then_inc(late_in, 16)
            pool.wait_ge(rope_done, 10)
            attend_pool(None)
            for l in range(DEPTH):
                pool.wait_ge(rope_done, 10 + 9 * l + 1)
                pool.tensor_copy(mk[64:96, :, :], kpe[64:96, :].unsqueeze(1).broadcast_to([32, MH, SEQ])).then_inc(kb_done, 1)
                pool.wait_ge(kb_done, l + 1)
                pool.wait_ge(rope_done, 10 + 9 * (l + 1))
                pool.wait_ge(uq_done, 20 * (l + 1))
                attend_pool(l)


def tiles(w, cols, kc=None):
    k, n = w.shape
    return w.reshape(k // P, P, n // cols, cols).transpose(2, 1, 0, 3).reshape(n // cols, P, -1)


def columns(v):
    return np.moveaxis(v.reshape(v.shape[:-1] + (v.shape[-1] // P, P)), -1, 0).reshape(P, -1)


def layout(i):
    a = {}
    tokens = np.concatenate([i["ctx"][0], i["x"][0]], 0)
    a["x_t"] = tokens.T.reshape(DC, P, T).transpose(1, 0, 2)
    a["consts"] = constants()
    twice = lambda v: np.repeat(v, 2, axis=-1)
    rows = lambda v: np.broadcast_to(v.reshape(1, -1), (P, v.size))
    conv = lambda w: np.moveaxis(w.reshape(w.shape[:-1] + (-1, P)), -1, 0).swapaxes(-1, -2).reshape(P, -1)
    p = {
        "ada_b": twice(columns(i["ada_b"])), "norm_g": twice(columns(i["norm_g"])),
        "cond": np.stack([i["c_ctx"].reshape(DC, P).T, i["c"][0].reshape(DC, P).T], -1).reshape(P, -1),
    }
    dup = lambda v: np.broadcast_to(v[:, None, :], (2, 4, DNH))
    p["dn_conv"] = conv(i["dn_conv"][0])
    p["dn_a"], p["dn_dt"] = rows(dup(i["dn_a_log"][0])), rows(dup(i["dn_dt_bias"][0]))
    p["dn_gain"] = i["dn_o_gain"][0].reshape(P, 1)
    two = lambda v: np.tile(v[0], 2).reshape(P, 1)
    p["q_gain"], p["k_gain"] = two(i["swa_q_gain"]), two(i["swa_k_gain"])
    p["sink"] = rows(i["swa_sink"][0])
    p["conv_w"], p["fc_w"] = conv(i["conv_w_2"]), conv(i["ffn_conv_w_2"])
    for name, key in (("conv_b", "conv_b_2"), ("gx_b", "gx_b_2"), ("ga_b", "ga_b_2"), ("lam", "lru_lambda_2"),
                      ("qn_g", "q_norm_g_2"), ("kvn_g", "kv_norm_g_2"), ("ln1_g", "ln1_g_2"), ("ln1_b", "ln1_b_2"),
                      ("ln2_g", "ln2_g_2"), ("ln2_b", "ln2_b_2"), ("fc_b", "ffn_conv_b_2")):
        p[name] = columns(i[key])
    a["late"] = late_constants()
    a["positions"] = np.broadcast_to(i["positions_2"].reshape(1, SEQ), (P, SEQ)).astype(np.int32)
    a["params"] = np.concatenate([p.get(n, np.zeros((P, w), np.float32)) for n, w in PARAMS], 1)
    a["ada"] = np.concatenate([tiles(i["ada_w"][l], 256) for l in range(DEPTH)])
    for l in range(DEPTH):
        for s in range(2):
            w1 = i["ffn_w1"][l, s].reshape(DC, P, 2, FHC, P)
            a[f"w1_{l}{s}"] = w1.transpose(3, 1, 0, 2, 4).reshape(FHC, P, SLOT)
            w2 = i["ffn_w2"][l, s].reshape(2, FHC // 2, P, DC, P)
            a[f"w2_{l}{s}"] = w2.transpose(3, 0, 2, 1, 4).reshape(2 * DC, P, -1)
    a["dn_in"] = tiles(i["dn_w_in"][0][:, :4096], 256)
    a["dn_ab"] = tiles(i["dn_w_in"][0][:, 4096:], 32)
    outw = lambda w: w.reshape(DC, P, DC // 2, 2, P).transpose(2, 1, 3, 0, 4).reshape(DC // 2, P, -1)
    a["dn_out"] = outw(i["dn_w_out"][0])
    heads = [4 * (2 * (c // 4) + r) + c % 4 for c in range(8) for r in range(2)]
    w = i["swa_w_qkv"][0]
    wq = w[:, :1024].reshape(D, SH, SD)[:, heads].reshape(D, 1024)
    a["swa_qk"] = tiles(np.concatenate([wq, w[:, 1024:1280]], 1), 256)
    a["swa_v"] = tiles(w[:, 1280:], 256)
    a["swa_out"] = outw(i["swa_w_out"][0].reshape(SH, SD, D)[heads].reshape(D, D))
    pair = lambda w, n: w.reshape(DC, P, 2, n, P).transpose(3, 1, 0, 2, 4).reshape(n, P, SLOT)
    for l in range(DEPTH):
        w = i["w_in_2"][l]
        part = np.split(w, [1024, 2048, 2432, 2688, 2720, 3744], axis=1)
        rope = np.zeros((D, P), w.dtype)
        rope[:, 64:96] = part[4]
        a[f"mla_r{l}"] = tiles(part[0], 256)
        a[f"mla_in{l}"] = tiles(np.concatenate([part[1], part[2], part[3], part[5], part[6], rope], 1), 256)
        bd = np.zeros((P, 2, RC, P), w.dtype)
        for g, key in enumerate(("gx_w_2", "ga_w_2")):
            for c in range(RC):
                for r in range(2):
                    bd[64 * r:64 * r + 64, g, c, 64 * r:64 * r + 64] = i[key][l, 2 * c + r]
        a[f"rnn_gate{l}"] = bd.reshape(1, P, SLOT)
        a[f"mla_uq{l}"] = tiles(i["w_uq_2"][l], 384)
        ukv = i["w_ukv_2"][l].reshape(256, MH, 2, 64)
        a[f"mla_uk{l}"] = tiles(ukv[:, :, 0].reshape(256, 1024), 1024)
        a[f"mla_uv{l}"] = tiles(ukv[:, :, 1].reshape(256, 1024), 1024)
        a[f"mla_out{l}"] = outw(i["w_out_2"][l])
        a[f"up{l}"] = pair(i["w_up_2"][l], FC2)
        w = i["w_down_2"][l].reshape(2, FC2 // 2, P, DC, P)
        a[f"down{l}"] = w.transpose(3, 0, 2, 1, 4).reshape(2 * DC, P, -1)
    return {k: np.ascontiguousarray(v) for k, v in a.items()}


def kernel(**inputs):
    import concourse.bacc as bacc
    from concourse.bass_utils import run_bass_kernel_spmd

    arrays = layout({name: np.asarray(value) for name, value in inputs.items()})
    nc = bacc.Bacc("TRN2", target_bir_lowering=False, num_devices=1)
    A = {name: nc.dram_tensor(name, a.shape, mybir.dt.from_np(a.dtype), kind="ExternalInput").ap()
         for name, a in arrays.items()}
    out = nc.dram_tensor("out", (P, DC, SEQ), F32, kind="ExternalOutput").ap()
    build(nc, A, out)
    result = run_bass_kernel_spmd(nc, [arrays], core_ids=[0])
    return np.ascontiguousarray(result.results[0]["out"].transpose(2, 1, 0).reshape(1, SEQ, D))
```

```python
from contextlib import ExitStack

import numpy as np

import concourse.bass as bass
from concourse import mybir

F32 = mybir.dt.float32
F32R = mybir.dt.float32r
I32 = mybir.dt.int32
ALU = mybir.AluOpType
ACT = mybir.ActivationFunctionType
AX = mybir.AxisListType

P = 128
D = 1024
DC = D // P
CTX = 256
SEQ = 256
T = CTX + SEQ
DEPTH = 2
RING = 4
SLOT = 2048
BANK = 512
CREDIT = 2

FH = 2816
FHC = FH // P
NMOD = 9
DNH = 8
CONV = 5
CK = 128
LEVELS = 7
QUAD = 4
SH, SKV, SD = 16, 4, 64
WINDOW = 128
RC, FC2, CW, FCW = 8, 24, 4, 3
MH, NOPE, ROPE, VH = 16, 64, 32, 64
QL, KVL = 3, 2
ALPHA = float((2 * DEPTH) ** 0.25)
EPS = 1e-6
GELU_C = float(np.sqrt(2.0 / np.pi))

def _ffn(l, half):
    return [(f"{w}_{l}{half}{hf}", n, width) for hf in range(2) for w, n, width in (("w1", 11, 2048), ("w2", 8, 1408))]


STREAMS = [("ada", 12, 2048)]
for _l in range(DEPTH):
    STREAMS += _ffn(_l, 0)
    if _l == 0:
        STREAMS += [("dn_in", 16, 2048), ("dn_ab", 1, 256), ("dn_out", 4, 2048)]
    else:
        STREAMS += [("swa_qk", 5, 2048), ("swa_v", 1, 2048), ("swa_out", 4, 2048)]
    STREAMS += _ffn(_l, 1)
for _l in range(DEPTH):
    STREAMS += [(f"mla_r{_l}", 4, 2048), (f"mla_in{_l}", 15, 2048), (f"rnn_gate{_l}", 1, 2048), (f"mla_uq{_l}", 4, 1152),
                (f"mla_uk{_l}", 1, 2048), (f"mla_uv{_l}", 1, 2048),
                (f"mla_out{_l}", 4, 2048), (f"up{_l}", 24, 2048), (f"down{_l}", 16, 1536)]
WHOLE = ("ada", "rnn_gate", "mla_uq", "mla_uk", "mla_uv")
BASE, SPLIT = {}, {}
_n = _m = 0
for _name, _slots, _w in STREAMS:
    BASE[_name] = _n
    _n += _slots
    if not _name.startswith(WHOLE):
        SPLIT[_name] = _m
        _m += _slots
DEEP = ("w1_11", "w2_11", "mla_", "up", "down")
WIDTH = {n: w for n, _, w in STREAMS}
COUNT = {n: c for n, c, _ in STREAMS}
X_BEFORE = [0, 16, 24, 40, 56, 64]
X_FIRST = 80

UNITS = 12
MOD_IN = {(0, 0): 0, (0, 1): 1, (2, 0): 2, (2, 1): 3, (3, 0): 4}
FIRST_UNITS = UNITS // 2

PARAMS = [("ada_b", 288), ("norm_g", 96), ("dn_conv", 120), ("dn_a", 64), ("dn_dt", 64), ("dn_gain", 1),
          ("q_gain", 1), ("k_gain", 1), ("sink", 16), ("conv_w", 64), ("conv_b", 16), ("gx_b", 16), ("ga_b", 16),
          ("lam", 16), ("qn_g", 6), ("kvn_g", 4), ("ln1_g", 16), ("ln1_b", 16), ("ln2_g", 16), ("ln2_b", 16),
          ("fc_w", 288), ("fc_b", 96), ("cond", 16)]
POFF = {}
_n = 0
for _name, _w in PARAMS:
    POFF[_name] = _n
    _n += _w
NPARAM = _n
PW = dict(PARAMS)

CONSTS = [("eps", 1), ("ident", 128), ("ones", 128), ("level", 2 * LEVELS * 128), ("incl", 2 * 128)]
COFF = {}
_n = 0
for _name, _w in CONSTS:
    COFF[_name] = _n
    _n += _w
NCONST = _n


LATE = [("s_cos", 256), ("s_sin", 256), ("s_swap", 128), ("s_ones", 128), ("s_mask", 1024),
        ("m_swap", 128), ("m_mask", 384), ("m_freq", 1), ("m_sign", 1)]
TABLES = [("pos", 256), ("m_cos", 256), ("m_sin", 256), ("t0", 256), ("t1", 256), ("nspl", 16), ("sp", 96)]
LOFF = {}
_n = 0
for _name, _w in LATE + TABLES:
    LOFF[_name] = _n
    _n += _w
LW = dict(LATE + TABLES)
NLATE = LOFF["pos"]
TWO_PI = [6.28125, float(np.round((2 * np.pi - 6.28125) * 2 ** 21) / 2 ** 21)]
TWO_PI.append(float(2 * np.pi - TWO_PI[0] - TWO_PI[1]))
ROUND = 1.5 * 2.0 ** 23
PI_IN = 3.1415925


def late_constants():
    c = np.zeros((P, NLATE), np.float32)

    def put(name, v):
        c[:, LOFF[name]:LOFF[name] + LW[name]] = v
    j, i = np.meshgrid(np.arange(P), np.arange(P), indexing="ij")
    freq = np.float32(10000.0) ** (-np.arange(16, dtype=np.float32) / np.float32(16))
    t = np.arange(SEQ)
    ang = np.concatenate([(t // 64).astype(np.float32)[:, None] * freq, (t % 64).astype(np.float32)[:, None] * freq], 1)
    put("s_cos", np.tile(np.cos(ang).T, (4, 1)))
    put("s_sin", np.tile(np.concatenate([-np.sin(ang).T, np.sin(ang).T]), (2, 1)))
    put("s_swap", (j // 64 == i // 64) & ((j % 64 + 32) % 64 == i % 64))
    put("s_ones", j // 64 == i // 64)
    m = np.zeros((P, 2, T), np.float32)
    for blk in range(2):
        q = blk * P + np.arange(P)
        m[:, blk, CTX:] = np.where(np.abs(q[:, None] - t[None, :]) <= WINDOW, 0.0, -1e30)
    put("s_mask", m.reshape(P, -1))
    put("m_swap", (j >= 64) & (j < 96) & (i >= 64) & (i < 96) & ((j - 64 + 16) % 32 == i - 64))
    causal = np.where(j >= i, 0.0, -1e30)
    put("m_mask", np.concatenate([causal, np.zeros((P, P)), causal], 1))
    p = np.arange(P)
    inv = np.float32(10000.0) ** (-np.arange(0, 32, 2, dtype=np.float32) / np.float32(32))
    put("m_freq", inv[p % 16][:, None])
    put("m_sign", np.where(p % 32 < 16, -1.0, 1.0)[:, None])
    return c


def constants():
    c = np.zeros((P, NCONST), np.float32)
    j, i = np.meshgrid(np.arange(P), np.arange(P), indexing="ij")
    c[:, COFF["eps"]] = EPS
    c[:, COFF["ident"]:COFF["ident"] + 128] = j == i
    c[:, COFF["ones"]:COFF["ones"] + 128] = 1.0
    for s in range(2):
        a, b = (j, i) if s == 0 else (i, j)
        c[:, COFF["incl"] + 128 * s:COFF["incl"] + 128 * (s + 1)] = a <= b
        for n in range(LEVELS):
            m = 1 << n
            at = COFF["level"] + (s * LEVELS + n) * 128
            c[:, at:at + 128] = -1.0 * ((a // (2 * m) == b // (2 * m)) & ((a // m) % 2 == 0) & ((b // m) % 2 == 1))
    return c


def build(nc, A, out):
    es = ExitStack()
    with es:
        def sem(name):
            return es.enter_context(nc.semaphore(name))

        arena = [(nc.sbuf_base + 63) // 64 * 64]

        def at_byte(name, shape, where, dt=F32):
            return nc.alloc_sbuf_tensor_at(name, shape, dt, offset=where)

        def sb(name, shape, dt=F32):
            where = arena[0]
            place[name] = where
            arena[0] += (int(np.prod(shape[1:])) * 4 + 31) // 32 * 32
            return at_byte(name, shape, where, dt)

        place = {}
        x = sb("x", [P, DC, T])
        h = sb("h", [P, DC, T])
        ring = sb("ring", [P, RING, SLOT])
        big = sb("big", [P, 24 * T])
        core = sb("core", [P, 30 * 512])
        ring_lo = at_byte("ring_lo", [P, RING, SLOT], place["ring"], F32R)
        h_lo = at_byte("h_lo", [P, DC, T], place["h"], F32R)
        hid_r = at_byte("hid_r", [P, 24 * T], place["big"], F32R)
        h_hi = at_byte("h_hi", [P, DC, T], place["core"] + 4 * 7168, F32R)
        w_hi = at_byte("w_hi", [P, 2, SLOT], place["core"] + 4 * 11264, F32R)
        x_r = at_byte("x_r", [P, DC, T], place["x"], F32R)
        zbuf = sb("zbuf", [P, 8 * T])
        par = sb("par", [P, NPARAM])
        con = sb("con", [P, NCONST])
        mod = sb("mod", [P, 6, 3, 16])
        amp = sb("amp", [P, 6, 16])
        hgate = sb("hgate", [P, 6, 16])
        cond = sb("cond", [P, DC, 2])
        ctmp = sb("ctmp", [P, DC, 2])
        tok = sb("tok", [P, 8, 64])

        psum = [es.enter_context(nc.psum_tensor(f"bank{i}", [P, BANK], F32)) for i in range(8)]
        OUT_BANK, STAT, MISC = 4, 6, 7

        def p_(name, a=0, n=None):
            o = POFF[name] + a
            return par[:, o:o + (PW[name] - a if n is None else n)]

        def incl(s):
            return con[:, COFF["incl"] + 128 * s:COFF["incl"] + 128 * (s + 1)]

        def level(s, n):
            o = COFF["level"] + (s * LEVELS + n) * 128
            return con[:, o:o + 128]

        ident = con[:, COFF["ident"]:COFF["ident"] + 128]
        ones = con[:, COFF["ones"]:COFF["ones"] + 128]
        eps = con[:, COFF["eps"]:COFF["eps"] + 1]

        hid_hi = hid_r[:, 0:11 * T].rearrange("p (c t) -> p c t", t=T)
        hid_lo = hid_r[:, 11 * T:22 * T].rearrange("p (c t) -> p c t", t=T)
        hid2 = core[:, 3072:4096].rearrange("p (b t) -> p b t", b=2)
        std = core[:, 0:512]
        rstd = core[:, 512:1024]
        ada_acc = core[:, 4096:5120].rearrange("p (b s f) -> p b s f", b=2, s=2)
        ada_w = zbuf[:, 0:2 * SLOT].rearrange("p (b f) -> p b f", b=2)
        tanh2 = core[:, 1024:2048].rearrange("p (b t) -> p b t", b=2)
        swu2 = core[:, 2048:3072].rearrange("p (b t) -> p b t", b=2)

        def late(name, a=0, n=None):
            o = LOFF[name] + a
            return zbuf[:, o:o + (LW[name] - a if n is None else n)]

        sqk = big[:, 0:10 * T].rearrange("p (c t) -> p c t", t=T)
        svt = big[:, 10 * T:12 * T].rearrange("p (c f) -> p c f", f=256)
        stage_q = core[:, 13312:13312 + 2 * 512].rearrange("p (b t) -> p b t", b=2)
        stage_v = core[:, 14336:14336 + 2 * 256].rearrange("p (b c f) -> p b c f", b=2, c=2)
        logit = core[:, 0:1024].rearrange("p (b t) -> p b t", b=2)
        expo = core[:, 1024:2048].rearrange("p (b t) -> p b t", b=2)
        probt = core[:, 2048:3072].rearrange("p (b t) -> p b t", b=2)
        small = core[:, 14848:14848 + 8 * 8].rearrange("p (n u) -> p n u", n=8)
        by8 = lambda ap: ap.rearrange("p (c t) -> p c t", t=SEQ)
        xc = by8(big[:, 0:2048])
        gelu_in = big[:, 2048:4096]
        gate_a_b = big[:, 4096:8192]
        gate_a, gate_b = big[:, 4096:6144], big[:, 6144:8192]
        lat = by8(big[:, 8192:9472])
        vtok = big[:, 9472:11520].rearrange("p (c f) -> p c f", f=1024)
        kpe = big[:, 11520:11776]
        mhid_hi, mhid_lo = by8(hid_r[:, 0:FC2 * SEQ]), by8(hid_r[:, FC2 * SEQ:2 * FC2 * SEQ])
        mq = by8(core[:, 3072:3072 + 4096])
        mk = by8(core[:, 7168:7168 + 4096])
        mtmp = core[:, 11264:13312]
        lat_sq = by8(core[:, 0:1280])
        lat_std = core[:, 1280:1792]
        lat_r = core[:, 1792:2304]
        rx, ra = core[:, 3072:5120], core[:, 5120:7168]
        rdec, re2, rth = core[:, 7168:9216], core[:, 9216:11264], core[:, 11264:13312]
        hlow, hhigh = h[:, :, 0:SEQ], h[:, :, SEQ:T]
        ln_mu, ln_std, ln_r = core[:, 4096:4352], core[:, 0:256], core[:, 256:512]
        conv_g = core[:, 512:1024].rearrange("p (b t) -> p b t", b=2)
        conv_v = core[:, 1024:1536].rearrange("p (b t) -> p b t", b=2)
        gsq = core[:, 1536:2048].rearrange("p (b t) -> p b t", b=2)
        gpoly = core[:, 2048:2560].rearrange("p (b t) -> p b t", b=2)
        gtanh = core[:, 2560:3072].rearrange("p (b t) -> p b t", b=2)

        qkv = big[:, 0:24 * T].rearrange("p (c t) -> p c t", t=T)
        zs = zbuf[:, :].rearrange("p (c t) -> p c t", t=T)
        conv2 = core[:, 3072:4096].rearrange("p (b t) -> p b t", b=2)
        ttmp = core[:, 4096:5120].rearrange("p (b t) -> p b t", b=2)
        sqh = core[:, 5120:5120 + 4 * 512].rearrange("p (b t) -> p b t", b=4)
        dstd = core[:, 7168:7168 + 8 * 512].rearrange("p (b t) -> p b t", b=8)
        grec = core[:, 11264:11264 + 4 * 512].rearrange("p (b t) -> p b t", b=4)
        TOK_G, TOK_BETA, TOK_GC, TOK_EGC, TOK_BEG, TOK_T1, TOK_T2, TOK_T3 = range(8)

        def tokv(n):
            return tok[:, n, :]

        QN = ["K", "V", "TG", "TB", "DT", "EG", "QD", "LT", "M0", "M1", "X", "XT", "Y", "KD", "S"]
        quad = [{q: core[:, (s * len(QN) + n) * 512:(s * len(QN) + n + 1) * 512].rearrange("p (h t) -> p h t", h=QUAD)
                 for n, q in enumerate(QN)} for s in range(2)]
        SEEN, SEEING = [slice(0, 64), slice(64, 128)], [slice(64, 128), slice(0, 64)]

        def seen(s, n):
            return SEEN[s] if n == LEVELS - 1 else slice(0, CK)

        dbank = [[psum[4 * s + n][:, :].rearrange("p (h t) -> p h t", h=QUAD) for n in range(4)] for s in range(2)]

        landed = [sem(f"landed{i}") for i in range(RING)]
        hi_done = sem("hi_done")
        lo_done = sem("lo_done")
        hh_done = sem("hh_done")
        hl_done = sem("hl_done")
        slots_used = sem("slots_used")
        params_in = sem("params_in")
        consts_in = sem("consts_in")
        x_in = sem("x_in")
        cond_done = sem("cond_done")
        mod_done = sem("mod_done")
        ada_landed = [sem(f"ada_landed{b}") for b in range(2)]
        ada_used = sem("ada_used")
        ada_summed = sem("ada_summed")
        x_done = sem("x_done")
        sq_done = sem("sq_done")
        stat_done = sem("stat_done")
        std_done = sem("std_done")
        xn_done = sem("xn_done")
        h0_done = sem("h0_done")
        h1_done = sem("h1_done")
        tanh_done = sem("tanh_done")
        hid_done = sem("hid_done")
        stored = sem("stored")
        dve_step = sem("dve_step")
        dve_turn = sem("dve_turn")
        act_step = sem("act_step")
        pool_turn = sem("pool_turn")

        pr_free = sem("pr_free")
        pr_tanh = sem("pr_tanh")
        conv_done = sem("conv_done")
        hs_done = sem("hs_done")
        hsum_done = sem("hsum_done")
        hstd_done = sem("hstd_done")
        hnorm_done = sem("hnorm_done")
        gate_step = sem("gate_step")
        gate_pe = sem("gate_pe")
        gate_act = sem("gate_act")
        gates_done = sem("gates_done")
        y_in_done = sem("y_in_done")
        late_in = sem("late_in")
        sw_done = sem("sw_done")
        rot_done = sem("rot_done")
        rope_done = sem("rope_done")
        at = {nm: sem(f"at_{nm}") for nm in ("q", "s", "m", "e", "p", "t", "tc", "o", "od")}
        tab_dve = sem("tab_dve")
        tab_act = sem("tab_act")
        xc_done = sem("xc_done")
        pj_done = sem("pj_done")
        rg_done = sem("rg_done")
        rt_done = sem("rt_done")
        rl_dve = sem("rl_dve")
        rl_act = sem("rl_act")
        ml_sq = sem("ml_sq")
        ml_sum = sem("ml_sum")
        ml_std = sem("ml_std")
        ml_n = sem("ml_n")
        uq_done = sem("uq_done")
        uk_done = sem("uk_done")
        uv_done = sem("uv_done")
        kb_done = sem("kb_done")
        merged = sem("merged")
        ln_mean = sem("ln_mean")
        ln_cent = sem("ln_cent")
        ln_sq = sem("ln_sq")
        ln_var = sem("ln_var")
        ln_root = sem("ln_root")
        ln_done = sem("ln_done")
        cg_done = sem("cg_done")
        gs_done = sem("gs_done")
        gp_done = sem("gp_done")
        gt_done = sem("gt_done")
        h2_done = sem("h2_done")
        dn = {}
        for nm in ("staged", "gr", "kq", "eg", "d", "dt", "dtm", "lt", "qg", "xt0", "mt", "xtr", "ttok", "x0", "toks",
                   "y", "yc", "z", "xu", "wt", "nw", "vmm", "vn", "end", "state"):
            dn[nm] = [sem(f"dn_{nm}{s}") for s in range(2)]

        class Steps:

            def __init__(self, eng, s):
                self.eng, self.s, self.n = eng, s, 0

            def __call__(self, ins):
                self.n += 1
                ins.then_inc(self.s, 1)
                self.eng.wait_ge(self.s, self.n)

            def mark(self, ins):
                self.n += 1
                ins.then_inc(self.s, 1)
                return self.n

            def until(self, n):
                self.eng.wait_ge(self.s, n)

            def reset(self):
                self.until(self.n)
                self.eng.sem_clear(self.s)
                self.n = 0

            def last(self, ins):
                self(ins)
                self.eng.sem_clear(self.s)
                self.n = 0

        def over_slots(eng, slots, body, apart=0):
            full = (slots - apart) // RING
            if full > 1:
                with eng.Fori(0, full) as i:
                    for u in range(RING):
                        body(i * RING + u, i, u)
                rest = range(full * RING, slots)
            else:
                rest = range(slots)
            for n in rest:
                body(n, n // RING, n % RING)

        def landed_slot(eng, name, i, u):
            k = BASE[name] + u
            eng.wait_ge(landed[k % RING], 16 * (i + (k // RING + 1)))
            return k % RING

        H_SPLITS = ["k0", "k1", "dn_out", "k2", "k3", "k4", "swa_out", "k5"] \
            + [f"{n}{l}" for l in range(DEPTH) for n in ("mla_in", "mla_out", "up")]

        def h_split(name, c=DC - 1):
            return DC * H_SPLITS.index(name) + c + 1

        def ada_count(m, g):
            return g + (FIRST_UNITS + UNITS * m)

        def high_part(name, u, a, b):
            k = (SPLIT[name] + u) % (4 if name.startswith(DEEP) else 2)
            if k < 2:
                return w_hi[:, k, a:b]
            home = (h_hi, x_r)[k - 2]
            if b - a <= 128:
                return home[:, a // 256, a % 256:a % 256 + b - a]
            return home[:, a // 256:b // 256, 0:256]

        def pieces(name, u):
            w = WIDTH[name]
            whole = w // 256 * 256
            if (SPLIT[name] + u) % 4 < 2 or not name.startswith(DEEP) or whole == w:
                return [(0, w)]
            return [(0, whole), (whole, w)]

        def like(v, part):
            return v if len(part.shape) == 2 else v.rearrange("p (c f) -> p c f", f=256)

        def used(name, n):
            return BASE[name] + n + 1

        block = es.enter_context(nc.Block())

        @block.sync
        def _(sp):
            for name, slots, width in STREAMS:

                def load(n, i, u, name=name, width=width):
                    k = BASE[name] + u
                    if not (name == "ada" and isinstance(n, int) and n < RING):
                        sp.wait_ge(slots_used, n + (BASE[name] - RING + 1))
                    sp.dma_start(ring[:, k % RING, 0:width], A[name][n, :, :]).then_inc(landed[k % RING], 16)

                if name == "ada":
                    for n in range(RING):
                        load(n, 0, n)
                    sp.dma_start(x[:, :, :], A["x_t"]).then_inc(x_in, 16)
                    with sp.Fori(1, slots // RING) as i:
                        for u in range(RING):
                            load(i * RING + u, i, u)
                else:
                    over_slots(sp, slots, load)

            sp.wait_ge(ln_done, 4)
            sp.dma_start(out, x[:, :, CTX:T]).then_inc(stored, 16)
            sp.wait_ge(stored, 16)

        @block.tensor
        def _(pe):
            def weights(eng, name, i, u):
                if name not in SPLIT:
                    return ring[:, landed_slot(eng, name, i, u), :]
                k = SPLIT[name] + u
                eng.wait_ge(lo_done, i * RING + (k + 1))
                return (lambda a, b: high_part(name, u, a, b)), (lambda a, b: ring_lo[:, (BASE[name] + u) % RING, a:b])

            def product(out, a, b, start, stop):
                pe.matmul(out, a[0], b[0], start=start, stop=False)
                pe.matmul(out, a[0], b[1], start=False, stop=False)
                return pe.matmul(out, a[1], b[0], start=False, stop=stop)

            def cut(pair, f):
                return f(pair[0]), f(pair[1])

            hs = (h_hi, h_lo)

            def chunk_ready(name, first, c):
                if first and name is not None:
                    pe.wait_ge(hl_done, h_split(name, c))

            def column_sum(k, n_chunks, t0):
                for c in range(n_chunks):
                    pe.wait_ge(sq_done, DC * k + c + 1)
                    mm = pe.matmul(psum[STAT][:, t0:T], ones, h[:, c, t0:T], start=(c == 0), stop=(c == n_chunks - 1))
                mm.then_inc(stat_done, 1)

            def ada():
                pe.wait_ge(cond_done, 1)

                def slot(n, i, u):
                    if u % 2 == 1:
                        ada_sum(i * 2 + u // 2, u // 2, n).then_inc(slots_used, 1)
                        return
                    w = weights(pe, "ada", i, u)
                    for q in range(2):
                        for c in range(DC):
                            mm = pe.matmul(psum[MISC][:, bass.ds(n * 4 + 2 * q, 2)],
                                           w[:, c * 256 + q * 128:c * 256 + (q + 1) * 128], cond[:, c, :],
                                           start=(c == 0), stop=(c == DC - 1))
                    mm.then_inc(slots_used, 1)
                over_slots(pe, COUNT["ada"], slot)

            def ada_sum(count, b, n):
                pe.wait_ge(ada_used, count + (CREDIT + 1))
                for q in range(2):
                    for s in range(2):
                        mm = pe.matmul(psum[MISC][:, bass.ds(n * 4 + (2 * q + s), 1)] if not isinstance(n, int) else
                                       psum[MISC][:, 4 * n + 2 * q + s:4 * n + 2 * q + s + 1],
                                       ada_acc[:, b, s, q * 128:(q + 1) * 128], ones[:, 0:1], start=True, stop=True)
                return mm

            def ffn(f, k, t0):
                l, half = divmod(f, 2)
                for hf in range(2):
                    name = f"w1_{l}{half}{hf}"

                    def up(n, i, u, name=name, hf=hf):
                        w = weights(pe, name, i, u)
                        pe.wait_ge(hid_done, n + (FHC * f + 11 * hf + 1))
                        for q in range(2):
                            for c in range(DC):
                                chunk_ready(f"k{k}", hf == 0 and u == 0 and q == 0, c)
                                mm = product(psum[2 * q + u % 2][:, t0:T],
                                             cut(w, lambda v: v(c * 256 + q * 128, c * 256 + (q + 1) * 128)),
                                             cut(hs, lambda v: v[:, c, t0:T]), c == 0, c == DC - 1)
                        mm.then_inc(slots_used, 1)
                        if m is not None and not isinstance(n, int):
                            ada_sum(ada_count(m, n), u % 2, n).then_inc(ada_summed, 1)
                    m = MOD_IN.get((k, hf))
                    if m is not None:
                        pe.wait_ge(mod_done, m + 1)
                    over_slots(pe, 11, up)
                    project_out(f"w2_{l}{half}{hf}", X_BEFORE[k] + DC * hf, (hid_hi, hid_lo), 11, 0, t0, m=m,
                                ready=(hid_done, CREDIT + FHC * f + 11 * hf))

            def project_out(name, base, src, kc, parts, t0, s0=None, m=None, ready=None):
                s0 = t0 if s0 is None else s0
                s1 = s0 + T - t0

                def slot(n, i, u):
                    w = weights(pe, name, i, u)
                    for q in range(2 if parts == 1 else 1):
                        o = u // 2 if parts == 2 else u % 2 if parts == 0 else q
                        part = u % 2 if parts == 2 else 0
                        if part == 0:
                            pe.wait_ge(x_done, {0: n, 1: 2 * n, 2: 2 * i}[parts] + (base + (0 if parts == 0 else o) + 1))
                        for c in range(kc):
                            if isinstance(ready, str):
                                chunk_ready(ready, u == 0 and q == 0, c)
                            elif u == 0 or parts == 2 and u == 1:
                                pe.wait_ge(ready[0], part * kc + c + (ready[1] + 1))
                            mm = product(psum[OUT_BANK + o][:, t0:T],
                                         cut(w, lambda v: v((q * kc + c) * 128, (q * kc + c + 1) * 128)),
                                         cut(src, lambda v: v[:, part * kc + c, s0:s1]),
                                         part == 0 and c == 0, (parts != 2 or part == 1) and c == kc - 1)
                    mm.then_inc(slots_used, 1)
                    if m is not None and u % 2 == 0:
                        g = i * 2 + (8 + u // 2)
                        ada_sum(ada_count(m, g), u // 2, g).then_inc(ada_summed, 1)
                over_slots(pe, {0: DC, 1: DC // 2, 2: 2 * DC}[parts], slot)

            def delta_in(k):
                def slot(n, i, u):
                    w = weights(pe, "dn_in", i, u)
                    for q in range(2):
                        bank = (2 * u + q) % 4
                        pe.wait_ge(pr_free, 2 * n + (q + 1))
                        for c in range(DC):
                            chunk_ready("k1", u == 0 and q == 0, c)
                            mm = product(psum[bank][:, :], cut(w, lambda v: v(c * 256 + q * 128, c * 256 + (q + 1) * 128)),
                                         cut(hs, lambda v: v[:, c, :]), c == 0, c == DC - 1)
                    mm.then_inc(slots_used, 1)
                over_slots(pe, 16, slot)
                w = weights(pe, "dn_ab", 0, 0)
                for tc in range(4):
                    for c in range(DC):
                        mm = product(psum[MISC][:, tc * 32:(tc + 1) * 32], cut(hs, lambda v: v[:, c, tc * CK:(tc + 1) * CK]),
                                     cut(w, lambda v: v(c * 32, (c + 1) * 32)), c == 0, c == DC - 1)
                mm.then_inc(slots_used, 1)
                for c in range(16):
                    pe.wait_ge(hs_done, c + 1)
                    if c >= 2:
                        pe.wait_ge(hstd_done, c - 1)
                    pe.matmul(psum[4 + c % 2][:, :], ones, sqh[:, c % 4, :], start=True, stop=True).then_inc(hsum_done, 1)
                pe.wait_ge(gates_done, 1)
                for s in range(2):
                    mm = pe.matmul(psum[MISC][:, 32 * s:32 * (s + 1)], incl(s), tokv(TOK_G)[:, 32 * s:32 * (s + 1)],
                                   start=True, stop=True)
                mm.then_inc(gate_pe, 1)

            def delta_core():
                pe.wait_ge(gates_done, 2)
                pe.wait_ge(hnorm_done, 16)
                with pe.Fori(0, 2) as hg:
                    with pe.Fori(0, 2) as cp:
                        for cc in range(2):
                            delta_unit_pe(hg, cp, cc)

            def delta_unit_pe(hg, cp, cc):
                U = hg * 4 + cp * 2 + cc
                for s in range(2):
                    q, b = quad[s], dbank[s]
                    tc = 2 * cp + (cc if s == 0 else 1 - cc)
                    pe.wait_ge(dn["staged"][s], 4 * U + 4)
                    pe.wait_ge(dn["state"][s], U + hg + 1)
                    pe.matmul(psum[4 * s][:, :], ones, q["TG"].rearrange("p h t -> p (h t)"), start=True, stop=True)\
                        .then_inc(dn["gr"][s], 1)
                    pe.matmul(psum[4 * s + 1][:, :], ones, q["TB"].rearrange("p h t -> p (h t)"), start=True, stop=True)
                    for hd in range(QUAD):
                        pe.matmul(b[2][:, hd, :], q["K"][:, hd, :], q["K"][:, hd, :], start=True, stop=True)
                    for hd in range(QUAD):
                        mm = pe.matmul(b[3][:, hd, :], q["K"][:, hd, :],
                                       big[:, bass.ds(hg * (QUAD * T) + tc * CK + hd * T, CK)], start=True, stop=True)
                    mm.then_inc(dn["kq"][s], 1)
                for s in range(2):
                    q, b = quad[s], dbank[s]
                    pe.wait_ge(dn["xt0"][s], U + 1)
                    for hd in range(QUAD):
                        mm = pe.transpose(b[0][:, hd, :], q["XT"][:, hd, :], ident)
                    mm.then_inc(dn["xtr"][s], 1)
                    for hd in range(QUAD):
                        pe.transpose(b[2][:, hd, :], q["K"][:, hd, :], ident)
                    for hd in range(QUAD):
                        mm = pe.transpose(b[3][:, hd, :], q["V"][:, hd, :], ident)
                    mm.then_inc(dn["ttok"][s], 1)
                for n in range(1, LEVELS):
                    for s in range(2):
                        q, b = quad[s], dbank[s]
                        if n == 1:
                            pe.wait_ge(dn["x0"][s], U + 1)
                            pe.wait_ge(dn["toks"][s], U + 1)
                        else:
                            pe.wait_ge(dn["xu"][s], U * (LEVELS - 1) + n - 1)
                        pe.wait_ge(dn["mt"][s], U * (LEVELS - 1) + n)
                        for hd in range(QUAD):
                            mm = pe.matmul(b[0][:, hd, seen(s, n)], q[f"M{n % 2}"][:, hd, :], q["X"][:, hd, seen(s, n)],
                                           start=True, stop=True)
                        mm.then_inc(dn["y"][s], 1)
                    for s in range(2):
                        q, b = quad[s], dbank[s]
                        pe.wait_ge(dn["yc"][s], U * (LEVELS - 1) + n)
                        if n < LEVELS - 1:
                            for hd in range(QUAD):
                                pe.matmul(b[1][:, hd, :], q["XT"][:, hd, :], q["Y"][:, hd, :], start=True, stop=True)
                            for hd in range(QUAD):
                                mm = pe.matmul(b[2][:, hd, :], q["Y"][:, hd, :], q["XT"][:, hd, :], start=True, stop=True)
                        else:
                            for hd in range(QUAD):
                                mm = pe.matmul(b[2][SEEN[s], hd, SEEING[s]], q["Y"][:, hd, SEEN[s]], q["XT"][:, hd, SEEING[s]],
                                               start=True, stop=True)
                        mm.then_inc(dn["z"][s], 1)
                for s in range(2):
                    q, b = quad[s], dbank[s]
                    pe.wait_ge(dn["xu"][s], U * (LEVELS - 1) + LEVELS - 1)
                    for hd in range(QUAD):
                        mm = pe.matmul(b[0][:, hd, :], q["K"][:, hd, :], q["XT"][:, hd, :], start=True, stop=True)
                    mm.then_inc(dn["wt"][s], 1)
                for s in range(2):
                    q, b = quad[s], dbank[s]
                    pe.wait_ge(dn["nw"][s], U + 1)
                    for hd in range(QUAD):
                        pe.matmul(b[1][:, hd, :], q["XT"][:, hd, :], q["V"][:, hd, :], start=True, stop=False)
                        mm = pe.matmul(b[1][:, hd, :], q["Y"][:, hd, :], q["S"][:, hd, :], start=False, stop=True)
                    mm.then_inc(dn["vmm"][s], 1)
                for s in range(2):
                    q, b = quad[s], dbank[s]
                    pe.wait_ge(dn["vn"][s], U + 1)
                    pe.wait_ge(dn["qg"][s], U + 1)
                    for hd in range(QUAD):
                        pe.matmul(b[2][:, hd, :], q["S"][:, hd, :], q["TB"][:, hd, :], start=True, stop=False)
                        pe.matmul(b[2][:, hd, :], q["X"][:, hd, :], q["QD"][:, hd, :], start=False, stop=True)
                    for hd in range(QUAD):
                        mm = pe.matmul(b[3][:, hd, :], q["KD"][:, hd, :], q["X"][:, hd, :], start=True, stop=True)
                    mm.then_inc(dn["end"][s], 1)

            def delta_out(k):
                for c in range(DNH):
                    pe.wait_ge(hs_done, 16 + c + 1)
                    if c >= 2:
                        pe.wait_ge(hstd_done, 16 + c - 1)
                    pe.matmul(psum[6 + c % 2][:, :], ones, sqh[:, c % 4, :], start=True, stop=True).then_inc(hsum_done, 1)
                project_out("dn_out", X_BEFORE[1], hs, DC, 1, 0, ready="dn_out")

            def window(k):
                for n in range(5):
                    w = weights(pe, "swa_qk", n // RING, n % RING)
                    t0 = CTX if n < 4 else 0
                    for q in range(2):
                        m = 2 * n + q
                        if m >= 4:
                            pe.wait_ge(sw_done, m - 3)
                        for c in range(DC):
                            chunk_ready("k4", m == 0, c)
                            mm = product(psum[m % 4][:, t0:T], cut(w, lambda v: v(c * 256 + q * 128, c * 256 + (q + 1) * 128)),
                                         cut(hs, lambda v: v[:, c, t0:T]), c == 0, c == DC - 1)
                    mm.then_inc(slots_used, 1)
                w = weights(pe, "swa_v", 0, 0)
                for tc in range(4):
                    pe.wait_ge(sw_done, 7 + tc)
                    for c in range(DC):
                        mm = product(psum[(tc + 2) % 4][:, 0:256], cut(hs, lambda v: v[:, c, tc * P:(tc + 1) * P]),
                                     cut(w, lambda v: v(c * 256, (c + 1) * 256)), c == 0, c == DC - 1)
                mm.then_inc(slots_used, 1)
                for c in range(10):
                    t0 = CTX if c < 8 else 0
                    pe.wait_ge(hs_done, 24 + c + 1)
                    if c == 0:
                        pe.wait_ge(late_in, 32)
                    if c >= 2:
                        pe.wait_ge(hstd_done, 24 + c - 1)
                    pe.matmul(psum[4 + c % 2][:, t0:T], late("s_ones"), sqh[:, c % 4, t0:T], start=True, stop=True)\
                        .then_inc(hsum_done, 1)
                    if c >= 1:
                        rotate(c - 1)
                rotate(9)
                pe.wait_ge(rope_done, 10)
                for kvp in range(2):
                    with pe.Fori(0, 2) as i:
                        attend_pe(8, lambda U: U + i * 8 + kvp * 16, lambda u: scores(kvp, u),
                                  lambda u: values(kvp, u), 4, lambda u: 2 * (kvp * 2 + i) + u // 4 + 1)
                project_out("swa_out", X_BEFORE[4], hs, DC, 1, CTX, ready="swa_out")

            def rotate(c):
                pe.wait_ge(hnorm_done, 24 + c + 1)
                if c >= 2:
                    pe.wait_ge(rope_done, c - 1)
                pe.matmul(psum[6 + c % 2][:, 0:SEQ], late("s_swap"), sqk[:, c, CTX:T], start=True, stop=True).then_inc(rot_done, 1)

            def scores(kvp, u):
                b, j, r = u // 4, u // 2 % 2, u % 2
                pe.matmul(psum[u % 2][:, :], stage_q[64 * r:64 * r + 64, b, j * P:(j + 1) * P], sqk[64 * r:64 * r + 64, 8 + kvp, :],
                          start=True, stop=True).then_inc(at["s"], 1)

            def values(kvp, u):
                r = u % 2
                kv = 2 * kvp + r
                for c in range(4):
                    mm = pe.matmul(psum[4 + u % 2][64 * r:64 * r + 64, 0:P], svt[:, c, kv * SD:(kv + 1) * SD],
                                   probt[:, u % 2, c * P:(c + 1) * P], start=(c == 0), stop=(c == 3))
                mm.then_inc(at["o"], 1)

            def attend_pe(units, at_unit, score, value, blocks, staged):
                for t in range(units + 2):
                    if t < units:
                        pe.wait_ge(at["q"], staged(t))
                        score(t)
                    if 1 <= t <= units:
                        u = t - 1
                        pe.wait_ge(at["p"], at_unit(u + 1))
                        for c in range(blocks):
                            mm = pe.transpose(psum[2 + u % 2][:, c * P:(c + 1) * P], expo[:, u % 2, c * P:(c + 1) * P], ident)
                        mm.then_inc(at["t"], 1)
                    if t >= 2:
                        u = t - 2
                        pe.wait_ge(at["tc"], at_unit(u + 1))
                        pe.wait_ge(at["od"], at_unit(u + 1))
                        value(u)

            def block2(l):
                def rnn_in(n):
                    w = weights(pe, f"mla_r{l}", 0, n)
                    for q in range(2):
                        m = 2 * n + q
                        if m >= 4:
                            pe.wait_ge(xc_done, 8 * l + m - 3)
                        for c in range(DC):
                            chunk_ready(f"mla_in{l}", m == 0, c)
                            mm = product(psum[m % 4][:, 0:SEQ], cut(w, lambda v: v(c * 256 + q * 128, c * 256 + (q + 1) * 128)),
                                         cut(hs, lambda v: v[:, c, CTX:T]), c == 0, c == DC - 1)
                    mm.then_inc(slots_used, 1)
                for n in range(4):
                    rnn_in(n)

                def proj(n, i, u):
                    w = weights(pe, f"mla_in{l}", i, u)
                    for q in range(2):
                        pe.wait_ge(pj_done, 2 * n + (30 * l + q + 1))
                        for c in range(DC):
                            mm = product(psum[(2 * u + q) % 4][:, 0:SEQ],
                                         cut(w, lambda v: v(c * 256 + q * 128, c * 256 + (q + 1) * 128)),
                                         cut(hs, lambda v: v[:, c, CTX:T]), c == 0, c == DC - 1)
                    mm.then_inc(slots_used, 1)
                pe.wait_ge(xc_done, 8 * l + 8)
                over_slots(pe, 15, proj)
                pe.wait_ge(ml_sq, l + 1)
                for c in range(QL):
                    pe.matmul(psum[STAT][:, 0:SEQ], ones, lat_sq[:, c, :], start=(c == 0), stop=(c == QL - 1))
                for c in range(KVL):
                    mm = pe.matmul(psum[STAT][:, SEQ:T], ones, lat_sq[:, QL + c, :], start=(c == 0), stop=(c == KVL - 1))
                mm.then_inc(ml_sum, 1)
                w = weights(pe, f"rnn_gate{l}", 0, 0)
                pe.wait_ge(pj_done, 4 + 30 * (l + 1))
                for c in range(RC):
                    if c >= 4:
                        pe.wait_ge(rt_done, RC * l + c - 3)
                    pe.matmul(psum[c % 4][:, 0:SEQ], w[:, c * P:(c + 1) * P], xc[:, c, :], start=True, stop=True)
                    mm = pe.matmul(psum[c % 4][:, SEQ:T], w[:, (RC + c) * P:(RC + c + 1) * P], xc[:, c, :], start=True, stop=True)
                    mm.then_inc(rg_done, 1)
                pe.matmul(psum[MISC][:, 0:1], ones, eps, start=True, stop=True).then_inc(slots_used, 1)
                pe.wait_ge(ml_n, l + 1)
                pe.wait_ge(rl_dve, 4 * (l + 1))
                for n in range(4):
                    w = weights(pe, f"mla_uq{l}", 0, n)
                    for q in range(2):
                        m = 2 * n + q
                        if m >= 4:
                            pe.wait_ge(uq_done, 20 * l + m - 3)
                        for e in range(2):
                            hd = 2 * q + e
                            for c in range(QL):
                                mm = pe.matmul(psum[m % 4][0:96, e * SEQ:(e + 1) * SEQ], w[:, c * 384 + hd * 96:c * 384 + hd * 96 + 96],
                                               lat[:, c, :], start=(c == 0), stop=(c == QL - 1))
                    mm.then_inc(slots_used, 1)
                w = weights(pe, f"mla_uk{l}", 0, 0)
                for m in range(8):
                    pe.wait_ge(uq_done, 20 * l + 8 + m - 3)
                    for e in range(2):
                        hd = 2 * m + e
                        for c in range(KVL):
                            mm = pe.matmul(psum[m % 4][0:64, e * SEQ:(e + 1) * SEQ], w[:, c * 1024 + hd * 64:c * 1024 + hd * 64 + 64],
                                           lat[:, QL + c, :], start=(c == 0), stop=(c == KVL - 1))
                    mm.then_inc(uk_done, 1)
                pe.matmul(psum[MISC][:, 0:1], ones, eps, start=True, stop=True).then_inc(slots_used, 1)
                w = weights(pe, f"mla_uv{l}", 0, 0)
                for m in range(4):
                    tc, half = divmod(m, 2)
                    pe.wait_ge(uq_done, 20 * l + 16 + m - 3)
                    for c in range(KVL):
                        mm = pe.matmul(psum[m % 4][:, :], lat[:, QL + c, tc * P:(tc + 1) * P],
                                       w[:, c * 1024 + half * 512:c * 1024 + half * 512 + 512], start=(c == 0), stop=(c == KVL - 1))
                    mm.then_inc(uv_done, 1)
                pe.matmul(psum[MISC][:, 0:1], ones, eps, start=True, stop=True).then_inc(slots_used, 1)
                for m in range(9):
                    if m >= 2:
                        pe.wait_ge(rope_done, 10 + 9 * l + m - 1)
                    if m == 0:
                        pe.wait_ge(tab_dve, 5)
                        pe.matmul(psum[4][0:96, 0:SEQ], late("m_swap")[64:96, 0:96], kpe[64:96, :], start=True, stop=True)\
                            .then_inc(rot_done, 1)
                    else:
                        pe.wait_ge(uq_done, 20 * l + m)
                        pe.matmul(psum[4 + m % 2][0:96, :], late("m_swap")[0:96, 0:96],
                                  mq[0:96, 2 * m - 2:2 * m, :].rearrange("p c t -> p (c t)"), start=True, stop=True).then_inc(rot_done, 1)
                pe.wait_ge(kb_done, l + 1)
                pe.wait_ge(uq_done, 20 * (l + 1))
                with pe.Fori(0, 4) as i:
                    attend_pe(4, lambda U: U + i * 4 + (32 + 16 * l), lambda u: mla_scores(i, u), mla_values, 3,
                              lambda u: 2 * i + (8 + 8 * l) + u // 2 + 1)
                project_out(f"mla_out{l}", X_FIRST + 2 * DC * l, hs, DC, 1, CTX, ready=f"mla_out{l}")
                layer_norm(2 * l)

                def up(n, i, u):
                    w = weights(pe, f"up{l}", i, u)
                    pe.wait_ge(h2_done, n + (FC2 * l + 1))
                    for q in range(2):
                        for c in range(DC):
                            chunk_ready(f"up{l}", u == 0 and q == 0, c)
                            mm = product(psum[u % 4][:, q * SEQ:(q + 1) * SEQ],
                                         cut(w, lambda v: v(c * 256 + q * 128, c * 256 + (q + 1) * 128)),
                                         cut(hs, lambda v: v[:, c, CTX:T]), c == 0, c == DC - 1)
                    mm.then_inc(slots_used, 1)
                over_slots(pe, FC2, up)
                project_out(f"down{l}", X_FIRST + 2 * DC * l + DC, (mhid_hi, mhid_lo), 12, 2, CTX, 0,
                            ready=(h2_done, 4 + FC2 * l))
                layer_norm(2 * l + 1)

            def mla_scores(i, u):
                b, e = u // 2, u % 2
                keys = lambda n: mk[0:96, bass.ds(i * 4 + u, 1), 0:n].rearrange("p a t -> p (a t)")
                pe.matmul(psum[u % 2][:, 0:P], stage_q[0:96, b, e * SEQ:e * SEQ + P], keys(P), start=True, stop=True)
                pe.matmul(psum[u % 2][:, P:3 * P], stage_q[0:96, b, e * SEQ + P:e * SEQ + 2 * P], keys(SEQ), start=True, stop=True)\
                    .then_inc(at["s"], 1)

            def mla_values(u):
                b, r = u // 2, u % 2
                dst = psum[4 + u % 2][64 * r:64 * r + 64, :]
                v = lambda c: stage_v[:, b, c, r * VH:(r + 1) * VH]
                pe.matmul(dst[:, 0:P], v(0), probt[:, u % 2, 0:P], start=True, stop=True)
                pe.matmul(dst[:, P:2 * P], v(0), probt[:, u % 2, P:2 * P], start=True, stop=False)
                pe.matmul(dst[:, P:2 * P], v(1), probt[:, u % 2, 2 * P:3 * P], start=False, stop=True).then_inc(at["o"], 1)

            def layer_norm(m):
                for c in range(DC):
                    pe.wait_ge(x_done, CREDIT + X_FIRST + DC * m + c + 1)
                    mm = pe.matmul(psum[STAT][:, 0:SEQ], ones, x[:, c, CTX:T], start=(c == 0), stop=(c == DC - 1))
                mm.then_inc(ln_mean, 1)
                for c in range(DC):
                    pe.wait_ge(ln_sq, DC * m + c + 1)
                    mm = pe.matmul(psum[STAT][:, SEQ:T], ones, hlow[:, c, :], start=(c == 0), stop=(c == DC - 1))
                mm.then_inc(ln_var, 1)

            pe.wait_ge(consts_in, 16)
            for _ in range(CREDIT):
                pe.sem_inc(ada_summed, 1)
            ada()
            for l in range(DEPTH):
                for sub in range(3):
                    k = 3 * l + sub
                    t0 = CTX if k == 5 else 0
                    column_sum(k, DC, t0)
                    if sub != 1:
                        ffn(2 * l + sub // 2, k, t0)
                    if k == 4:
                        window(k)
                    if k == 1:
                        delta_in(k)
                        delta_core()
                        delta_out(k)

            for l in range(DEPTH):
                block2(l)

        @block.scalar
        def _(act):
            act.dma_start(par[:, :], A["params"]).then_inc(params_in, 16)
            act.dma_start(con[:, :], A["consts"]).then_inc(consts_in, 16)
            act.wait_ge(params_in, 16)
            act.activation(ctmp[:, :, :], p_("cond").rearrange("p (c s) -> p c s", s=2), ACT.Tanh, scale=0.5)\
                .then_inc(act_step, 1)

            def high(name, n, i, u):
                r = landed_slot(act, name, i, u)
                act.wait_ge(slots_used, n + (BASE[name] - (3 if name.startswith(DEEP) else 1)))
                for a, b in pieces(name, u):
                    part = high_part(name, u, a, b)
                    ins = act.activation(part, like(ring[:, r, a:b], part), ACT.Copy)
                ins.then_inc(hi_done, 1)

            def first_highs(name):
                for n in range(2 if name.startswith(DEEP) else 1):
                    high(name, n, 0, n)

            def stream(name, after=None, body=None, ahead=None):
                ahead = ahead or (2 if name.startswith(DEEP) else 1)

                def slot(n, i, u):
                    if isinstance(n, int) and n + ahead >= COUNT[name]:
                        if after is not None and n + ahead - COUNT[name] < COUNT[after]:
                            high(after, n + ahead - COUNT[name], 0, n + ahead - COUNT[name])
                    else:
                        high(name, n + ahead, i + (u + ahead) // RING, (u + ahead) % RING)
                    if body is not None:
                        body(n, i, u)
                over_slots(act, COUNT[name], slot, apart=ahead)

            def load_ada(m, g, b):
                act.wait_ge(ada_used, ada_count(m, g) + (CREDIT - 1))
                act.dma_start(ada_w[:, b, :], A["ada_later"][g + UNITS * m, :, :]).then_inc(ada_landed[b], 16)

            def norm(k, t0):
                act.wait_ge(x_done, CREDIT + X_BEFORE[k])
                if (k, 0) in MOD_IN:
                    for g in range(2):
                        load_ada(MOD_IN[k, 0], g, g)
                for c in range(DC):
                    act.activation(h[:, c, t0:T], x[:, c, t0:T], ACT.Square).then_inc(sq_done, 1)
                act.wait_ge(stat_done, k + 1)
                act.activation(std[:, t0:T], psum[STAT][:, t0:T], ACT.Sqrt, scale=1.0 / D, bias=eps).then_inc(std_done, 1)
                if t0 == 0:
                    act.wait_ge(mod_done, k + 1)
                    for c in range(DC):
                        act.wait_ge(xn_done, DC * k + c + 1)
                        act.activation(h[:, c, 0:CTX], h[:, c, 0:CTX], ACT.Identity, scale=amp[:, k, 2 * c:2 * c + 1],
                                       bias=mod[:, k, 0, 2 * c:2 * c + 1]).then_inc(h0_done, 1)

            def ffn(f, k, t0, after):
                l, half = divmod(f, 2)
                for hf in range(2):
                    def slot(n, i, u, hf=hf):
                        act.wait_ge(slots_used, n + used(f"w1_{l}{half}{hf}", 0))
                        act.activation(tanh2[:, u % 2, t0:T], psum[u % 2][:, t0:T], ACT.Tanh, scale=0.5).then_inc(tanh_done, 1)
                        if m is not None and not isinstance(n, int):
                            load_ada(m, n + 2, u % 2)

                    def out_slot(n, i, u):
                        if m is not None and n % 2 == 0:
                            g = 8 + n // 2 + 2
                            if g < UNITS:
                                load_ada(m, g, g % 2)
                            elif (k, hf + 1) in MOD_IN:
                                load_ada(m + 1, g - UNITS, g % 2)
                    m = MOD_IN.get((k, hf))
                    stream(f"w1_{l}{half}{hf}", f"w2_{l}{half}{hf}", slot)
                    stream(f"w2_{l}{half}{hf}", f"w1_{l}{half}1" if hf == 0 else after, out_slot)

            def window(k):
                def take(n, i, u):
                    for m in (2 * n, 2 * n + 1):
                        t0 = CTX if m < 8 else 0
                        act.wait_ge(slots_used, used("swa_qk", n))
                        act.activation(sqk[:, m, t0:T], psum[m % 4][:, t0:T], ACT.Copy).then_inc(sw_done, 1)
                for n in range(5):
                    if n < 4:
                        high("swa_qk", n + 1, (n + 1) // RING, (n + 1) % RING)
                    else:
                        high("swa_v", 0, 0, 0)
                    take(n, 0, 0)
                act.wait_ge(slots_used, used("swa_v", 0))
                for tc in range(4):
                    act.activation(svt[:, tc, :], psum[(tc + 2) % 4][:, 0:256], ACT.Copy).then_inc(sw_done, 1)
                for c in range(10):
                    t0 = CTX if c < 8 else 0
                    act.wait_ge(sw_done, c + 1)
                    if c >= 4:
                        act.wait_ge(hsum_done, 24 + c - 3)
                    act.activation(sqh[:, c % 4, t0:T], sqk[:, c, t0:T], ACT.Square).then_inc(hs_done, 1)
                    if c >= 1:
                        roots(c - 1, 24, 10, 1.0 / SD, 4, CTX if c - 1 < 8 else 0)
                roots(9, 24, 10, 1.0 / SD, 4)
                for kvp in range(2):
                    with act.Fori(0, 2) as i:
                        attend_act(8, lambda U: U + i * 8 + kvp * 16, lambda u: window_exp(kvp, i, u), 512)
                act.wait_ge(at["od"], CREDIT + 32)
                high("swa_out", 0, 0, 0)
                stream("swa_out")
                act.wait_ge(slots_used, BASE["w1_110"])
                first_highs("w1_110")

            def window_exp(kvp, i, u):
                j, r = u // 2 % 2, u % 2
                sink = par[:, bass.ds(i * 2 + (POFF["sink"] + 4 * (2 * kvp + r) + u // 4), 1)]
                act.activation(expo[:, u % 2, :], logit[:, u % 2, :], ACT.Exp, bias=small[:, 1, u:u + 1],
                               accum_out=small[:, 2, u:u + 1])
                act.activation(small[:, 3, u:u + 1], sink, ACT.Exp, bias=small[:, 1, u:u + 1]).then_inc(at["e"], 1)

            def attend_act(units, at_unit, exps, width):
                for t in range(units + 1):
                    if t < units:
                        act.wait_ge(at["m"], at_unit(t + 1))
                        exps(t)
                    if t >= 1:
                        u = t - 1
                        act.wait_ge(at["t"], at_unit(u + 1))
                        act.activation(probt[:, u % 2, 0:width], psum[2 + u % 2][:, 0:width], ACT.Copy).then_inc(at["tc"], 1)

            def tables():
                act.wait_ge(tab_dve, 1)
                act.activation(late("sp", 0, 16), late("sp", 0, 16), ACT.Exp).then_inc(tab_act, 1)
                act.wait_ge(tab_dve, 2)
                act.activation(late("sp", 32, 16), late("sp", 16, 16), ACT.Ln).then_inc(tab_act, 1)
                act.wait_ge(tab_dve, 3)
                act.activation(late("m_sin"), late("t0"), ACT.Sin).then_inc(tab_act, 1)
                act.wait_ge(tab_dve, 4)
                act.activation(late("m_cos"), late("t0"), ACT.Sin).then_inc(tab_act, 1)

            def block2(l):
                if l == 0:
                    act.sem_inc(pj_done, 4)

                def proj(n, i, u):
                    for q in range(2):
                        if q == 0:
                            act.wait_ge(slots_used, n + used(f"mla_in{l}", 0))
                        m = 2 * n + q
                        src = psum[(2 * u + q) % 4][:, 0:SEQ]
                        if m < 8:
                            act.activation(gelu_in[:, m * SEQ:(m + 1) * SEQ], src, ACT.Copy).then_inc(pj_done, 1)
                        elif m < 13:
                            act.activation(lat[:, m - 8, :], src, ACT.Copy).then_inc(pj_done, 1)
                        elif m < 29:
                            act.activation(gate_a_b[:, (m - 13) * SEQ:(m - 12) * SEQ], src, ACT.Tanh, scale=0.5).then_inc(pj_done, 1)
                        else:
                            act.activation(kpe[64:96, :], src[64:96, :], ACT.Copy).then_inc(pj_done, 1)
                stream(f"mla_r{l}", f"mla_in{l}")
                for n in range(15):
                    if n < 13:
                        high(f"mla_in{l}", n + 2, (n + 2) // RING, (n + 2) % RING)
                    proj(n, n // RING, n % RING)
                act.wait_ge(pj_done, 4 + 30 * (l + 1))
                act.activation(core[:, 0:1280], big[:, 8192:9472], ACT.Square).then_inc(ml_sq, 1)
                act.wait_ge(ml_sum, l + 1)
                act.activation(lat_std[:, 0:SEQ], psum[STAT][:, 0:SEQ], ACT.Sqrt, scale=1.0 / (QL * P), bias=eps)
                act.activation(lat_std[:, SEQ:T], psum[STAT][:, SEQ:T], ACT.Sqrt, scale=1.0 / (KVL * P), bias=eps)\
                    .then_inc(ml_std, 1)
                for c in range(RC):
                    act.wait_ge(rg_done, RC * l + c + 1)
                    act.activation(rx[:, c * SEQ:(c + 1) * SEQ], psum[c % 4][:, 0:SEQ], ACT.Tanh, scale=0.5,
                                   bias=p_("gx_b", RC * l + c, 1))
                    act.activation(ra[:, c * SEQ:(c + 1) * SEQ], psum[c % 4][:, SEQ:T], ACT.Tanh, scale=0.5,
                                   bias=p_("ga_b", RC * l + c, 1)).then_inc(rt_done, 1)
                act.wait_ge(rl_dve, 4 * l + 1)
                act.activation(rdec, ra, ACT.Exp)
                act.activation(re2, ra, ACT.Exp, scale=2.0)
                act.activation(rth, ra, ACT.Tanh).then_inc(rl_act, 1)
                act.wait_ge(rl_dve, 4 * l + 2)
                act.activation(re2, re2, ACT.Sqrt, scale=-1.0).then_inc(rl_act, 1)
                act.activation(rth, gelu_in, ACT.Square).then_inc(rl_act, 1)
                act.wait_ge(rl_dve, 4 * l + 3)
                act.activation(rth, rth, ACT.Tanh, scale=GELU_C).then_inc(rl_act, 1)
                for m in range(20):
                    if m < 8:
                        act.wait_ge(slots_used, used(f"mla_uq{l}", m // 2))
                        act.activation(mq[0:96, 2 * m:2 * m + 2, :].rearrange("p c t -> p (c t)"), psum[m % 4][0:96, :], ACT.Copy)\
                            .then_inc(uq_done, 1)
                    elif m < 16:
                        c = m - 8
                        act.wait_ge(uk_done, 8 * l + c + 1)
                        act.activation(mk[0:64, 2 * c:2 * c + 2, :].rearrange("p c t -> p (c t)"), psum[m % 4][0:64, :], ACT.Copy)\
                            .then_inc(uq_done, 1)
                    else:
                        c = m - 16
                        act.wait_ge(uv_done, 4 * l + c + 1)
                        act.activation(vtok[:, c // 2, (c % 2) * 512:(c % 2) * 512 + 512], psum[m % 4][:, :], ACT.Copy)\
                            .then_inc(uq_done, 1)
                with act.Fori(0, 4) as i:
                    attend_act(4, lambda U: U + i * 4 + (32 + 16 * l), mla_exp, 384)
                act.wait_ge(at["od"], CREDIT + 32 + 16 * (l + 1))
                first_highs(f"mla_out{l}")
                stream(f"mla_out{l}", f"up{l}")
                layer_norm(2 * l)

                def gel(n, i, u):
                    act.wait_ge(cg_done, n + (FC2 * l + 1))
                    act.activation(gsq[:, u % 2, :], conv_g[:, u % 2, :], ACT.Square).then_inc(gs_done, 1)
                    act.wait_ge(gp_done, n + (FC2 * l + 1))
                    act.activation(gtanh[:, u % 2, :], gpoly[:, u % 2, :], ACT.Tanh, scale=GELU_C).then_inc(gt_done, 1)
                stream(f"up{l}", f"down{l}", gel)
                stream(f"down{l}", f"mla_r{l + 1}" if l < DEPTH - 1 else None)
                layer_norm(2 * l + 1)

            def mla_exp(u):
                act.activation(expo[:, u % 2, 0:P], logit[:, u % 2, 0:P], ACT.Exp, bias=small[:, 2, u:u + 1],
                               accum_out=small[:, 4, u:u + 1])
                act.activation(expo[:, u % 2, P:3 * P], logit[:, u % 2, P:3 * P], ACT.Exp, bias=small[:, 3, u:u + 1],
                               accum_out=small[:, 5, u:u + 1]).then_inc(at["e"], 1)

            def layer_norm(m):
                for c in range(DC):
                    act.wait_ge(ln_cent, DC * m + c + 1)
                    act.activation(hlow[:, c, :], hhigh[:, c, :], ACT.Square).then_inc(ln_sq, 1)
                act.wait_ge(ln_var, m + 1)
                act.activation(ln_std, psum[STAT][:, SEQ:T], ACT.Sqrt, scale=1.0 / D, bias=eps).then_inc(ln_root, 1)

            def delta(k):
                mine = Steps(act, act_step)
                mine.n = act_steps[0]

                def proj(n, i, u):
                    for q in range(2):
                        act.wait_ge(conv_done, 2 * n + (q + 1))
                        act.activation(ttmp[:, q, :], conv2[:, q, :], ACT.Tanh).then_inc(pr_tanh, 1)
                high("dn_in", 1, 0, 1)
                stream("dn_in", "dn_ab", proj, ahead=2)
                for c in range(16):
                    if c >= 4:
                        act.wait_ge(hsum_done, c - 3)
                    if c == 0:
                        act.wait_ge(pr_free, 4 + 32)
                        act.wait_ge(slots_used, used("dn_ab", 0))
                    act.activation(sqh[:, c % 4, :], qkv[:, c, :], ACT.Square).then_inc(hs_done, 1)
                    if c >= 1:
                        roots(c - 1, 0, 16, 1.0, 4)
                roots(15, 0, 16, 1.0, 4)
                act.wait_ge(gate_step, 1)
                mine(act.activation(tokv(TOK_T2), tokv(TOK_T2), ACT.Exp, scale=-1.0))
                mine(act.activation(p_("dn_a"), p_("dn_a"), ACT.Exp))
                act.activation(tokv(TOK_T2), tokv(TOK_T2), ACT.Ln, bias=ones[:, 0:1]).then_inc(gate_act, 1)
                act.activation(tokv(TOK_BETA), tokv(TOK_BETA), ACT.Tanh, scale=0.5).then_inc(gate_act, 1)
                act.wait_ge(gate_pe, 1)
                act.activation(tokv(TOK_EGC), psum[MISC][:, 0:64], ACT.Exp).then_inc(gate_act, 1)
                with act.Fori(0, 2) as hg:
                    with act.Fori(0, 2) as cp:
                        for cc in range(2):
                            delta_unit_act(hg, cp, cc)
                for c in range(DNH):
                    if c == 0:
                        act.wait_ge(dn["state"][0], 10)
                        act.wait_ge(dn["state"][1], 10)
                    if c >= 4:
                        act.wait_ge(hsum_done, 16 + c - 3)
                    act.activation(sqh[:, c % 4, :], h[:, c, :], ACT.Square).then_inc(hs_done, 1)
                    if c >= 1:
                        roots(c - 1, 16, DNH, 1.0 / 128, 6)
                roots(DNH - 1, 16, DNH, 1.0 / 128, 6)
                act_steps[0] = mine.n
                act.wait_ge(y_in_done, DNH)
                high("dn_out", 0, 0, 0)
                stream("dn_out", "w1_010")

            act_steps = [1]

            def roots(c, base, count, scale, bank, t0=0):
                act.wait_ge(hsum_done, base + c + 1)
                if c >= 8:
                    act.wait_ge(hnorm_done, base + c - 7)
                act.activation(dstd[:, c % 8, t0:T], psum[bank + c % 2][:, t0:T], ACT.Sqrt, scale=scale, bias=eps)\
                    .then_inc(hstd_done, 1)

            def delta_unit_act(hg, cp, cc):
                U = hg * 4 + cp * 2 + cc
                for s in range(2):
                    q, b = quad[s], dbank[s]
                    act.wait_ge(dn["gr"][s], U + 1)
                    act.activation(q["EG"], b[0], ACT.Exp).then_inc(dn["eg"][s], 1)
                for s in range(2):
                    q, b = quad[s], dbank[s]
                    act.wait_ge(dn["d"][s], U + 1)
                    act.activation(q["DT"], q["TG"], ACT.Exp).then_inc(dn["dt"][s], 1)
                for s in range(2):
                    q, b = quad[s], dbank[s]
                    act.wait_ge(dn["xtr"][s], U + 1)
                    act.activation(q["X"], b[0], ACT.Copy).then_inc(dn["x0"][s], 1)
                for n in range(1, LEVELS):
                    for s in range(2):
                        q, b = quad[s], dbank[s]
                        act.wait_ge(dn["y"][s], U * (LEVELS - 1) + n)
                        act.activation(q["Y"][:, :, seen(s, n)], b[0][:, :, seen(s, n)], ACT.Copy).then_inc(dn["yc"][s], 1)
                for s in range(2):
                    q, b = quad[s], dbank[s]
                    act.wait_ge(dn["wt"][s], U + 1)
                    act.activation(q["Y"], b[0], ACT.Copy, scale=-1.0).then_inc(dn["nw"][s], 1)
                for s in range(2):
                    q, b = quad[s], dbank[s]
                    act.wait_ge(dn["vmm"][s], U + 1)
                    act.activation(q["X"], b[1], ACT.Copy).then_inc(dn["vn"][s], 1)

            first_highs("w1_000")
            act.wait_ge(x_in, 16)
            act.wait_ge(consts_in, 16)
            for l in range(DEPTH):
                for sub in range(3):
                    k = 3 * l + sub
                    t0 = CTX if k == 5 else 0
                    norm(k, t0)
                    if sub != 1:
                        ffn(2 * l + sub // 2, k, t0, {0: "dn_in", 2: "w1_100", 3: "swa_qk", 5: "mla_r0"}[k])
                    if k == 1:
                        delta(k)
                    if k == 4:
                        window(k)

            tables()
            for l in range(DEPTH):
                block2(l)

        @block.vector
        def _(dve):
            step = Steps(dve, dve_step)
            turn = Steps(dve, dve_turn)
            for _ in range(CREDIT):
                dve.sem_inc(x_done, 1)
                dve.sem_inc(hid_done, 1)
                dve.sem_inc(ada_used, 1)
            dve.sem_inc(h2_done, 4)
            dve.sem_inc(pr_free, 4)
            dve.wait_ge(act_step, 1)
            step(dve.scalar_tensor_tensor(ctmp[:, :, :], ctmp[:, :, :], 1.0, p_("cond").rearrange("p (c s) -> p c s", s=2),
                                          ALU.add, ALU.mult))
            dve.tensor_scalar(cond[:, :, :], ctmp[:, :, :], 0.5, None, ALU.mult).then_inc(cond_done, 1)
            dve.wait_ge(cond_done, 1)

            def ada_tile(mark, w, b):
                n = [0, 0]
                for c in range(DC):
                    wc = w[:, c * 256:(c + 1) * 256]
                    for s in range(2):
                        acc = ada_acc[:, b, s, :]
                        if c == 0:
                            ins = dve.tensor_scalar(acc, wc, cond[:, c, s:s + 1], None, ALU.mult)
                        else:
                            mark.until(n[s])
                            ins = dve.scalar_tensor_tensor(acc, wc, cond[:, c, s:s + 1], acc, ALU.mult, ALU.add)
                        if c < DC - 1:
                            n[s] = mark.mark(ins)
                ins.then_inc(ada_used, 1)

            def ada_step(mark, m, g, h, b):
                dve.wait_ge(ada_landed[b], h * 16 + 16)
                dve.wait_ge(ada_summed, g + (UNITS * m + CREDIT - 1))
                ada_tile(mark, ada_w[:, b, :], b)

            def modulation(k):
                mk_ = mod[:, k, :, :].rearrange("p b c -> p (b c)")
                step(dve.tensor_tensor(mk_, psum[MISC][:, 0:48], p_("ada_b", 48 * k, 48), ALU.add))
                dve.tensor_scalar(hgate[:, k, :], mod[:, k, 2, :], 0.5, None, ALU.mult)
                dve.scalar_tensor_tensor(amp[:, k, :], mod[:, k, 1, :], 1.0, p_("norm_g", 16 * k, 16),
                                         ALU.add, ALU.mult).then_inc(mod_done, 1)
                dve.wait_ge(mod_done, k + 1)

            with dve.Fori(0, UNITS // RING) as i:
                for u in (1, 3):
                    ada_tile(turn, ring[:, landed_slot(dve, "ada", i, u), :], u // 2)
                turn.reset()
            dve.wait_ge(slots_used, used("ada", UNITS - 1))
            modulation(0)

            def split(name, c, v, t0, t1=T):
                n = h_split(name, c)
                dve.tensor_copy(h_hi[:, c, t0:t1], v).then_inc(hh_done, 1)
                dve.wait_ge(hh_done, n)
                return dve.tensor_tensor(h_lo[:, c, t0:t1], v, h_hi[:, c, t0:t1].bitcast(F32), ALU.subtract)\
                    .then_inc(hl_done, 1)

            def norm(k, t0):
                dve.wait_ge(std_done, k + 1)
                step(dve.reciprocal(rstd[:, t0:T], std[:, t0:T]))
                for c in range(DC):
                    dve.tensor_tensor(h[:, c, t0:T], x[:, c, t0:T], rstd[:, t0:T], ALU.mult).then_inc(xn_done, 1)
                for c in range(DC):
                    dve.wait_ge(xn_done, DC * k + c + 1)
                    dve.tensor_scalar(h[:, c, CTX:T], h[:, c, CTX:T], amp[:, k, 2 * c + 1:2 * c + 2],
                                      mod[:, k, 0, 2 * c + 1:2 * c + 2], ALU.mult, ALU.add).then_inc(h1_done, 1)
                    dve.wait_ge(h1_done, DC * k + c + 1)
                    if t0 == 0:
                        dve.wait_ge(h0_done, DC * k + c + 1)
                    split(f"k{k}", c, h[:, c, t0:T], t0)

            def add_out(name, k, per_chunk, gate, t0, m=None):
                for c in range(DC):
                    if m is not None and c % 2 == 0:
                        g = 8 + c // 2
                        ada_step(step, m, g, UNITS // 2 * m + g // 2, g % 2)
                    slot = c if per_chunk == 0 else c // 2
                    dve.wait_ge(slots_used, used(name, slot))
                    for s in range(0 if t0 == 0 else 1, 2):
                        xs = x[:, c, s * CTX:(s + 1) * CTX]
                        ins = dve.scalar_tensor_tensor(xs, psum[OUT_BANK + c % 2][:, s * CTX:(s + 1) * CTX],
                                                       gate[:, 2 * c + s:2 * c + s + 1], xs, ALU.mult, ALU.add)
                    ins.then_inc(x_done, 1)

            def ffn(f, k, t0):
                l, half = divmod(f, 2)
                for hf in range(2):
                    def slot(n, i, u, hf=hf):
                        if m is not None and not isinstance(n, int):
                            ada_step(turn, m, n, i * 2 + (UNITS // 2 * m + u // 2), u % 2)
                        dve.wait_ge(tanh_done, n + (FHC * f + 11 * hf + 1))
                        turn(dve.scalar_tensor_tensor(swu2[:, u % 2, t0:T], tanh2[:, u % 2, t0:T], 1.0, psum[u % 2][:, t0:T],
                                                      ALU.add, ALU.mult))
                        turn(dve.scalar_tensor_tensor(hid2[:, u % 2, t0:T], swu2[:, u % 2, t0:T], 0.5, psum[2 + u % 2][:, t0:T],
                                                      ALU.mult, ALU.mult))
                        one = lambda v: v[:, bass.ds(n, 1), t0:T].rearrange("p a t -> p (a t)")
                        turn.last(dve.tensor_copy(one(hid_hi), hid2[:, u % 2, t0:T]))
                        dve.tensor_tensor(one(hid_lo), hid2[:, u % 2, t0:T], one(hid_hi).bitcast(F32), ALU.subtract)\
                            .then_inc(hid_done, 1)
                    m = MOD_IN.get((k, hf))
                    over_slots(dve, 11, slot)
                    add_out(f"w2_{l}{half}{hf}", k, 0, hgate[:, k, :], t0, m)
                    if m is not None:
                        dve.wait_ge(ada_summed, CREDIT + UNITS * (m + 1))
                        modulation(m + 1)

            def window(k):
                dve.sem_inc(at["od"], CREDIT)
                dve.wait_ge(late_in, 32)
                for c in range(10):
                    t0 = CTX if c < 8 else 0
                    gain = p_("q_gain") if c < 8 else p_("k_gain")
                    dve.wait_ge(hstd_done, 24 + c + 1)
                    step(dve.reciprocal(grec[:, c % 4, t0:T], dstd[:, c % 8, t0:T]))
                    dve.scalar_tensor_tensor(sqk[:, c, t0:T], sqk[:, c, t0:T], gain, grec[:, c % 4, t0:T],
                                             ALU.mult, ALU.mult).then_inc(hnorm_done, 1)
                    if c >= 1:
                        rope(c - 1)
                rope(9)
                for kvp in range(2):
                    with dve.Fori(0, 2) as i:
                        sink_now[0] = (kvp, i)
                        attend_dve(8, lambda U: U + i * 8 + kvp * 16, window_logits, window_norm,
                                   lambda u: window_take(kvp, i, u))
                for c in range(DC):
                    dve.wait_ge(at["od"], CREDIT + 32)
                    split("swa_out", c, h[:, c, CTX:T], CTX)
                add_out("swa_out", k, 1, mod[:, k, 2, :], CTX)

            def rope(c):
                xs = sqk[:, c, CTX:T]
                tmp = conv2[:, c % 2, 0:SEQ]
                dve.wait_ge(rot_done, c + 1)
                step(dve.tensor_tensor(tmp, psum[6 + c % 2][:, 0:SEQ], late("s_sin"), ALU.mult))
                step(dve.tensor_tensor(xs, xs, late("s_cos"), ALU.mult))
                dve.tensor_tensor(xs, xs, tmp, ALU.add).then_inc(rope_done, 1)

            def attend_dve(units, at_unit, logits, norm, take):
                for t in range(units + 2):
                    if t < units:
                        dve.wait_ge(at["s"], at_unit(t + 1))
                        logits(t)
                    if 1 <= t <= units:
                        dve.wait_ge(at["e"], at_unit(t))
                        norm(t - 1)
                    if t >= 2:
                        dve.wait_ge(at["o"], at_unit(t - 1))
                        take(t - 2)

            def window_logits(u):
                j, r = u // 2 % 2, u % 2
                turn(dve.scalar_tensor_tensor(logit[:, u % 2, :], psum[u % 2][:, :], SD ** -0.5, late("s_mask", j * T, T),
                                              ALU.mult, ALU.add))
                turn(dve.reduce_max(small[:, 0, u:u + 1], logit[:, u % 2, :], AX.X))
                dve.tensor_scalar(small[:, 1, u:u + 1], small[:, 0, u:u + 1], sink_of(u), -1.0, ALU.max, ALU.mult)\
                    .then_inc(at["m"], 1)

            sink_now = [None]

            def sink_of(u):
                kvp, i = sink_now[0]
                return par[:, bass.ds(i * 2 + (POFF["sink"] + 4 * (2 * kvp + u % 2) + u // 4), 1)]

            def window_norm(u):
                turn(dve.tensor_tensor(small[:, 4, u:u + 1], small[:, 2, u:u + 1], small[:, 3, u:u + 1], ALU.add))
                (turn.last if u == 7 else turn)(dve.reciprocal(small[:, 5, u:u + 1], small[:, 4, u:u + 1]))
                dve.tensor_scalar(expo[:, u % 2, :], expo[:, u % 2, :], small[:, 5, u:u + 1], None, ALU.mult).then_inc(at["p"], 1)

            def window_take(kvp, i, u):
                b, j, r = u // 4, u // 2 % 2, u % 2
                dst = h[64 * r:64 * r + 64, bass.ds(i * 2 + (kvp * 4 + b), 1), CTX + j * P:CTX + (j + 1) * P]
                dve.tensor_copy(dst.rearrange("p a t -> p (a t)"), psum[4 + u % 2][64 * r:64 * r + 64, 0:P]).then_inc(at["od"], 1)

            def tables():
                lam = p_("lam")
                dve.wait_ge(late_in, 32)
                dve.scalar_tensor_tensor(late("sp", 0, 16), lam, -1.0, lam, ALU.mult, ALU.min).then_inc(tab_dve, 1)
                for nm in ("gx_b", "ga_b"):
                    step(dve.tensor_scalar(p_(nm), p_(nm), 0.5, None, ALU.mult))
                dve.wait_ge(tab_act, 1)
                dve.tensor_scalar(late("sp", 16, 16), late("sp", 0, 16), 1.0, None, ALU.add).then_inc(tab_dve, 1)
                dve.wait_ge(tab_dve, 2)
                step(dve.tensor_scalar(late("sp", 48, 16), late("sp", 16, 16), -1.0, None, ALU.add))
                step(dve.tensor_scalar(late("sp", 64, 16), late("sp", 48, 16), 0.0, None, ALU.is_equal))
                step(dve.tensor_tensor(late("sp", 48, 16), late("sp", 48, 16), late("sp", 64, 16), ALU.add))
                dve.wait_ge(tab_act, 2)
                step(dve.tensor_tensor(late("sp", 32, 16), late("sp", 32, 16), late("sp", 64, 16), ALU.add))
                step(dve.reciprocal(late("sp", 80, 16), late("sp", 48, 16)))
                step(dve.tensor_tensor(late("sp", 32, 16), late("sp", 32, 16), late("sp", 80, 16), ALU.mult))
                step(dve.tensor_tensor(late("sp", 32, 16), late("sp", 32, 16), late("sp", 0, 16), ALU.mult))
                step(dve.tensor_scalar(late("sp", 0, 16), lam, -1.0, 0.0, ALU.mult, ALU.max))
                step(dve.tensor_tensor(late("sp", 0, 16), late("sp", 0, 16), late("sp", 32, 16), ALU.add))
                step(dve.tensor_scalar(late("nspl"), late("sp", 0, 16), -4.0, None, ALU.mult))
                t0, t1, cos = late("t0"), late("t1"), late("m_cos")
                pos = late("pos").bitcast(I32)
                step(dve.tensor_copy(t1, pos))
                step(dve.tensor_scalar(t1, t1, late("m_freq"), None, ALU.mult))
                for n, quarter in enumerate((0.0, 0.25)):
                    if n:
                        dve.wait_ge(tab_act, 3)
                    k = cos
                    step(dve.tensor_scalar(k, t1, 1.0 / (2 * np.pi), quarter, ALU.mult, ALU.add))
                    step(dve.tensor_scalar(k, k, ROUND, None, ALU.add))
                    step(dve.tensor_scalar(k, k, -ROUND, None, ALU.add))
                    step(dve.scalar_tensor_tensor(t0, k, -TWO_PI[0], t1, ALU.mult, ALU.add))
                    step(dve.scalar_tensor_tensor(t0, k, -TWO_PI[1], t0, ALU.mult, ALU.add))
                    step(dve.scalar_tensor_tensor(t0, k, -TWO_PI[2], t0, ALU.mult, ALU.add))
                    step(dve.tensor_scalar(t0, t0, 2 * np.pi * quarter, None, ALU.add))
                    dve.tensor_scalar(t0, t0, -PI_IN, PI_IN, ALU.max, ALU.min).then_inc(tab_dve, 1)
                dve.wait_ge(tab_act, 4)
                dve.tensor_scalar(late("m_sin"), late("m_sin"), late("m_sign"), None, ALU.mult).then_inc(tab_dve, 1)
                dve.wait_ge(tab_dve, 5)

            def block2(l):
                if l == 0:
                    dve.wait_ge(x_done, CREDIT + X_FIRST)
                split_x(f"mla_in{l}")
                cw = lambda c, tap: p_("conv_w", (RC * l + c) * CW + tap, 1)
                for c in range(RC):
                    if c % 2 == 0:
                        dve.wait_ge(slots_used, used(f"mla_r{l}", c // 2))
                    src, dst = psum[c % 4], xc[:, c, :]
                    step(dve.tensor_scalar(dst, src[:, 0:SEQ], cw(c, 3), p_("conv_b", RC * l + c, 1), ALU.mult, ALU.add))
                    for tap in (0, 1, 2):
                        o = 3 - tap
                        ins = dve.scalar_tensor_tensor(dst[:, o:SEQ], src[:, 0:SEQ - o], cw(c, tap), dst[:, o:SEQ],
                                                       ALU.mult, ALU.add)
                        if tap < 2:
                            step(ins)
                        else:
                            ins.then_inc(xc_done, 1)
                dve.wait_ge(ml_std, l + 1)
                step(dve.reciprocal(lat_r, lat_std))
                for c in range(QL + KVL):
                    g = p_("qn_g", QL * l + c, 1) if c < QL else p_("kvn_g", KVL * l + c - QL, 1)
                    r = lat_r[:, 0:SEQ] if c < QL else lat_r[:, SEQ:T]
                    ins = dve.scalar_tensor_tensor(lat[:, c, :], lat[:, c, :], g, r, ALU.mult, ALU.mult)
                ins.then_inc(ml_n, 1)
                for c in range(RC):
                    dve.wait_ge(rt_done, RC * l + c + 1)
                    n = late("nspl", RC * l + c, 1)
                    seg = ra[:, c * SEQ:(c + 1) * SEQ]
                    ins = dve.tensor_scalar(seg, seg, n, n, ALU.mult, ALU.add)
                ins.then_inc(rl_dve, 1)
                step(dve.scalar_tensor_tensor(rx, rx, 1.0, big[:, 0:2048], ALU.add, ALU.mult))
                dve.wait_ge(rl_act, 4 * l + 1)
                dve.scalar_tensor_tensor(re2, re2, 1.0, rth, ALU.add, ALU.mult).then_inc(rl_dve, 1)
                dve.wait_ge(rl_act, 4 * l + 2)
                step(dve.scalar_tensor_tensor(rx, rx, 0.5, re2, ALU.mult, ALU.mult))
                for c in range(RC):
                    sl = slice(c * SEQ, (c + 1) * SEQ)
                    step(dve.tensor_tensor_scan(ra[:, sl], rdec[:, sl], rx[:, sl], 0.0, ALU.mult, ALU.add))
                dve.wait_ge(rl_act, 4 * l + 3)
                step(dve.tensor_scalar(rth, rth, 0.044715, 1.0, ALU.mult, ALU.add))
                dve.tensor_tensor(rth, rth, gelu_in, ALU.mult).then_inc(rl_dve, 1)
                step(dve.scalar_tensor_tensor(gate_a, gate_a, 1.0, ra, ALU.add, ALU.mult))
                step(dve.tensor_tensor(gate_a, gate_a, gelu_in, ALU.mult))
                dve.wait_ge(rl_act, 4 * l + 4)
                dve.scalar_tensor_tensor(gate_a, rth, 1.0, gate_a, ALU.add, ALU.mult).then_inc(rl_dve, 1)
                dve.wait_ge(rl_dve, 4 * (l + 1))
                for m in range(9):
                    dve.wait_ge(rot_done, 10 + 9 * l + m + 1)
                    if m == 0:
                        v, tmp, sw = kpe[64:96, :], mtmp[64:96, 0:SEQ], psum[4][64:96, 0:SEQ]
                        cs, sn = late("m_cos")[64:96, :], late("m_sin")[64:96, :]
                    else:
                        v, tmp = mq[64:96, 2 * m - 2:2 * m, :], by8(mtmp[64:96, 512:1024])
                        sw = psum[4 + m % 2][64:96, :].rearrange("p (c t) -> p c t", t=SEQ)
                        cs, sn = (late(nm)[64:96, :].unsqueeze(1).broadcast_to([32, 2, SEQ]) for nm in ("m_cos", "m_sin"))
                    step(dve.tensor_tensor(tmp, sw, sn, ALU.mult))
                    step(dve.tensor_tensor(v, v, cs, ALU.mult))
                    dve.tensor_tensor(v, v, tmp, ALU.add).then_inc(rope_done, 1)
                    dve.wait_ge(rope_done, 10 + 9 * l + m + 1)
                with dve.Fori(0, 4) as i:
                    attend_dve(4, lambda U: U + i * 4 + (32 + 16 * l), mla_logits, mla_norm, lambda u: mla_take(i, u, l))
                dve.wait_ge(at["od"], CREDIT + 32 + 16 * (l + 1))
                step(dve.tensor_scalar(gate_a, gate_a, 0.25, None, ALU.mult))
                dve.scalar_tensor_tensor(hhigh, hhigh, 0.5, by8(gate_a), ALU.mult, ALU.add).then_inc(merged, 1)
                dve.wait_ge(merged, l + 1)
                for c in range(DC):
                    split(f"mla_out{l}", c, hhigh[:, c, :], CTX)
                add_scaled(f"mla_out{l}", 1, 6 + 2 * l)
                layer_norm(2 * l, "ln1", l)
                split_x(f"up{l}")

                def conv(dst, src, c):
                    w = lambda tap: par[:, bass.ds(c * FCW + (POFF["fc_w"] + tap), 1)]
                    turn(dve.tensor_scalar(dst, src, w(2), par[:, bass.ds(c + POFF["fc_b"], 1)], ALU.mult, ALU.add))
                    turn(dve.scalar_tensor_tensor(dst[:, 1:SEQ], src[:, 0:SEQ - 1], w(1), dst[:, 1:SEQ], ALU.mult, ALU.add))
                    return dve.scalar_tensor_tensor(dst[:, 2:SEQ], src[:, 0:SEQ - 2], w(0), dst[:, 2:SEQ], ALU.mult, ALU.add)

                def gel(n, i, u):
                    b = u % 2
                    bank = psum[u % 4]
                    dve.wait_ge(slots_used, n + used(f"up{l}", 0))
                    dve.wait_ge(h2_done, n + (FC2 * l + 3))
                    conv(conv_g[:, b, :], bank[:, 0:SEQ], n + 48 * l).then_inc(cg_done, 1)
                    turn(conv(conv_v[:, b, :], bank[:, SEQ:T], n + (48 * l + 24)))
                    if u > 0:
                        finish(n - 1, u - 1)
                    dve.wait_ge(gs_done, n + (FC2 * l + 1))
                    turn(dve.tensor_scalar(gpoly[:, b, :], gsq[:, b, :], 0.044715, 1.0, ALU.mult, ALU.add))
                    dve.tensor_tensor(gpoly[:, b, :], gpoly[:, b, :], conv_g[:, b, :], ALU.mult).then_inc(gp_done, 1)
                    if u == RING - 1:
                        finish(n, u)

                def finish(n, u):
                    b = u % 2
                    dve.wait_ge(gt_done, n + (FC2 * l + 1))
                    turn(dve.scalar_tensor_tensor(conv_g[:, b, :], gtanh[:, b, :], 1.0, conv_g[:, b, :], ALU.add, ALU.mult))
                    turn(dve.scalar_tensor_tensor(hid2[:, b, 0:SEQ], conv_g[:, b, :], 0.5, conv_v[:, b, :], ALU.mult, ALU.mult))
                    one = lambda v: v[:, bass.ds(n, 1), :].rearrange("p a t -> p (a t)")
                    (turn.last if u == RING - 1 else turn)(dve.tensor_copy(one(mhid_hi), hid2[:, b, 0:SEQ]))
                    dve.tensor_tensor(one(mhid_lo), hid2[:, b, 0:SEQ], one(mhid_hi).bitcast(F32), ALU.subtract)\
                        .then_inc(h2_done, 1)
                over_slots(dve, FC2, gel)
                add_scaled(f"down{l}", 2, 7 + 2 * l)
                layer_norm(2 * l + 1, "ln2", l)

            def split_x(name):
                if H_SPLITS.index(name) > H_SPLITS.index("mla_in0"):
                    dve.wait_ge(ln_done, 2 * int(name[-1]) + (1 if name[:2] == "up" else 0))
                for c in range(DC):
                    split(name, c, x[:, c, CTX:T], CTX)

            def mla_logits(u):
                turn(dve.scalar_tensor_tensor(logit[:, u % 2, 0:384], psum[u % 2][:, 0:384], (NOPE + ROPE) ** -0.5, late("m_mask"),
                                              ALU.mult, ALU.add))
                dve.reduce_max(small[:, 0, u:u + 1], logit[:, u % 2, 0:P], AX.X)
                turn(dve.reduce_max(small[:, 1, u:u + 1], logit[:, u % 2, P:3 * P], AX.X))
                dve.tensor_scalar(small[:, 2:4, u:u + 1], small[:, 0:2, u:u + 1], -1.0, None, ALU.mult).then_inc(at["m"], 1)

            def mla_norm(u):
                (turn.last if u == 3 else turn)(dve.reciprocal(small[:, 6:8, u:u + 1], small[:, 4:6, u:u + 1]))
                dve.tensor_scalar(expo[:, u % 2, 0:P], expo[:, u % 2, 0:P], small[:, 6, u:u + 1], None, ALU.mult)
                dve.tensor_scalar(expo[:, u % 2, P:3 * P], expo[:, u % 2, P:3 * P], small[:, 7, u:u + 1], None, ALU.mult)\
                    .then_inc(at["p"], 1)

            def mla_take(i, u, l):
                r = u % 2
                dst = h[64 * r:64 * r + 64, bass.ds(i * 2 + u // 2, 1), CTX:T].rearrange("p a t -> p (a t)")
                g = gate_b[64 * r:64 * r + 64, bass.ds(i * (2 * SEQ) + (u // 2) * SEQ, SEQ)]
                dve.scalar_tensor_tensor(dst, g, 1.0, psum[4 + u % 2][64 * r:64 * r + 64, 0:SEQ], ALU.add, ALU.mult)\
                    .then_inc(at["od"], 1)

            def add_scaled(name, per_chunk, k):
                for c in range(DC):
                    dve.wait_ge(slots_used, used(name, 2 * c + 1 if per_chunk == 2 else c // 2))
                    xs = x[:, c, CTX:T]
                    dve.scalar_tensor_tensor(xs, xs, ALPHA, psum[OUT_BANK + c % 2][:, CTX:T], ALU.mult, ALU.add).then_inc(x_done, 1)

            def layer_norm(m, name, l):
                dve.wait_ge(ln_mean, m + 1)
                step(dve.tensor_scalar(ln_mu, psum[STAT][:, 0:SEQ], 1.0 / D, None, ALU.mult))
                for c in range(DC):
                    dve.tensor_tensor(hhigh[:, c, :], x[:, c, CTX:T], ln_mu, ALU.subtract).then_inc(ln_cent, 1)
                dve.wait_ge(ln_root, m + 1)
                step(dve.reciprocal(ln_r, ln_std))
                for c in range(DC):
                    ins = dve.scalar_tensor_tensor(x[:, c, CTX:T], hhigh[:, c, :], p_(name + "_g", DC * l + c, 1), ln_r, ALU.mult, ALU.mult)
                step(ins)
                for c in range(DC):
                    ins = dve.tensor_scalar(x[:, c, CTX:T], x[:, c, CTX:T], p_(name + "_b", DC * l + c, 1), None, ALU.add)
                ins.then_inc(ln_done, 1)

            def delta(k):
                halves = lambda ap: ap.rearrange("p (s t) -> p s t", s=2)
                step(dve.tensor_scalar(p_("dn_conv"), p_("dn_conv"), 0.5, None, ALU.mult))
                def taps(n, i, u):
                    for q in range(2):
                        bank = (2 * u + q) % 4
                        src, dst = halves(psum[bank][:, :]), halves(conv2[:, q, :])
                        if q == 0:
                            dve.wait_ge(slots_used, n + used("dn_in", 0))
                        dve.wait_ge(pr_free, 2 * n + (q + 3))
                        w = lambda tap: par[:, bass.ds(n * (2 * CONV) + (POFF["dn_conv"] + q * CONV + tap), 1)]
                        turn(dve.tensor_scalar(dst, src, w(2), None, ALU.mult))
                        for tap, o in ((0, -2), (1, -1), (3, 1), (4, 2)):
                            a0, a1 = max(0, -o), CTX - max(0, o)
                            ins = dve.scalar_tensor_tensor(dst[:, :, a0:a1], src[:, :, a0 + o:a1 + o], w(tap),
                                                           dst[:, :, a0:a1], ALU.mult, ALU.add)
                            if tap < 4:
                                (turn.last if (q, tap) == (1, 3) else turn)(ins)
                            else:
                                ins.then_inc(conv_done, 1)
                        dve.wait_ge(conv_done, 2 * n + (q + 1))
                    for q in range(2):
                        dve.wait_ge(pr_tanh, 2 * n + (q + 1))
                        dve.scalar_tensor_tensor(big[:, bass.ds(n * (2 * T) + q * T, T)], ttmp[:, q, :], 1.0, conv2[:, q, :],
                                                 ALU.add, ALU.mult).then_inc(pr_free, 1)

                def gate(n, i, u):
                    for q in range(2):
                        c = 2 * n + q - 24
                        if q == 0:
                            dve.wait_ge(slots_used, used("dn_in", n))
                        dve.wait_ge(pr_free, 2 * n + q + 3)
                        dve.tensor_scalar(conv2[:, q, :], psum[(2 * u + q) % 4][:, :], 0.5, None, ALU.mult).then_inc(conv_done, 1)
                    for q in range(2):
                        c = 2 * n + q - 24
                        dve.wait_ge(pr_tanh, 2 * n + q + 1)
                        dve.scalar_tensor_tensor(zs[:, c, :], ttmp[:, q, :], 1.0, conv2[:, q, :], ALU.add, ALU.mult)\
                            .then_inc(pr_free, 1)
                over_slots(dve, 12, taps)
                for n in range(12, 16):
                    gate(n, n // 4, n % 4)

                dve.wait_ge(slots_used, used("dn_ab", 0))
                ab = psum[MISC][:, 0:128].rearrange("p (c d g h) -> p d g c h", c=4, d=2, g=2)
                by = lambda n: tokv(n).rearrange("p (d c h) -> p d c h", d=2, c=4)
                for d in range(2):
                    step(dve.tensor_copy(by(TOK_BETA)[:, d], ab[:, d, 1]))
                    step(dve.tensor_tensor(by(TOK_T1)[:, d], ab[:, d, 0], p_("dn_dt").rearrange("p (d c h) -> p d c h", d=2, c=4)[:, d], ALU.add))
                dve.scalar_tensor_tensor(tokv(TOK_T2), tokv(TOK_T1), -1.0, tokv(TOK_T1), ALU.mult, ALU.max).then_inc(gate_step, 1)
                heads_norm(0, 16)
                dve.wait_ge(gate_act, 1)
                step(dve.scalar_tensor_tensor(tokv(TOK_T3), tokv(TOK_T1), 0.0, tokv(TOK_T2), ALU.max, ALU.add))
                dve.scalar_tensor_tensor(tokv(TOK_G), tokv(TOK_T3), -1.0, p_("dn_a"), ALU.mult, ALU.mult).then_inc(gates_done, 1)
                dve.wait_ge(gate_act, 2)
                step(dve.tensor_scalar(tokv(TOK_BETA), tokv(TOK_BETA), 0.5, 0.5, ALU.mult, ALU.add))
                dve.wait_ge(gate_act, 3)
                dve.tensor_copy(tokv(TOK_GC), psum[MISC][:, 0:64])
                dve.tensor_tensor(tokv(TOK_BEG), tokv(TOK_BETA), tokv(TOK_EGC), ALU.mult).then_inc(gates_done, 1)
                with dve.Fori(0, 2) as hg:
                    for s in range(2):
                        dve.memset(quad[s]["S"], 0.0).then_inc(dn["state"][s], 1)
                    with dve.Fori(0, 2) as cp:
                        for cc in range(2):
                            delta_unit_dve(hg, cp, cc)
                heads_norm(16, DNH)
                for c in range(DC):
                    dve.wait_ge(y_in_done, c + 1)
                    split("dn_out", c, h[:, c, :], 0)
                add_out("dn_out", k, 1, mod[:, k, 2, :], 0)

            def heads_norm(base, count):
                for c in range(count):
                    dve.wait_ge(hstd_done, base + c + 1)
                    step(dve.reciprocal(grec[:, c % 4, :], dstd[:, c % 8, :]))
                    if base == 0:
                        dve.scalar_tensor_tensor(qkv[:, c, :], qkv[:, c, :], P ** -0.5 if c < DNH else 1.0, grec[:, c % 4, :],
                                                 ALU.mult, ALU.mult).then_inc(hnorm_done, 1)
                    else:
                        dve.scalar_tensor_tensor(h[:, c, :], h[:, c, :], p_("dn_gain"), grec[:, c % 4, :],
                                                 ALU.mult, ALU.mult).then_inc(hnorm_done, 1)
                        dve.wait_ge(hnorm_done, base + c + 1)
                        dve.tensor_tensor(h[:, c, :], h[:, c, :], zs[:, c, :], ALU.mult).then_inc(y_in_done, 1)

            def delta_unit_dve(hg, cp, cc):
                U = hg * 4 + cp * 2 + cc

                def percol(n, s, tc):
                    return tok[:, n, bass.ds(tc * DNH + hg * QUAD + 32 * s, QUAD)].unsqueeze(2).broadcast_to([P, QUAD, CK])
                tcs = [2 * cp + cc, 2 * cp + (1 - cc)]
                for s in range(2):
                    q, b = quad[s], dbank[s]
                    dve.wait_ge(dn["eg"][s], U + 1)
                    turn(dve.tensor_tensor(q["TG"], b[0], percol(TOK_GC, s, tcs[s]), ALU.subtract))
                    dve.tensor_scalar(q["TG"], q["TG"], 0.0, None, ALU.min).then_inc(dn["d"][s], 1)
                for s in range(2):
                    q, b = quad[s], dbank[s]
                    dve.wait_ge(dn["dtm"][s], U + 1)
                    dve.wait_ge(dn["kq"][s], U + 1)
                    turn(dve.tensor_tensor(q["LT"], b[2], q["DT"], ALU.mult))
                    dve.tensor_tensor(q["QD"], b[3], q["DT"], ALU.mult)
                    dve.tensor_tensor(q["LT"], b[1], q["LT"], ALU.mult).then_inc(dn["lt"][s], 1)
                for s in range(2):
                    q, b = quad[s], dbank[s]
                    edge = CK - 1 if s == 0 else 0
                    dve.wait_ge(dn["ttok"][s], U + 1)
                    dve.tensor_tensor(q["V"], b[3], percol(TOK_BETA, s, tcs[s]), ALU.mult)
                    dve.tensor_tensor(q["KD"], b[2], q["DT"][:, :, edge:edge + 1].broadcast_to([P, QUAD, CK]), ALU.mult)
                    dve.tensor_tensor(q["K"], b[2], percol(TOK_BEG, s, tcs[s]), ALU.mult).then_inc(dn["toks"][s], 1)
                for n in range(1, LEVELS):
                    for s in range(2):
                        q, b = quad[s], dbank[s]
                        dve.wait_ge(dn["z"][s], U * (LEVELS - 1) + n)
                        if n < LEVELS - 1:
                            dve.tensor_tensor(q["X"], q["X"], b[1], ALU.add)
                            dve.tensor_tensor(q["XT"], q["XT"], b[2], ALU.add).then_inc(dn["xu"][s], 1)
                        else:
                            join = (SEEN[s], slice(None), SEEING[s])
                            dve.tensor_tensor(q["XT"][join], q["XT"][join], b[2][join], ALU.add).then_inc(dn["xu"][s], 1)
                for s in range(2):
                    q, b = quad[s], dbank[s]
                    edge = CK - 1 if s == 0 else 0
                    dve.wait_ge(dn["end"][s], U + 1)
                    dst = h[:, bass.ds(hg * QUAD, QUAD), bass.ds(tcs[s] * CK, CK)]
                    if cc == 0:
                        dve.tensor_copy(dst, b[2])
                    else:
                        dve.wait_ge(dn["state"][1 - s], U + hg + 1)
                        dve.tensor_tensor(dst, dst, b[2], ALU.add)
                    (turn.last if s == 1 else turn)(dve.tensor_tensor(q["S"], q["S"], q["EG"][:, :, edge:edge + 1].broadcast_to([P, QUAD, CK]), ALU.mult))
                    dve.tensor_tensor(q["S"], q["S"], b[3], ALU.add).then_inc(dn["state"][s], 1)
                    dve.wait_ge(dn["state"][s], U + hg + 2)

            for l in range(DEPTH):
                for sub in range(3):
                    k = 3 * l + sub
                    t0 = CTX if k == 5 else 0
                    norm(k, t0)
                    if sub != 1:
                        ffn(2 * l + sub // 2, k, t0)
                    if k == 1:
                        delta(k)
                    if k == 4:
                        window(k)

            tables()
            for l in range(DEPTH):
                block2(l)

        @block.gpsimd
        def _(pool):
            psteps = Steps(pool, pool_turn)

            def low(*names):
                for name in names:
                    def slot(n, i, u, name=name):
                        pool.wait_ge(hi_done, n + (SPLIT[name] + 1))
                        r = (BASE[name] + u) % RING
                        for a, b in pieces(name, u):
                            part = high_part(name, u, a, b)
                            ins = pool.tensor_tensor(like(ring_lo[:, r, a:b], part), like(ring[:, r, a:b], part),
                                                     part.bitcast(F32), ALU.subtract)
                        ins.then_inc(lo_done, 1)
                    over_slots(pool, COUNT[name], slot)

            def low_ffn(l, half):
                low(*(f"{w}_{l}{half}{hf}" for hf in range(2) for w in ("w1", "w2")))

            def delta():
                pool.wait_ge(gates_done, 2)
                pool.wait_ge(hnorm_done, 16)
                with pool.Fori(0, 2) as hg:
                    with pool.Fori(0, 2) as cp:
                        for cc in range(2):
                            delta_unit_pool(hg, cp, cc)

            def delta_unit_pool(hg, cp, cc):
                U = hg * 4 + cp * 2 + cc

                def percol(n, s, tc):
                    return tok[:, n, bass.ds(tc * DNH + hg * QUAD + 32 * s, QUAD)].unsqueeze(2).broadcast_to([P, QUAD, CK])

                def over_heads(m):
                    return m.unsqueeze(1).broadcast_to([P, QUAD, CK])
                tcs = [2 * cp + cc, 2 * cp + (1 - cc)]
                for s in range(2):
                    q = quad[s]
                    pool.wait_ge(dn["state"][s], U + hg + 1)
                    pool.tensor_tensor(q["TG"], over_heads(incl(s)), percol(TOK_G, s, tcs[s]), ALU.mult)\
                        .then_inc(dn["staged"][s], 1)
                    pool.tensor_tensor(q["TB"], over_heads(ident), percol(TOK_BETA, s, tcs[s]), ALU.mult)\
                        .then_inc(dn["staged"][s], 1)
                    for nm, first in (("K", DNH), ("V", 2 * DNH)):
                        pool.tensor_copy(q[nm], qkv[:, bass.ds(hg * QUAD + first, QUAD), bass.ds(tcs[s] * CK, CK)])\
                            .then_inc(dn["staged"][s], 1)
                for s in range(2):
                    q = quad[s]
                    pool.wait_ge(dn["dt"][s], U + 1)
                    pool.tensor_tensor(q["DT"], q["DT"], over_heads(incl(s)), ALU.mult).then_inc(dn["dtm"][s], 1)
                for s in range(2):
                    q = quad[s]
                    pool.wait_ge(dn["lt"][s], U + 1)
                    (psteps.last if s == 1 else psteps)(pool.tensor_tensor(q["XT"], q["LT"], over_heads(level(s, 0)), ALU.mult))
                    pool.tensor_tensor(q["XT"], q["XT"], over_heads(ident), ALU.add).then_inc(dn["xt0"][s], 1)
                    pool.tensor_tensor(q["M1"], q["LT"], over_heads(level(s, 1)), ALU.mult).then_inc(dn["mt"][s], 1)
                for s in range(2):
                    q = quad[s]
                    pool.tensor_tensor(q["TB"], qkv[:, bass.ds(hg * QUAD, QUAD), bass.ds(tcs[s] * CK, CK)], q["EG"], ALU.mult)\
                        .then_inc(dn["qg"][s], 1)
                for n in range(2, LEVELS):
                    for s in range(2):
                        q = quad[s]
                        if n > 2:
                            pool.wait_ge(dn["y"][s], U * (LEVELS - 1) + n - 2)
                        pool.tensor_tensor(q[f"M{n % 2}"], q["LT"], over_heads(level(s, n)), ALU.mult).then_inc(dn["mt"][s], 1)

            def attend_pool(l):
                if l is None:
                    for kvp in range(2):
                        with pool.Fori(0, 2) as i:
                            for b in range(2):
                                pool.wait_ge(at["od"], i * 8 + (kvp * 16 + CREDIT - (4 if kvp == 1 and b == 0 else 0)))
                                pool.tensor_copy(stage_q[:, b, 0:SEQ], sqk[:, bass.ds(i * 2 + (kvp * 4 + b), 1), CTX:T]
                                                 .rearrange("p a t -> p (a t)")).then_inc(at["q"], 1)
                else:
                    with pool.Fori(0, 4) as i:
                        for b in range(2):
                            pool.wait_ge(at["o"], i * 4 + (2 * b - 2 + 32 + 16 * l))
                            pool.tensor_copy(stage_q[0:96, b, :], mq[0:96, bass.ds(i * 4 + 2 * b, 2), :].rearrange("p a t -> p (a t)"))
                            pool.tensor_copy(stage_v[:, b, :, :], vtok[:, :, bass.ds(i * 256 + b * 128, 128)]).then_inc(at["q"], 1)

            low_ffn(0, 0)
            low("dn_in", "dn_ab")
            delta()
            low("dn_out")
            low_ffn(0, 1)
            low_ffn(1, 0)
            low("swa_qk", "swa_v")
            pool.wait_ge(ada_used, CREDIT + FIRST_UNITS + UNITS * len(MOD_IN))
            pool.dma_start(zbuf[:, 0:NLATE], A["late"]).then_inc(late_in, 16)
            pool.dma_start(late("pos").bitcast(I32), A["positions"]).then_inc(late_in, 16)
            pool.wait_ge(rope_done, 10)
            attend_pool(None)
            low("swa_out")
            low_ffn(1, 1)
            for l in range(DEPTH):
                low(f"mla_r{l}", f"mla_in{l}")
                pool.wait_ge(rope_done, 10 + 9 * l + 1)
                pool.tensor_copy(mk[64:96, :, :], kpe[64:96, :].unsqueeze(1).broadcast_to([32, MH, SEQ])).then_inc(kb_done, 1)
                pool.wait_ge(kb_done, l + 1)
                pool.wait_ge(rope_done, 10 + 9 * (l + 1))
                pool.wait_ge(uq_done, 20 * (l + 1))
                attend_pool(l)
                low(f"mla_out{l}", f"up{l}", f"down{l}")


def tiles(w, cols, kc=None):
    k, n = w.shape
    return w.reshape(k // P, P, n // cols, cols).transpose(2, 1, 0, 3).reshape(n // cols, P, -1)


def columns(v):
    return np.moveaxis(v.reshape(v.shape[:-1] + (v.shape[-1] // P, P)), -1, 0).reshape(P, -1)


def layout(i):
    a = {}
    tokens = np.concatenate([i["ctx"][0], i["x"][0]], 0)
    a["x_t"] = tokens.T.reshape(DC, P, T).transpose(1, 0, 2)
    a["consts"] = constants()
    twice = lambda v: np.repeat(v, 2, axis=-1)
    rows = lambda v: np.broadcast_to(v.reshape(1, -1), (P, v.size))
    conv = lambda w: np.moveaxis(w.reshape(w.shape[:-1] + (-1, P)), -1, 0).swapaxes(-1, -2).reshape(P, -1)
    p = {
        "ada_b": twice(columns(i["ada_b"])), "norm_g": twice(columns(i["norm_g"])),
        "cond": np.stack([i["c_ctx"].reshape(DC, P).T, i["c"][0].reshape(DC, P).T], -1).reshape(P, -1),
    }
    dup = lambda v: np.broadcast_to(v[:, None, :], (2, 4, DNH))
    p["dn_conv"] = conv(i["dn_conv"][0])
    p["dn_a"], p["dn_dt"] = rows(dup(i["dn_a_log"][0])), rows(dup(i["dn_dt_bias"][0]))
    p["dn_gain"] = i["dn_o_gain"][0].reshape(P, 1)
    two = lambda v: np.tile(v[0], 2).reshape(P, 1)
    p["q_gain"], p["k_gain"] = two(i["swa_q_gain"]), two(i["swa_k_gain"])
    p["sink"] = rows(i["swa_sink"][0])
    p["conv_w"], p["fc_w"] = conv(i["conv_w_2"]), conv(i["ffn_conv_w_2"])
    for name, key in (("conv_b", "conv_b_2"), ("gx_b", "gx_b_2"), ("ga_b", "ga_b_2"), ("lam", "lru_lambda_2"),
                      ("qn_g", "q_norm_g_2"), ("kvn_g", "kv_norm_g_2"), ("ln1_g", "ln1_g_2"), ("ln1_b", "ln1_b_2"),
                      ("ln2_g", "ln2_g_2"), ("ln2_b", "ln2_b_2"), ("fc_b", "ffn_conv_b_2")):
        p[name] = columns(i[key])
    a["late"] = late_constants()
    a["positions"] = np.broadcast_to(i["positions_2"].reshape(1, SEQ), (P, SEQ)).astype(np.int32)
    a["params"] = np.concatenate([p.get(n, np.zeros((P, w), np.float32)) for n, w in PARAMS], 1)
    ada = np.concatenate([tiles(i["ada_w"][l], 256) for l in range(DEPTH)])
    a["ada"], a["ada_later"] = ada[:UNITS], ada[UNITS:]
    for l in range(DEPTH):
        for s in range(2):
            w1 = i["ffn_w1"][l, s].reshape(DC, P, 2, FHC, P).transpose(3, 1, 0, 2, 4).reshape(FHC, P, SLOT)
            w2 = i["ffn_w2"][l, s].reshape(2, FHC // 2, P, DC, P).transpose(0, 3, 2, 1, 4).reshape(2, DC, P, -1)
            for hf in range(2):
                a[f"w1_{l}{s}{hf}"] = w1[11 * hf:11 * (hf + 1)]
                a[f"w2_{l}{s}{hf}"] = w2[hf]
    a["dn_in"] = tiles(i["dn_w_in"][0][:, :4096], 256)
    a["dn_ab"] = tiles(i["dn_w_in"][0][:, 4096:], 32)
    outw = lambda w: w.reshape(DC, P, DC // 2, 2, P).transpose(2, 1, 3, 0, 4).reshape(DC // 2, P, -1)
    a["dn_out"] = outw(i["dn_w_out"][0])
    heads = [4 * (2 * (c // 4) + r) + c % 4 for c in range(8) for r in range(2)]
    w = i["swa_w_qkv"][0]
    wq = w[:, :1024].reshape(D, SH, SD)[:, heads].reshape(D, 1024)
    a["swa_qk"] = tiles(np.concatenate([wq, w[:, 1024:1280]], 1), 256)
    a["swa_v"] = tiles(w[:, 1280:], 256)
    a["swa_out"] = outw(i["swa_w_out"][0].reshape(SH, SD, D)[heads].reshape(D, D))
    pair = lambda w, n: w.reshape(DC, P, 2, n, P).transpose(3, 1, 0, 2, 4).reshape(n, P, SLOT)
    for l in range(DEPTH):
        w = i["w_in_2"][l]
        part = np.split(w, [1024, 2048, 2432, 2688, 2720, 3744], axis=1)
        rope = np.zeros((D, P), w.dtype)
        rope[:, 64:96] = part[4]
        a[f"mla_r{l}"] = tiles(part[0], 256)
        a[f"mla_in{l}"] = tiles(np.concatenate([part[1], part[2], part[3], part[5], part[6], rope], 1), 256)
        bd = np.zeros((P, 2, RC, P), w.dtype)
        for g, key in enumerate(("gx_w_2", "ga_w_2")):
            for c in range(RC):
                for r in range(2):
                    bd[64 * r:64 * r + 64, g, c, 64 * r:64 * r + 64] = i[key][l, 2 * c + r]
        a[f"rnn_gate{l}"] = bd.reshape(1, P, SLOT)
        a[f"mla_uq{l}"] = tiles(i["w_uq_2"][l], 384)
        ukv = i["w_ukv_2"][l].reshape(256, MH, 2, 64)
        a[f"mla_uk{l}"] = tiles(ukv[:, :, 0].reshape(256, 1024), 1024)
        a[f"mla_uv{l}"] = tiles(ukv[:, :, 1].reshape(256, 1024), 1024)
        a[f"mla_out{l}"] = outw(i["w_out_2"][l])
        a[f"up{l}"] = pair(i["w_up_2"][l], FC2)
        w = i["w_down_2"][l].reshape(2, FC2 // 2, P, DC, P)
        a[f"down{l}"] = w.transpose(3, 0, 2, 1, 4).reshape(2 * DC, P, -1)
    return {k: np.ascontiguousarray(v) for k, v in a.items()}


def kernel(**inputs):
    import concourse.bacc as bacc
    from concourse.bass_utils import run_bass_kernel_spmd

    arrays = layout({name: np.asarray(value) for name, value in inputs.items()})
    nc = bacc.Bacc("TRN2", target_bir_lowering=False, num_devices=1)
    A = {name: nc.dram_tensor(name, a.shape, mybir.dt.from_np(a.dtype), kind="ExternalInput").ap()
         for name, a in arrays.items()}
    out = nc.dram_tensor("out", (P, DC, SEQ), F32, kind="ExternalOutput").ap()
    build(nc, A, out)
    result = run_bass_kernel_spmd(nc, [arrays], core_ids=[0])
    return np.ascontiguousarray(result.results[0]["out"].transpose(2, 1, 0).reshape(1, SEQ, D))
```
